# Optimizing a Trainium2 kernel written in Bass

```python
import jax, jax.numpy as jnp
from jax import lax
import numpy as np

'''Two-layer hybrid decoder trunk (causal).
Each layer: x += W_out( sum_i sigmoid(gate_i(h)) * P_i(branch_i) ), h = RMSNorm(x), with three parallel
token mixers fed by ONE combined input projection of h:
  A: forgetting attention (FoX) with per-head QK RMS-norm, swept in 128-query blocks,
  B: causal multi-scale mean pooling (windows 2/4/8/16 per channel group) minus identity,
  C: chunked causal spatial gating unit (gMLP), 128-position chunks, per-group 128x128 lower-triangular mixing;
then x += HierMoE(RMSNorm(x)) with top-1 expert-group routing and top-2 expert routing inside the group.
Input x: (BATCH, SEQ, D_MODEL) float32. Output: (BATCH, SEQ, D_MODEL).
'''

D_MODEL = 1024
BATCH = 1
SEQ = 2048
DEPTH = 1

RMS_EPS = 1e-6
BRANCH_WIDTH = 512
N_BRANCH = 3
A_HEADS = 8
A_HEAD_DIM = 64
A_WIDTH = A_HEADS * A_HEAD_DIM
Q_BLOCK = 128
POOL_WINDOWS = (2, 4, 8, 16)
B_GROUPS = 4
B_GROUP_DIM = 128
B_WIDTH = B_GROUPS * B_GROUP_DIM
C_GROUPS = 4
C_GROUP_DIM = 128
C_WIDTH = C_GROUPS * C_GROUP_DIM
C_CHUNK = 128
OFF_Q = 0
OFF_K = OFF_Q + A_WIDTH
OFF_V = OFF_K + A_WIDTH
OFF_F = OFF_V + A_WIDTH
OFF_P = OFF_F + A_HEADS
OFF_U = OFF_P + B_WIDTH
OFF_SV = OFF_U + C_WIDTH
OFF_G = OFF_SV + C_WIDTH
D_IN = OFF_G + N_BRANCH * D_MODEL
N_EXPERT_GROUPS = 4
EXPERTS_PER_GROUP = 8
N_EXPERTS = N_EXPERT_GROUPS * EXPERTS_PER_GROUP
TOP_K = 2
D_EXPERT = 256
MOE_BLOCK = 256

kernel_name = 'hybrid_fox_pool_sgu_hiermoe'

def rms_norm(x, g):
    xf = x.astype(jnp.float32)
    y = xf * lax.rsqrt(jnp.mean(xf * xf, axis=-1, keepdims=True) + RMS_EPS)
    return (y * g.astype(jnp.float32)).astype(x.dtype)

def forgetting_attention(q, k, v, log_f):
    S = q.shape[2]
    c = jnp.cumsum(log_f, axis=-1)
    scale = A_HEAD_DIM ** -0.5
    outs = []
    for blk in range(S // Q_BLOCK):
        q0 = blk * Q_BLOCK
        q1 = q0 + Q_BLOCK
        qb = q[:, :, q0:q1]
        kb = k[:, :, :q1]
        vb = v[:, :, :q1]
        s = jnp.einsum('bhqd,bhkd->bhqk', qb, kb).astype(jnp.float32) * scale
        s = s + c[:, :, q0:q1, None] - c[:, :, None, :q1]
        mask = (q0 + jnp.arange(Q_BLOCK))[:, None] >= jnp.arange(q1)[None, :]
        s = jnp.where(mask, s, -jnp.inf)
        p = jax.nn.softmax(s, axis=-1)
        outs.append(jnp.einsum('bhqk,bhkd->bhqd', p.astype(vb.dtype), vb))
    return jnp.concatenate(outs, axis=2)

def multiscale_pool(p, w_pool, s_pool):
    B, S, _ = p.shape
    pf = p.astype(jnp.float32)
    cs = jnp.concatenate([jnp.zeros((B, 1, B_WIDTH), jnp.float32), jnp.cumsum(pf, axis=1)], axis=1)
    t = jnp.arange(S)
    outs = []
    for g, w in enumerate(POOL_WINDOWS):
        sl = slice(g * B_GROUP_DIM, (g + 1) * B_GROUP_DIM)
        lo = jnp.maximum(t + 1 - w, 0)
        cnt = jnp.minimum(t + 1, w).astype(jnp.float32)
        win_mean = (cs[:, 1:, sl] - cs[:, lo, sl]) / cnt[None, :, None]
        pooled = (win_mean - pf[:, :, sl]).astype(p.dtype)
        outs.append(jnp.einsum('bsc,cd->bsd', pooled, w_pool[g]))
    return jnp.concatenate(outs, axis=-1) * s_pool

def spatial_gating(z, g_v, w_s, b_s):
    B, S, _ = z.shape
    u = z[..., :C_WIDTH]
    vv = z[..., C_WIDTH:].reshape(B, S // C_CHUNK, C_CHUNK, C_GROUPS, C_GROUP_DIM)
    vv = rms_norm(vv, g_v.reshape(C_GROUPS, C_GROUP_DIM))
    causal = jnp.tril(jnp.ones((C_CHUNK, C_CHUNK), w_s.dtype))
    w_c = w_s * causal
    mixed = jnp.einsum('gts,bnsgc->bntgc', w_c, vv) + b_s.T[None, None, :, :, None]
    return u * mixed.reshape(B, S, C_WIDTH)

def hybrid_mixer(h, w_in, b_fgate, b_gate, g_q, g_k, w_pool, s_pool, g_sgu, w_sgu, b_sgu, w_branch, w_out):
    B, S, _ = h.shape
    z = h @ w_in

    def heads(t):
        return t.reshape(B, S, A_HEADS, A_HEAD_DIM).transpose(0, 2, 1, 3)

    q = rms_norm(heads(z[..., OFF_Q:OFF_K]), g_q)
    k = rms_norm(heads(z[..., OFF_K:OFF_V]), g_k)
    v = heads(z[..., OFF_V:OFF_F])
    log_f = jax.nn.log_sigmoid((z[..., OFF_F:OFF_P] + b_fgate).astype(jnp.float32)).transpose(0, 2, 1)
    y_a = forgetting_attention(q, k, v, log_f).transpose(0, 2, 1, 3).reshape(B, S, A_WIDTH)
    y_b = multiscale_pool(z[..., OFF_P:OFF_U], w_pool, s_pool)
    y_c = spatial_gating(jax.nn.gelu(z[..., OFF_U:OFF_G]), g_sgu, w_sgu, b_sgu)
    gates = jax.nn.sigmoid(z[..., OFF_G:].reshape(B, S, N_BRANCH, D_MODEL) + b_gate)
    merged = (gates[:, :, 0] * (y_a @ w_branch[0])
              + gates[:, :, 1] * (y_b @ w_branch[1])
              + gates[:, :, 2] * (y_c @ w_branch[2]))
    return merged @ w_out

def hierarchical_moe(h, w_rg, b_rg, w_re, b_re, w1, w3, w2):
    B, S, D = h.shape
    N = B * S
    xt = h.reshape(N, D)
    lg = (xt @ w_rg).astype(jnp.float32) + b_rg
    pg = jax.nn.softmax(lg, axis=-1)
    grp = jnp.argmax(lg, axis=-1)
    p_grp = jnp.take_along_axis(pg, grp[:, None], axis=-1)
    le = ((xt @ w_re).astype(jnp.float32) + b_re).reshape(N, N_EXPERT_GROUPS, EXPERTS_PER_GROUP)
    le = jnp.take_along_axis(le, grp[:, None, None], axis=1)[:, 0]
    top_p, top_i = lax.top_k(jax.nn.softmax(le, axis=-1), TOP_K)
    gate = p_grp * (top_p / jnp.sum(top_p, axis=-1, keepdims=True))
    expert = grp[:, None] * EXPERTS_PER_GROUP + top_i

    A = N * TOP_K
    e_flat = expert.reshape(A).astype(jnp.int32)
    g_flat = gate.reshape(A)
    tok_flat = (jnp.arange(A, dtype=jnp.int32) // TOP_K)
    order = jnp.argsort(e_flat)
    e_sorted = e_flat[order]
    counts = jnp.bincount(e_flat, length=N_EXPERTS).astype(jnp.int32)
    start = jnp.cumsum(counts) - counts
    padded = (counts + MOE_BLOCK - 1) // MOE_BLOCK * MOE_BLOCK
    pend = jnp.cumsum(padded)
    pstart = pend - padded
    dest = pstart[e_sorted] + (jnp.arange(A, dtype=jnp.int32) - start[e_sorted])
    n_blocks = -(-(A + N_EXPERTS * (MOE_BLOCK - 1)) // MOE_BLOCK)
    P = n_blocks * MOE_BLOCK
    slot_tok = jnp.full((P,), N, jnp.int32).at[dest].set(tok_flat[order])
    slot_gate = jnp.zeros((P,), g_flat.dtype).at[dest].set(g_flat[order])
    block_start = jnp.arange(n_blocks, dtype=jnp.int32) * MOE_BLOCK
    block_expert = jnp.minimum(jnp.searchsorted(pend, block_start, side='right'), N_EXPERTS - 1)
    x_pad = jnp.concatenate([xt, jnp.zeros((1, D), xt.dtype)], axis=0)
    xs = x_pad[slot_tok].reshape(n_blocks, MOE_BLOCK, D)

    def expert_block(args):
        xb, e = args
        return (jax.nn.silu(xb @ w1[e]) * (xb @ w3[e])) @ w2[e]

    yb = lax.map(expert_block, (xs, block_expert))
    y = yb.reshape(P, D) * slot_gate[:, None].astype(yb.dtype)
    out = jax.ops.segment_sum(y, slot_tok, num_segments=N + 1)[:N]
    return out.reshape(B, S, D)

def setup_inputs(seed: int = 0) -> dict:
    key = jax.random.key(seed)
    ks = jax.random.split(key, 24)
    f32 = jnp.float32

    def nrm(k, shape, fan_in):
        return jax.random.normal(k, shape, f32) * (fan_in ** -0.5)

    def gain(k, shape):
        return 1.0 + 0.02 * jax.random.normal(k, shape, f32)

    return {
        'x': jax.random.normal(ks[0], (BATCH, SEQ, D_MODEL), f32),
        'g_mix': gain(ks[1], (DEPTH, D_MODEL)),
        'w_in': nrm(ks[2], (DEPTH, D_MODEL, D_IN), D_MODEL),
        'b_fgate': jax.random.uniform(ks[3], (DEPTH, A_HEADS), f32, 1.0, 5.0),
        'b_gate': 0.02 * jax.random.normal(ks[4], (DEPTH, N_BRANCH, D_MODEL), f32),
        'g_q': gain(ks[5], (DEPTH, A_HEAD_DIM)),
        'g_k': gain(ks[6], (DEPTH, A_HEAD_DIM)),
        'w_pool': nrm(ks[7], (DEPTH, B_GROUPS, B_GROUP_DIM, B_GROUP_DIM), B_GROUP_DIM),
        's_pool': gain(ks[8], (DEPTH, B_WIDTH)),
        'g_sgu': gain(ks[9], (DEPTH, C_WIDTH)),
        'w_sgu': nrm(ks[10], (DEPTH, C_GROUPS, C_CHUNK, C_CHUNK), C_CHUNK),
        'b_sgu': gain(ks[11], (DEPTH, C_GROUPS, C_CHUNK)),
        'w_branch': nrm(ks[12], (DEPTH, N_BRANCH, BRANCH_WIDTH, D_MODEL), BRANCH_WIDTH),
        'w_out': nrm(ks[13], (DEPTH, D_MODEL, D_MODEL), D_MODEL),
        'g_ffn': gain(ks[14], (DEPTH, D_MODEL)),
        'w_rg': nrm(ks[15], (DEPTH, D_MODEL, N_EXPERT_GROUPS), D_MODEL),
        'b_rg': 0.01 * jax.random.normal(ks[16], (DEPTH, N_EXPERT_GROUPS), f32),
        'w_re': nrm(ks[17], (DEPTH, D_MODEL, N_EXPERTS), D_MODEL),
        'b_re': 0.01 * jax.random.normal(ks[18], (DEPTH, N_EXPERTS), f32),
        'w1': nrm(ks[19], (DEPTH, N_EXPERTS, D_MODEL, D_EXPERT), D_MODEL),
        'w3': nrm(ks[20], (DEPTH, N_EXPERTS, D_MODEL, D_EXPERT), D_MODEL),
        'w2': nrm(ks[21], (DEPTH, N_EXPERTS, D_EXPERT, D_MODEL), D_EXPERT),
    }

def reference(x, g_mix, w_in, b_fgate, b_gate, g_q, g_k, w_pool, s_pool, g_sgu, w_sgu, b_sgu,
              w_branch, w_out, g_ffn, w_rg, b_rg, w_re, b_re, w1, w3, w2):
    for l in range(DEPTH):
        h = rms_norm(x, g_mix[l])
        x = x + hybrid_mixer(h, w_in[l], b_fgate[l], b_gate[l], g_q[l], g_k[l], w_pool[l], s_pool[l],
                             g_sgu[l], w_sgu[l], b_sgu[l], w_branch[l], w_out[l])
        h = rms_norm(x, g_ffn[l])
        x = x + hierarchical_moe(h, w_rg[l], b_rg[l], w_re[l], b_re[l], w1[l], w3[l], w2[l])
    return x


_drawn_inputs = setup_inputs


def setup_inputs(seed=0):
    import zlib

    import numpy as np

    out = dict(_drawn_inputs(seed))
    spreads = {}
    factors = {'b_gate': 4.178,
     'g_q': 8.0,
     'g_k': 8.0,
     's_pool': 13.511,
     'g_sgu': 24.88,
     'b_sgu': 17.294,
     'b_rg': 33.595,
     'b_re': 20.592,
     'g_ffn': 4.711}
    for name, (base, spread) in spreads.items():
        noise = np.random.default_rng([zlib.crc32(name.encode()), seed]).standard_normal(out[name].shape)
        drawn = base * np.exp(spread * noise) if base else spread * noise
        out[name] = __import__('jax').numpy.asarray(drawn.astype(out[name].dtype))
    for name, factor in factors.items():
        out[name] = (out[name] * factor).astype(out[name].dtype)
    return out
```

```python
from contextlib import ExitStack

import concourse.bass as bass
from concourse import mybir

F32 = mybir.dt.float32
F32R = mybir.dt.float32r
I32 = mybir.dt.int32
U32 = mybir.dt.uint32
ALU = mybir.AluOpType
ACT = mybir.ActivationFunctionType
AX = mybir.AxisListType

P = 128
S, D = 2048, 1024
NT = S // P
KD = D // P
CH = 512
NCH = S // CH
TPC = CH // P
EPS = 1e-6
HEADS, HD = 8, 64
GROUPS = 4
WINDOWS = (2, 4, 8, 16)
HALO = 16
OFF_F, OFF_P, OFF_U, OFF_SV, OFF_G = 1536, 1544, 2056, 2568, 3080
QK_TILES, V_TILES, GATE_TILES = 8, 4, 24
T_F, T_QK = 0, 1
T_V = T_QK + QK_TILES
T_P = T_V + V_TILES
T_SU = T_P + GROUPS
T_G = T_SU + 2 * GROUPS
T_END = T_G + GATE_TILES


def w_in_offset(t):
    if t == T_F:
        return OFF_F
    if t < T_P:
        return P * (t - T_QK)
    if t < T_SU:
        return OFF_P + P * (t - T_P)
    if t < T_G:
        g, is_u = divmod(t - T_SU, 2)
        return (OFF_U if is_u else OFF_SV) + P * g
    return OFF_G + P * (t - T_G)


def build_constants(nc, ident, head_ones, ones_col):
    with nc.semaphore("const_zeroed") as zeroed, nc.semaphore("const_made") as made, \
            nc.semaphore("const_cleared") as cleared, nc.Block() as block:
        @block.gpsimd
        def _(pool):
            pool.memset(ident[:, :], 0.0).then_inc(zeroed, 1)
            pool.memset(ones_col[:, :], 1.0).then_inc(made, 1)
            pool.wait_ge(zeroed, 1)
            pool.affine_select(out=ident[:, :], in_=ident[:, :], compare_op=ALU.not_equal, fill=1.0, base=0,
                               pattern=[[-1, P]], channel_multiplier=1).then_inc(made, 1)
            pool.wait_ge(made, 2)

        @block.vector
        def _(dve):
            dve.memset(head_ones[:, :], 0.0).then_inc(cleared, 1)
            dve.wait_ge(cleared, 1)
            dve.memset(head_ones[0:HD, 0:HD], 1.0).then_inc(cleared, 1)
            dve.memset(head_ones[HD:P, HD:P], 1.0).then_inc(cleared, 1)
            dve.wait_ge(cleared, 3)
    return [zeroed, made, cleared]


def norm_and_transpose(nc, x, gain, ident, hT_hi, hT_lo):
    used = []
    with ExitStack() as ctx:
        def sb(name, shape, dt=F32):
            return ctx.enter_context(nc.sbuf_tensor(name, shape, dt))

        def sem(name):
            used.append(ctx.enter_context(nc.semaphore(name)))
            return used[-1]

        XB = 4
        xt = sb("p0_x", [P, XB, D])
        hh = sb("p0_h", [P, 2, D])
        squares = sb("p0_squares", [P, D])
        gain_rows = sb("p0_gain", [P, D])
        sums = sb("p0_sums", [P, NT])
        rms = sb("p0_rms", [P, NT])
        rstd = sb("p0_rstd", [P, NT])
        ps = ctx.enter_context(nc.psum_tensor("p0_turned", [P, 4, 4, P], F32))
        x_loaded = [sem(f"p0_x_loaded{i}") for i in range(XB)]
        gain_loaded = sem("p0_gain_loaded")
        eps_col = sb("p0_eps", [P, 1])
        eps_set = sem("p0_eps_set")
        summed, rooted, inverted = sem("p0_summed"), sem("p0_rooted"), sem("p0_inverted")
        scaled, turned, hi_done, lo_done = sem("p0_scaled"), sem("p0_turned_s"), sem("p0_hi"), sem("p0_lo")
        block = ctx.enter_context(nc.Block())

        @block.sync
        def _(sp):
            sp.dma_start(gain_rows[:, :], gain.rearrange("o d -> (o d)").partition_broadcast(P)).then_inc(gain_loaded, 16)
            for i in range(NT):
                if i >= XB:
                    sp.wait_ge(scaled, i - XB + 1)
                sp.dma_start(xt[:, i % XB, :], x[i * P:(i + 1) * P, :]).then_inc(x_loaded[i % XB], 16)

        @block.scalar
        def _(act):
            def square(i):
                act.wait_ge(x_loaded[i % XB], 16 * (i // XB + 1))
                if i >= 1:
                    act.wait_ge(summed, i)
                nc.scalar.activation(squares[:, :], xt[:, i % XB, :], ACT.Square,
                                     accum_out=sums[:, i:i + 1]).then_inc(summed, 1)
                act.wait_ge(summed, i + 1)
                nc.scalar.activation(rms[:, i:i + 1], sums[:, i:i + 1], ACT.Sqrt, bias=eps_col[:, 0:1],
                                     scale=1.0 / D).then_inc(rooted, 1)

            def high_parts(i):
                for j in range(2):
                    act.wait_ge(turned, 2 * i + j + 1)
                    nc.scalar.copy(hT_hi[:, 4 * j:4 * j + 4, i * P:(i + 1) * P],
                                   ps[:, (2 * i + j) % 4, :, :]).then_inc(hi_done, 1)

            act.wait_ge(eps_set, 1)
            for i in range(NT + 1):
                if i < NT:
                    square(i)
                if i >= 1:
                    high_parts(i - 1)

        @block.gpsimd
        def _(pool):
            pool.memset(eps_col[:, :], EPS).then_inc(eps_set, 1)

        @block.vector
        def _(dve):
            dve.wait_ge(gain_loaded, 16)
            def scale(i):
                dve.wait_ge(rooted, i + 1)
                dve.reciprocal(rstd[:, i:i + 1], rms[:, i:i + 1]).then_inc(inverted, 1)
                dve.wait_ge(inverted, i + 1)
                if i >= 2:
                    dve.wait_ge(turned, 2 * (i - 1))
                dve.scalar_tensor_tensor(out=hh[:, i % 2, :], in0=xt[:, i % XB, :], scalar=rstd[:, i:i + 1],
                                         in1=gain_rows[:, :], op0=ALU.mult, op1=ALU.mult).then_inc(scaled, 1)

            def low_parts(i):
                for j in range(2):
                    dve.wait_ge(hi_done, 2 * i + j + 1)
                    cols = slice(i * P, (i + 1) * P)
                    dve.tensor_tensor(hT_lo[:, 4 * j:4 * j + 4, cols], ps[:, (2 * i + j) % 4, :, :],
                                      hT_hi[:, 4 * j:4 * j + 4, cols], ALU.subtract).then_inc(lo_done, 1)

            for i in range(NT + 1):
                if i < NT:
                    scale(i)
                if i >= 1:
                    low_parts(i - 1)

        @block.tensor
        def _(pe):
            for i in range(NT):
                pe.wait_ge(scaled, i + 1)
                for j in range(2):
                    if i >= 2:
                        pe.wait_ge(lo_done, 2 * (i - 2) + j + 1)
                    for q in range(4):
                        m = nc.tensor.transpose(ps[:, (2 * i + j) % 4, q, :],
                                                hh[:, i % 2, (4 * j + q) * P:(4 * j + q + 1) * P], ident[:, :])
                    m.then_inc(turned, 1)
    return used


def project(nc, hT_hi, hT_lo, ident, head_ones, ones_col, w_in, b_fgate, b_gate, g_q, g_k, w_pool, s_pool, g_sgu, w_sgu,
            b_sgu, scratch):
    used = []
    with ExitStack() as ctx:
        def sb(name, shape, dt=F32):
            return ctx.enter_context(nc.sbuf_tensor("p1_" + name, shape, dt))

        def sem(name):
            used.append(ctx.enter_context(nc.semaphore("p1_" + name)))
            return used[-1]

        raw = [sb(f"w_raw{i}", [P, KD, P]) for i in range(2)]
        w_hi = [sb(f"w_hi{i}", [P, KD, P], F32R) for i in range(2)]
        w_lo = [sb(f"w_lo{i}", [P, KD, P], F32R) for i in range(2)]
        work = [sb(f"work{i}", [P, HALO + CH]) for i in range(6)]
        out = [sb(f"out{i}", [P, 2, CH], F32R) for i in range(2)]
        out_a, out_b = [o[:, 0, :] for o in out], [o[:, 1, :] for o in out]
        out_v = [o[:, :, :].rearrange("p a b -> p (a b)").rearrange("p (n h l d) -> p n h l d", n=TPC, h=2, l=2) for o in out]
        long_a = sb("long_a", [P, S])
        gates = [sb(f"gate{i}", [P, CH]) for i in range(3)]
        cum_chunk = [work[3 + i][0:HEADS, 0:CH] for i in range(2)]
        cum_parts = [sb(f"cum_parts{i}", [HEADS, 2, CH], F32R) for i in range(2)]
        qk_gain = sb("qk_gain", [P, 2])
        f_bias = sb("f_bias", [HEADS, 1])
        gate_bias = sb("gate_bias", [P, GATE_TILES])
        pool_w = sb("pool_w", [P, GROUPS, P])
        pool_scale = sb("pool_scale", [P, GROUPS])
        pool_count = sb("pool_count", [P, GROUPS, HALO])
        pool_inverse = sb("pool_inverse", [P, GROUPS, HALO])
        sgu_gain = sb("sgu_gain", [P, GROUPS])
        sgu_w = sb("sgu_w", [P, GROUPS, P])
        sgu_wT = sb("sgu_wT", [P, GROUPS, P])
        sgu_bias = sb("sgu_bias", [P, GROUPS, P])
        square_sums = sb("square_sums", [P, NT])
        square_roots = sb("square_roots", [P, NT])
        inverse_roots = sb("inverse_roots", [P, NT])
        ones8 = work[5][0:HEADS, 0:CH]
        eps = sb("eps", [P, 1])
        qk_gain8 = sb("qk_gain8", [P, QK_TILES])
        gate_bias_now = [sb(f"gate_bias_now{i}", [P, 1]) for i in range(2)]
        sgu_now = sb("sgu_now", [P, P])
        main = [ctx.enter_context(nc.psum_tensor(f"p1_main{i}", [P, CH], F32)) for i in range(NCH)]
        aux = [ctx.enter_context(nc.psum_tensor(f"p1_aux{i}", [P, CH], F32)) for i in range(4)]

        w_loaded = [sem(f"w_loaded{i}") for i in range(2)]
        split_hi, split_done = sem("split_hi"), sem("split_done")
        main_done = sem("main_done")
        bank_free = [sem(f"bank_free{i}") for i in range(NCH)]
        params_loaded, consts, f_chain, cum_stored = sem("params_loaded"), sem("consts"), sem("f_chain"), [sem(f"cum_stored{i}") for i in range(2)]
        turned_w, sgu_w_ready = sem("turned_w"), sem("sgu_w_ready")
        sq_done, ssq_done, root_done, inv_done = sem("sq_done"), sem("ssq_done"), sem("root_done"), sem("inv_done")
        hi_done, lo_done = sem("hi_done"), sem("lo_done")
        hi_stored = [sem(f"hi_stored{i}") for i in range(2)]
        lo_stored = [sem(f"lo_stored{i}") for i in range(2)]
        v_turned, v_hi, v_lo = sem("v_turned"), sem("v_hi"), sem("v_lo")
        v_stored = [sem(f"v_stored{i}") for i in range(2)]
        halo_done, sum_step, pooled_done, pool_mm = sem("halo_done"), sem("sum_step"), sem("pooled_done"), sem("pool_mm")
        yb_done, yb_stored = sem("yb_done"), [sem(f"yb_stored{i}") for i in range(2)]
        sv_turned, sv_copied, sv_squared, sv_summed = sem("sv_turned"), sem("sv_copied"), sem("sv_squared"), sem("sv_summed")
        sv_rooted, sv_inverted, sv_scaled, mixed = sem("sv_rooted"), sem("sv_inverted"), sem("sv_scaled"), sem("mixed")
        gained, biased, yc_done = sem("gained"), sem("biased"), sem("yc_done")
        yc_stored = [sem(f"yc_stored{i}") for i in range(2)]
        gains_ready, sgu_now_set, gate_bias_set = sem("gains_ready"), sem("sgu_now_set"), sem("gate_bias_set")
        cum_high, cum_split = sem("cum_high"), sem("cum_split")
        gate_stored = [sem(f"gate_stored{i}") for i in range(4)]
        gates.append(work[5][:, 0:CH])
        gate_buf = lambda j: gates[j] if j == 3 else gates[j][:, :]

        w_view = w_in.rearrange("o (k p) n -> p (o k) n", p=P)
        block = ctx.enter_context(nc.Block())

        @block.sync
        def _(sp):
            def load(offset, t, tr):
                if not (isinstance(tr, int) and tr < 2):
                    sp.wait_ge(split_done, tr - 1)
                sp.dma_start(raw[t % 2][:, :, :], w_view[:, :, bass.ds(offset, P)]).then_inc(w_loaded[t % 2], 16)

            load(w_in_offset(0), 0, 0)
            load(w_in_offset(1), 1, 1)
            with nc.allow_non_contiguous_dma("small parameters"):
                for half in range(2):
                    rows = slice(half * HD, half * HD + HD)
                    sp.dma_start(qk_gain[rows, 0:1], g_q.rearrange("o d -> d o")).then_inc(params_loaded, 16)
                    sp.dma_start(qk_gain[rows, 1:2], g_k.rearrange("o d -> d o")).then_inc(params_loaded, 16)
                sp.dma_start(f_bias[:, :], b_fgate.rearrange("o h -> h o")).then_inc(params_loaded, 16)
                sp.dma_start(gate_bias[:, :], b_gate.rearrange("o b (k p) -> p (o b k)", p=P)).then_inc(params_loaded, 16)
                sp.dma_start(pool_w[:, :, :], w_pool.rearrange("o g c d -> c (o g) d")).then_inc(params_loaded, 16)
                sp.dma_start(pool_scale[:, :], s_pool.rearrange("o (g p) -> p (o g)", p=P)).then_inc(params_loaded, 16)
                sp.dma_start(sgu_gain[:, :], g_sgu.rearrange("o (g p) -> p (o g)", p=P)).then_inc(params_loaded, 16)
                sp.dma_start(sgu_w[:, :, :], w_sgu.rearrange("o g t s -> t (o g) s")).then_inc(params_loaded, 16)
                sp.dma_start(sgu_bias[:, :, :], b_sgu.rearrange("o g t -> (o g) t").partition_broadcast(P)).then_inc(params_loaded, 16)
            load(w_in_offset(2), 2, 2)
            for c in range(NCH):
                sp.wait_ge(cum_split, c + 1)
                sp.dma_start(scratch["cum"][:, :, c * CH:(c + 1) * CH], cum_parts[c % 2][:, :, :].bitcast(F32)).then_inc(cum_stored[c % 2], 16)

            def store_qk(t, k, c):
                cols = slice(c * CH, (c + 1) * CH)
                sp.wait_ge(hi_done, k + 1)
                sp.dma_start(scratch["qk_hi"][t - T_QK, :, cols], out_a[c % 2].bitcast(F32)).then_inc(hi_stored[c % 2], 16)
                sp.wait_ge(lo_done, k + 1)
                sp.dma_start(scratch["qk_lo"][t - T_QK, :, cols], out_b[c % 2].bitcast(F32)).then_inc(lo_stored[c % 2], 16)

            with sp.Fori(0, QK_TILES // 2) as i:
                for u in range(2):
                    t = i * 2 + (T_QK + u)
                    load(i * (2 * P) + P * (u + 1 + 1), T_QK + u + 2, t + 2)
                    for c in range(NCH):
                        store_qk(t, i * (2 * NCH) + (u * NCH + c), c)
            for t in range(T_V, T_P):
                load(w_in_offset(t + 2), t + 2, t + 2)
                for c in range(NCH):
                    k = (t - T_V) * NCH + c
                    dst = scratch["v"][c, :, :, 2 * (t - T_V):2 * (t - T_V) + 2]
                    sp.wait_ge(v_lo, k + 1)
                    sp.dma_start(dst, out_v[c % 2].bitcast(F32)).then_inc(v_stored[c % 2], 16)
            for t in range(T_P, T_SU):
                load(w_in_offset(t + 2), t + 2, t + 2)
                for c in range(NCH):
                    sp.wait_ge(yb_done, (t - T_P) * NCH + c + 1)
                    sp.dma_start(scratch["y"][1, t - T_P, :, c * CH:(c + 1) * CH], out_b[c % 2].bitcast(F32)).then_inc(yb_stored[c % 2], 16)

            def pair(g, load_u_offset, load_sv_offset, t):
                load(load_sv_offset, T_SU, t + 2)
                load(load_u_offset, T_SU + 1, t + 3)
                for c in range(NCH):
                    sp.wait_ge(yc_done, g * NCH + (c + 1))
                    sp.dma_start(scratch["y"][2, g, :, c * CH:(c + 1) * CH], out_b[c % 2].bitcast(F32)).then_inc(yc_stored[c % 2], 16)

            with sp.Fori(0, GROUPS - 1) as g:
                pair(g, g * P + (OFF_U + P), g * P + (OFF_SV + P), g * 2 + T_SU)
            pair(GROUPS - 1, w_in_offset(T_G + 1), w_in_offset(T_G), T_G - 2)

            def gate_pair(i, last):
                for u in range(2):
                    t = i * 2 + (T_G + u)
                    if not last:
                        load(i * (2 * P) + (OFF_G + P * (u + 2)), T_G + u + 2, t + 2)
                    for c in range(NCH):
                        sp.wait_ge(bank_free[c], t + 1)
                        sp.dma_start(scratch["gates"][t - T_G, :, c * CH:(c + 1) * CH], gate_buf(c)).then_inc(gate_stored[c], 16)

            with sp.Fori(0, GATE_TILES // 2 - 1) as i:
                gate_pair(i, False)
            gate_pair(GATE_TILES // 2 - 1, True)
            for j in range(2):
                sp.wait_ge(cum_stored[j], 16 * NCH // 2)
                sp.wait_ge(hi_stored[j], 16 * QK_TILES * NCH // 2)
                sp.wait_ge(lo_stored[j], 16 * QK_TILES * NCH // 2)
                sp.wait_ge(v_stored[j], 16 * V_TILES * NCH // 2)
                sp.wait_ge(yb_stored[j], 16 * GROUPS * NCH // 2)
                sp.wait_ge(yc_stored[j], 16 * GROUPS * NCH // 2)
            for j in range(4):
                sp.wait_ge(gate_stored[j], 16 * GATE_TILES)

        @block.gpsimd
        def _(pool):
            pool.memset(eps[:, :], EPS).then_inc(consts, 1)
            pool.memset(ones8, 1.0).then_inc(consts, 1)
            pool.iota(pool_count[:, :, :], pattern=[[0, GROUPS], [1, HALO]], base=1, channel_multiplier=0,
                      allow_small_or_imprecise_dtypes=True).then_inc(consts, 1)
            pool.wait_ge(consts, 3)
            for g, w in enumerate(WINDOWS):
                pool.tensor_scalar(pool_count[:, g, :], pool_count[:, g, :], float(w), None, ALU.min).then_inc(consts, 1)
            pool.wait_ge(params_loaded, 16 * 11)
            for g in range(GROUPS):
                pool.affine_select(out=sgu_w[:, g, :], in_=sgu_w[:, g, :], compare_op=ALU.is_ge, fill=0.0, base=0,
                                   pattern=[[-1, P]], channel_multiplier=1).then_inc(consts, 1)

            def split(t, tr):
                b = t % 2
                if isinstance(tr, int):
                    pool.wait_ge(w_loaded[b], 16 * (tr // 2 + 1))
                else:
                    pool.wait_ge(w_loaded[b], tr * 8 + (8 if b else 16))
                if not (isinstance(tr, int) and tr < 2):
                    pool.wait_ge(main_done, tr * NCH - NCH)
                pool.tensor_tensor(w_hi[b][:, :, :], raw[b][:, :, :], ones_col[:, 0:1, None].broadcast_to([P, KD, P]), ALU.mult).then_inc(split_hi, 1)
                pool.wait_ge(split_hi, tr + 1)
                pool.tensor_tensor(w_lo[b][:, :, :], raw[b][:, :, :], w_hi[b][:, :, :], ALU.subtract).then_inc(split_done, 1)

            for t in range(3):
                split(t, t)
            with pool.Fori(0, (T_END - 3) // 2) as i:
                split(3, i * 2 + 3)
                split(4, i * 2 + 4)

        @block.tensor
        def _(pe):
            def chunk(t, tr, c):
                if c == 0:
                    pe.wait_ge(split_done, tr + 1)
                if not (isinstance(tr, int) and tr == 0):
                    pe.wait_ge(bank_free[c], tr)
                b = t % 2
                cols = slice(c * CH, (c + 1) * CH)
                n = 0
                for k in range(KD):
                    for w, h in ((w_hi, hT_hi), (w_hi, hT_lo), (w_lo, hT_hi)):
                        m = nc.tensor.matmul(main[c][:, :], w[b][:, k, :], h[:, k, cols], start=(n == 0), stop=(n == 3 * KD - 1))
                        n += 1
                m.then_inc(main_done, 1)

            for c in range(NCH):
                chunk(0, 0, c)
            pe.wait_ge(consts, 7 + GROUPS)
            for g in range(GROUPS):
                m = nc.tensor.transpose(aux[3][:, g * P:(g + 1) * P], sgu_w[:, g, :], ident[:, :])
            m.then_inc(turned_w, 1)

            def head_sums(c, k):
                pe.wait_ge(sq_done, k + 1)
                if not (isinstance(k, int) and k < 2):
                    pe.wait_ge(root_done, k - 1)
                nc.tensor.matmul(aux[c % 2][:, :], head_ones[:, :], work[c % 2][:, 0:CH], start=True, stop=True).then_inc(ssq_done, 1)

            def qk_pair(i):
                for s in range(2 * NCH + 1):
                    if s < 2 * NCH:
                        u, c = divmod(s, NCH)
                        chunk(T_QK + u, i * 2 + (T_QK + u), c)
                    if s >= 1:
                        head_sums(s - 1, i * (2 * NCH) + (s - 1))

            qk_pair(0)
            with pe.Fori(1, QK_TILES // 2) as i:
                qk_pair(i)

            def v_turn(k):
                c = k % NCH
                pe.wait_ge(bank_free[c], T_V + k // NCH + 1)
                if k < 2:
                    pe.wait_ge(root_done, QK_TILES * NCH - 1 + k)
                else:
                    pe.wait_ge(v_lo, k - 1)
                for n in range(TPC):
                    m = nc.tensor.transpose(aux[c % 2][:, n * P:(n + 1) * P], work[c % 2][:, n * P:(n + 1) * P], ident[:, :])
                m.then_inc(v_turned, 1)

            for k in range(V_TILES * NCH + 1):
                if k < V_TILES * NCH:
                    chunk(T_V + k // NCH, T_V + k // NCH, k % NCH)
                if k >= 1:
                    v_turn(k - 1)

            def pool_product(k):
                g, c = divmod(k, NCH)
                pe.wait_ge(pooled_done, k + 1)
                if k < 2:
                    pe.wait_ge(v_lo, V_TILES * NCH - 1 + k)
                else:
                    pe.wait_ge(yb_done, k - 1)
                nc.tensor.matmul(aux[c % 2][:, :], pool_w[:, g, :], work[4 + c % 2][:, 0:CH], start=True, stop=True).then_inc(pool_mm, 1)

            for k in range(GROUPS * NCH + 1):
                if k < GROUPS * NCH:
                    chunk(T_P + k // NCH, T_P + k // NCH, k % NCH)
                if k >= 1:
                    pool_product(k - 1)

            def su_pair(g):
                t = g * 2 + T_SU
                for s in range(NCH + 1):
                    if s < NCH:
                        chunk(T_SU, t, s)
                    else:
                        chunk(T_SU + 1, t + 1, 0)
                    if s >= 1:
                        c = s - 1
                        pe.wait_ge(bank_free[c], t + 1)
                        if c >= 2:
                            pe.wait_ge(sv_copied, g * NCH + (c - 1))
                        elif not isinstance(g, int):
                            pe.wait_ge(sv_copied, g * NCH + (c - 1))
                        else:
                            pe.wait_ge(yb_done, GROUPS * NCH - 1 + c)
                        for n in range(TPC):
                            m = nc.tensor.transpose(aux[c % 2][:, n * P:(n + 1) * P], work[c % 2][:, n * P:(n + 1) * P], ident[:, :])
                        m.then_inc(sv_turned, 1)
                for s in range(1, NCH + 1):
                    if s < NCH:
                        chunk(T_SU + 1, t + 1, s)
                    c = s - 1
                    pe.wait_ge(sv_scaled, g * NCH + s)
                    if c >= 2 or not isinstance(g, int):
                        pe.wait_ge(gained, g * NCH + (c - 1))
                    for n in range(TPC):
                        cols = slice((c * TPC + n) * P, (c * TPC + n + 1) * P)
                        m = nc.tensor.matmul(aux[2 + c % 2][:, n * P:(n + 1) * P], long_a[:, cols], sgu_now[:, :], start=True, stop=True)
                    m.then_inc(mixed, 1)

            su_pair(0)
            with pe.Fori(1, GROUPS) as g:
                su_pair(g)
            with pe.Fori(0, GATE_TILES // 2) as i:
                for u in range(2):
                    for c in range(NCH):
                        chunk(T_G + u, i * 2 + (T_G + u), c)

        @block.scalar
        def _(act):
            act.wait_ge(params_loaded, 16 * 11)
            act.wait_ge(consts, 3)
            for c in range(NCH):
                act.wait_ge(f_chain, 6 * c + 2)
                nc.scalar.activation(work[1][0:HEADS, 0:CH], work[1][0:HEADS, 0:CH], ACT.Exp).then_inc(f_chain, 1)
                act.wait_ge(f_chain, 6 * c + 3)
                nc.scalar.activation(work[1][0:HEADS, 0:CH], work[1][0:HEADS, 0:CH], ACT.Ln, bias=1.0).then_inc(f_chain, 1)

            def square(u, c, i):
                k = i * (2 * NCH) + (u * NCH + c)
                act.wait_ge(main_done, k + (T_QK * NCH + 1))
                if isinstance(k, int) and k < 2:
                    act.wait_ge(f_chain, 6 * NCH)
                else:
                    act.wait_ge(ssq_done, k - 1)
                nc.scalar.activation(work[c % 2][:, 0:CH], main[c][:, :], ACT.Square).then_inc(sq_done, 1)

            def root(u, c, i):
                k = i * (2 * NCH) + (u * NCH + c)
                act.wait_ge(ssq_done, k + 1)
                if not (isinstance(k, int) and k < 2):
                    act.wait_ge(inv_done, k - 1)
                else:
                    act.wait_ge(cum_split, NCH)
                nc.scalar.activation(work[2 + c % 2][:, 0:CH], aux[c % 2][:, :], ACT.Sqrt, bias=eps[:, 0:1], scale=1.0 / HD).then_inc(root_done, 1)

            def high(u, c, i):
                k = i * (2 * NCH) + (u * NCH + c)
                act.wait_ge(bank_free[c], i * 2 + (T_QK + u + 1))
                if not (isinstance(k, int) and k < 2):
                    stored = (k - (c % 2)) * 8
                    act.wait_ge(hi_stored[c % 2], stored)
                nc.scalar.copy(out_a[c % 2], gates[c % 2][:, :]).then_inc(hi_done, 1)

            def qk_pair(i):
                for s in range(2 * NCH + 2):
                    if s < 2 * NCH:
                        square(s // NCH, s % NCH, i)
                    if 1 <= s <= 2 * NCH:
                        root((s - 1) // NCH, (s - 1) % NCH, i)
                    if s >= 2:
                        high((s - 2) // NCH, (s - 2) % NCH, i)

            qk_pair(0)
            with act.Fori(1, QK_TILES // 2) as i:
                qk_pair(i)

            def v_copy(k):
                c = k % NCH
                act.wait_ge(main_done, T_V * NCH + k + 1)
                if k >= 2:
                    act.wait_ge(v_turned, k - 1)
                else:
                    act.wait_ge(ssq_done, QK_TILES * NCH)
                nc.scalar.copy(work[c % 2][:, 0:CH], main[c][:, :]).then_inc(bank_free[c], 1)

            def v_high(k):
                c = k % NCH
                act.wait_ge(v_turned, k + 1)
                if k < 2:
                    act.wait_ge(hi_stored[c], 16 * QK_TILES * NCH // 2)
                    act.wait_ge(lo_stored[c], 16 * QK_TILES * NCH // 2)
                else:
                    act.wait_ge(v_stored[c % 2], 16 * (k // 2))
                nc.scalar.copy(out_v[c % 2][:, :, :, 0, :], aux[c % 2][:, :].rearrange("p (n h d) -> p n h d", n=TPC, h=2)).then_inc(v_hi, 1)

            for k in range(V_TILES * NCH + 1):
                if k < V_TILES * NCH:
                    v_copy(k)
                if k >= 1:
                    v_high(k - 1)

            def p_copy(k):
                c = k % NCH
                act.wait_ge(main_done, T_P * NCH + k + 1)
                if k < 2:
                    act.wait_ge(v_turned, V_TILES * NCH)
                else:
                    act.wait_ge(pooled_done, k - 1)
                    act.wait_ge(halo_done, k)
                nc.scalar.copy(work[c % 2][:, HALO:HALO + CH], main[c][:, :]).then_inc(bank_free[c], 1)

            def yb_scale(k):
                g, c = divmod(k, NCH)
                act.wait_ge(pool_mm, k + 1)
                if k < 2:
                    act.wait_ge(v_stored[c], 16 * V_TILES * NCH // 2)
                else:
                    act.wait_ge(yb_stored[c % 2], 16 * (k // 2))
                nc.scalar.activation(out_b[c % 2].bitcast(F32), aux[c % 2][:, :], ACT.Copy, scale=pool_scale[:, g:g + 1]).then_inc(yb_done, 1)

            for k in range(GROUPS * NCH + 2):
                if k < GROUPS * NCH:
                    p_copy(k)
                if k >= 2:
                    yb_scale(k - 2)

            def su_pair(g):
                t = g * 2 + T_SU
                for s in range(NCH + 1):
                    if s < NCH:
                        act.wait_ge(main_done, t * NCH + (s + 1))
                        if s >= 2 or not isinstance(g, int):
                            act.wait_ge(sv_turned, g * NCH + (s - 1))
                        else:
                            act.wait_ge(pooled_done, GROUPS * NCH)
                        nc.scalar.activation(work[s % 2][:, 0:CH], main[s][:, :], ACT.Gelu_apprx_tanh).then_inc(bank_free[s], 1)
                    if s >= 1:
                        c = s - 1
                        act.wait_ge(sv_turned, g * NCH + s)
                        if c == 0 and not isinstance(g, int):
                            act.wait_ge(mixed, g * NCH)
                        nc.scalar.copy(long_a[:, c * CH:(c + 1) * CH], aux[c % 2][:, :]).then_inc(sv_copied, 1)
                act.wait_ge(sv_summed, g * NCH + NCH)
                nc.scalar.activation(square_roots[:, :], square_sums[:, :], ACT.Sqrt, bias=eps[:, 0:1], scale=1.0 / P).then_inc(sv_rooted, 1)
                for c in range(NCH):
                    act.wait_ge(main_done, t * NCH + (NCH + c + 1))
                    if c >= 2 or not isinstance(g, int):
                        act.wait_ge(yc_done, g * NCH + (c - 1))
                    else:
                        act.wait_ge(pool_mm, GROUPS * NCH)
                    nc.scalar.activation(work[4 + c % 2][:, 0:CH], main[c][:, :], ACT.Gelu_apprx_tanh).then_inc(bank_free[c], 1)

            su_pair(0)
            with act.Fori(1, GROUPS) as g:
                su_pair(g)

            def gate_pair(i):
                for u in range(2):
                    for c in range(NCH):
                        tile = i * 2 + u
                        if c == 0:
                            act.wait_ge(gate_bias_set, tile + 1)
                        act.wait_ge(main_done, i * (2 * NCH) + ((T_G + u) * NCH + c + 1))
                        if not (isinstance(tile, int) and tile == 0):
                            act.wait_ge(gate_stored[c], tile * 16)
                        elif c < 3:
                            act.wait_ge(lo_done, QK_TILES * NCH)
                        else:
                            act.wait_ge(yc_done, GROUPS * NCH)
                        nc.scalar.activation(gate_buf(c), main[c][:, :], ACT.Sigmoid, bias=gate_bias_now[u][:, 0:1]).then_inc(bank_free[c], 1)

            gate_pair(0)
            with act.Fori(1, GATE_TILES // 2) as i:
                gate_pair(i)

        @block.vector
        def _(dve):
            dve.wait_ge(params_loaded, 16 * 11)
            dve.wait_ge(consts, 7)
            for c in range(NCH):
                low, mag = work[0][0:HEADS, 0:CH], work[1][0:HEADS, 0:CH]
                dve.wait_ge(main_done, c + 1)
                dve.tensor_scalar(low, main[c][0:HEADS, :], f_bias[:, 0:1], 0.0, ALU.add, ALU.min).then_inc(f_chain, 1)
                dve.tensor_scalar(mag, main[c][0:HEADS, :], f_bias[:, 0:1], 0.0, ALU.add, ALU.max).then_inc(bank_free[c], 1)
                dve.wait_ge(f_chain, 6 * c + 1)
                dve.wait_ge(bank_free[c], 1)
                dve.tensor_tensor(mag, low, mag, ALU.subtract).then_inc(f_chain, 1)
                dve.wait_ge(f_chain, 6 * c + 4)
                dve.tensor_tensor(low, low, mag, ALU.subtract).then_inc(f_chain, 1)
                dve.wait_ge(f_chain, 6 * c + 5)
                dve.tensor_tensor_scan(cum_chunk[c % 2], ones8, low,
                                       0.0 if c == 0 else cum_chunk[(c - 1) % 2][:, CH - 1:CH],
                                       ALU.mult, ALU.add).then_inc(f_chain, 1)
                dve.wait_ge(f_chain, 6 * c + 6)
                if c >= 2:
                    dve.wait_ge(cum_stored[c % 2], 16)
                dve.tensor_copy(cum_parts[c % 2][:, 0, :], cum_chunk[c % 2]).then_inc(cum_high, 1)
                dve.wait_ge(cum_high, c + 1)
                dve.tensor_tensor(cum_parts[c % 2][:, 1, :], cum_chunk[c % 2], cum_parts[c % 2][:, 0, :], ALU.subtract).then_inc(cum_split, 1)
            dve.wait_ge(turned_w, 1)
            dve.tensor_copy(sgu_wT[:, :, :], aux[3][:, :].rearrange("p (g t) -> p g t", g=GROUPS)).then_inc(sgu_w_ready, 1)
            dve.reciprocal(pool_inverse[:, :, :], pool_count[:, :, :]).then_inc(sgu_w_ready, 1)

            def normalise(u, c, i):
                k = i * (2 * NCH) + (u * NCH + c)
                dve.wait_ge(root_done, k + 1)
                dve.reciprocal(work[4 + c % 2][:, 0:CH], work[2 + c % 2][:, 0:CH]).then_inc(inv_done, 1)
                dve.wait_ge(inv_done, k + 1)
                if not (isinstance(k, int) and k < 2):
                    dve.wait_ge(lo_done, k - 1)
                tile = i * 2 + u
                gain = qk_gain_of(tile)
                dve.scalar_tensor_tensor(out=gates[c % 2][:, :], in0=main[c][:, :], scalar=gain,
                                         in1=work[4 + c % 2][:, 0:CH], op0=ALU.mult, op1=ALU.mult).then_inc(bank_free[c], 1)

            def low_part(u, c, i):
                k = i * (2 * NCH) + (u * NCH + c)
                dve.wait_ge(hi_done, k + 1)
                if not (isinstance(k, int) and k < 2):
                    dve.wait_ge(lo_stored[c % 2], (k - (c % 2)) * 8)
                dve.tensor_tensor(out_b[c % 2], gates[c % 2][:, :], out_a[c % 2], ALU.subtract).then_inc(lo_done, 1)

            def qk_gain_of(tile):
                return qk_gain8[:, bass.ds(tile, 1)]

            for j in range(QK_TILES):
                src = qk_gain[:, 0:1] if j < QK_TILES // 2 else qk_gain[:, 1:2]
                dve.tensor_scalar(qk_gain8[:, j:j + 1], src, -HD ** -0.5 if j < QK_TILES // 2 else 1.0, None, ALU.mult).then_inc(gains_ready, 1)
            dve.wait_ge(gains_ready, QK_TILES)

            def qk_pair(i):
                for s in range(2 * NCH + 1):
                    if s < 2 * NCH:
                        normalise(s // NCH, s % NCH, i)
                    if s >= 1:
                        low_part((s - 1) // NCH, (s - 1) % NCH, i)

            qk_pair(0)
            with dve.Fori(1, QK_TILES // 2) as i:
                qk_pair(i)

            for k in range(V_TILES * NCH):
                c = k % NCH
                dve.wait_ge(v_hi, k + 1)
                dve.tensor_tensor(out_v[c % 2][:, :, :, 1, :], aux[c % 2][:, :].rearrange("p (n h d) -> p n h d", n=TPC, h=2),
                                  out_v[c % 2][:, :, :, 0, :], ALU.subtract).then_inc(v_lo, 1)

            steps = 0
            E_ = HALO + CH
            for k in range(GROUPS * NCH):
                g, c = divmod(k, NCH)
                w = WINDOWS[g]
                p = work[c % 2]
                dve.wait_ge(bank_free[c], T_P + g + 1)
                if c == 0:
                    dve.memset(p[:, 0:HALO], 0.0).then_inc(halo_done, 1)
                else:
                    dve.tensor_copy(p[:, 0:HALO], work[(c - 1) % 2][:, CH:CH + HALO]).then_inc(halo_done, 1)
                dve.wait_ge(halo_done, k + 1)
                src, reach, b = p, 1, 0
                while reach < w:
                    dst = work[2 + b]
                    first = 2 * reach - 1
                    dve.tensor_tensor(dst[:, first:E_], src[:, first:E_], src[:, first - reach:E_ - reach], ALU.add).then_inc(sum_step, 1)
                    steps += 1
                    dve.wait_ge(sum_step, steps)
                    src, reach, b = dst, reach * 2, 1 - b
                if k >= 2:
                    dve.wait_ge(pool_mm, k - 1)
                pooled = work[4 + c % 2]
                if c == 0:
                    dve.tensor_tensor(work[2 + b][:, HALO:2 * HALO], src[:, HALO:2 * HALO], pool_inverse[:, g, :], ALU.mult).then_inc(sum_step, 1)
                    steps += 1
                    dve.wait_ge(sum_step, steps)
                    dve.tensor_tensor(pooled[:, 0:HALO], work[2 + b][:, HALO:2 * HALO], p[:, HALO:2 * HALO], ALU.subtract).then_inc(sum_step, 1)
                    steps += 1
                    dve.wait_ge(sum_step, steps)
                lo = HALO if c == 0 else 0
                dve.scalar_tensor_tensor(out=pooled[:, lo:CH], in0=src[:, HALO + lo:E_], scalar=1.0 / w, in1=p[:, HALO + lo:E_],
                                         op0=ALU.mult, op1=ALU.subtract).then_inc(pooled_done, 1)

            def su_pair(g):
                for c in range(NCH):
                    dve.wait_ge(sv_copied, g * NCH + (c + 1))
                    part = long_a[:, c * CH:(c + 1) * CH]
                    if c >= 1 or not isinstance(g, int):
                        dve.wait_ge(sv_summed, g * NCH + c)
                    dve.tensor_tensor(work[2][:, 0:CH], part, part, ALU.mult).then_inc(sv_squared, 1)
                    dve.wait_ge(sv_squared, g * NCH + (c + 1))
                    dve.tensor_reduce(square_sums[:, c * TPC:(c + 1) * TPC], work[2][:, 0:CH].rearrange("p (n d) -> p n d", n=TPC),
                                      AX.X, ALU.add).then_inc(sv_summed, 1)
                dve.tensor_copy(sgu_now[:, :], sgu_wT[:, bass.ds(g, 1), :].rearrange("p a t -> p (a t)")).then_inc(sgu_now_set, 1)
                dve.wait_ge(sv_rooted, g + 1)
                dve.reciprocal(inverse_roots[:, :], square_roots[:, :]).then_inc(sv_inverted, 1)
                dve.wait_ge(sv_inverted, g + 1)
                dve.wait_ge(sgu_now_set, g + 1)
                for c in range(NCH):
                    for n in range(TPC):
                        j = c * TPC + n
                        m = dve.tensor_scalar(long_a[:, j * P:(j + 1) * P], long_a[:, j * P:(j + 1) * P], inverse_roots[:, j:j + 1], None, ALU.mult)
                    m.then_inc(sv_scaled, 1)
                for c in range(NCH):
                    dve.wait_ge(mixed, g * NCH + (c + 1))
                    if c >= 1 or not isinstance(g, int):
                        dve.wait_ge(yc_done, g * NCH + c)
                    dve.tensor_scalar(work[2][:, 0:CH], aux[2 + c % 2][:, :], sgu_gain[:, bass.ds(g, 1)], None, ALU.mult).then_inc(gained, 1)
                    dve.wait_ge(gained, g * NCH + (c + 1))
                    bias = sgu_bias[:, bass.ds(g, 1), :].broadcast_to([P, TPC, P])
                    dve.tensor_tensor(work[3][:, 0:CH].rearrange("p (n t) -> p n t", n=TPC), work[2][:, 0:CH].rearrange("p (n t) -> p n t", n=TPC),
                                      bias, ALU.add).then_inc(biased, 1)
                    dve.wait_ge(biased, g * NCH + (c + 1))
                    dve.wait_ge(bank_free[c], g * 2 + (T_SU + 2))
                    if c >= 2:
                        dve.wait_ge(yc_stored[c % 2], g * 32 + 16 * (c // 2))
                    elif isinstance(g, int):
                        dve.wait_ge(yb_stored[c % 2], 16 * GROUPS * NCH // 2)
                    else:
                        dve.wait_ge(yc_stored[c % 2], g * 32)
                    dve.tensor_tensor(out_b[c % 2].bitcast(F32), work[3][:, 0:CH], work[4 + c % 2][:, 0:CH], ALU.mult).then_inc(yc_done, 1)

            su_pair(0)
            with dve.Fori(1, GROUPS) as g:
                su_pair(g)

            def gate_bias_columns(i):
                for u in range(2):
                    if not isinstance(i, int):
                        dve.wait_ge(bank_free[NCH - 1], i * 2 + (T_G + u - 1))
                    dve.tensor_copy(gate_bias_now[u][:, :], gate_bias[:, bass.ds(i * 2 + u, 1)]).then_inc(gate_bias_set, 1)

            gate_bias_columns(0)
            with dve.Fori(1, GATE_TILES // 2) as i:
                gate_bias_columns(i)
    return used


def groups_of(i):
    return i // 4 + 1


def attend(nc, ident, scratch, spent=()):
    PER_HEAD = sum(groups_of(i) for i in range(NT))
    RING = 4
    AHEAD_Q = 2
    Y_TILES = HEADS * HD // P
    DEPTH = 2
    with ExitStack() as ctx:
        def sb(name, shape, dt=F32):
            return ctx.enter_context(nc.sbuf_tensor("at_" + name, shape, dt))

        def sem(name):
            return ctx.enter_context(nc.semaphore("at_" + name))

        q_high = sb("q_high", [P, S], F32R)
        q_low = sb("q_low", [P, S], F32R)
        k_both = sb("k_both", [P, 2, S], F32R)
        k_cum = sb("k_cum", [P, 2, S], F32R)
        v_both = sb("v_both", [P, 2, NT, 2 * HD], F32R)
        scores = [sb(f"scores{b}", [P, S]) for b in range(RING)]
        probs = [sb(f"probs{b}", [P, S]) for b in range(2)]
        turned_hi = [sb(f"turned_hi{b}", [P, 4, P], F32R) for b in range(4)]
        turned_lo = [sb(f"turned_lo{b}", [P, 4, P], F32R) for b in range(4)]
        y = sb("y", [P, NT, HEADS * HD])
        least = sb("least", [P, RING, 4])
        row_sum = sb("row_sum", [P, 4])
        row_inv = sb("row_inv", [P, 2])
        y_part = sb("y_part", [P, 2, HD])
        ones_f = sb("ones_f", [P, S])
        mask_f = sb("mask_f", [P, P])
        mask = sb("mask", [P, P], F32R)
        ident_r = sb("ident_r", [P, P], F32R)
        s_ps = [ctx.enter_context(nc.psum_tensor(f"at_s{b}", [P, CH], F32)) for b in range(2)]
        t_ps = [ctx.enter_context(nc.psum_tensor(f"at_t{b}", [P, 4, P], F32)) for b in range(4)]
        o_ps = [ctx.enter_context(nc.psum_tensor(f"at_o{b}", [P, CH], F32)) for b in range(2)]

        consts, ones_set = sem("consts"), sem("ones_set")
        q_loaded = [sem(f"q_loaded{c}") for c in range(4)]
        kv_loaded_all = sem("kv_loaded")
        KV_INC = 16 * (4 + NCH)
        q_free, scored, moved, exped = sem("q_free"), sem("scored"), sem("moved"), sem("exped")
        turned, high, low = sem("turned"), sem("high"), sem("low")
        weighed, inverted, half, y_done = sem("weighed"), sem("inverted"), sem("half"), sem("y_done")
        y_turned, yT_copied = sem("y_turned"), [sem(f"yT_copied{b}") for b in range(2)]
        yT_stored = sem("yT_stored")
        block = ctx.enter_context(nc.Block())

        tiles = list(range(NT - 1, -1, -1))
        first = {}
        n = 0
        for s, i in enumerate(tiles):
            first[s] = n
            n += groups_of(i)

        @block.gpsimd
        def _(pool):
            if spent:
                pool.sem_clear(range(min(s.num for s in spent), max(s.num for s in spent) + 1))
            pool.memset(ones_f[:, :], 1.0).then_inc(consts, 1)
            pool.memset(mask_f[:, :], 0.0).then_inc(consts, 1)
            pool.wait_ge(consts, 2)
            pool.affine_select(out=mask_f[:, :], in_=mask_f[:, :], compare_op=ALU.is_ge, fill=1e30, base=0,
                               pattern=[[-1, P]], channel_multiplier=1).then_inc(consts, 1)

        @block.sync
        def _(sp):
            def load_q(h, c):
                if not isinstance(h, int) or h > 0:
                    sp.wait_ge(scored, h * PER_HEAD + (first[NT - 1 - 4 * c] + groups_of(4 * c) - PER_HEAD))
                    sp.sem_inc(q_free)
                cols = slice(c * CH, (c + 1) * CH)
                rows = bass.ds(h * HD, HD)
                sp.dma_start(q_high[0:HD, cols].bitcast(F32), scratch["q_rows"][0][rows, cols]).then_inc(q_loaded[c], 16)
                sp.dma_start(q_high[HD:P, cols].bitcast(F32), scratch["q_rows"][0][rows, cols]).then_inc(q_loaded[c], 16)
                sp.dma_start(q_low[0:HD, cols].bitcast(F32), scratch["q_rows"][1][rows, cols]).then_inc(q_loaded[c], 16)

            def load_kv(h):
                b = h % 2
                if not isinstance(h, int):
                    sp.wait_ge(y_done, h * NT - NT)
                if not isinstance(h, int) or h > 0:
                    sp.wait_ge(scored, (h - 1) * PER_HEAD + (first[2] + 1))
                rows = bass.ds(h * HD, HD)
                hi, lo = scratch["k_rows"][0][rows, :], scratch["k_rows"][1][rows, :]
                for dst, src in ((k_both[0:HD, bass.ds(b, 1), :], hi), (k_both[HD:P, bass.ds(b, 1), :], lo), (k_cum[0:HD, bass.ds(b, 1), :], hi),
                                 (k_cum[HD:HD + 2, bass.ds(b, 1), :], scratch["cum"][bass.ds(h, 1), :, :].rearrange("a l s -> (a l) s"))):
                    sp.dma_start(dst.rearrange("p a s -> p (a s)").bitcast(F32), src).then_inc(kv_loaded_all, 16)
                src = scratch["v"][:, :, :, bass.ds(h, 1), :, :].rearrange("c p n h l d -> p c n (h l d)")
                for c in range(NCH):
                    sp.dma_start(v_both[:, bass.ds(b, 1), c * TPC:(c + 1) * TPC, :].rearrange("p a n d -> p (a n) d").bitcast(F32),
                                 src[:, c]).then_inc(kv_loaded_all, 16)

            load_kv(0)
            for c in range(3, -1, -1):
                load_q(0, c)
            load_kv(1)
            for c in range(3, -1, -1):
                load_q(1, c)
            with sp.Fori(2, HEADS) as h:
                load_kv(h)
                for c in range(3, -1, -1):
                    load_q(h, c)
            for f in range(Y_TILES):
                for by in range(2):
                    sp.wait_ge(yT_copied[by], (f + 1) * NCH // 2)
                sp.dma_start(scratch["y"][0, f, :, :], scores[f][:, :]).then_inc(yT_stored, 16)
            sp.wait_ge(yT_stored, 16 * Y_TILES)

        @block.tensor
        def _(pe):
            def score(h, s, j):
                i = tiles[s]
                n = first[s] + j
                if j == 0:
                    if s == 0:
                        pe.wait_ge(kv_loaded_all, h * KV_INC + KV_INC)
                    if i % 4 == 3:
                        pe.wait_ge(q_loaded[i // 4], h * 48 + 48)
                if not (isinstance(h, int) and h == 0 and n < 2):
                    pe.wait_ge(moved, h * PER_HEAD + (n - 1))
                width = min(CH, (i + 1) * P - j * CH)
                cols = slice(j * CH, j * CH + width)
                b = h % 2
                diag = j == groups_of(i) - 1
                out = s_ps[n % 2][:, 0:width]
                kb = k_both[:, bass.ds(b, 1), cols].rearrange("p a s -> p (a s)")
                kc = k_cum[0:HD + 2, bass.ds(b, 1), cols].rearrange("p a s -> p (a s)")
                nc.tensor.matmul(out, q_high[:, i * P:(i + 1) * P], kb, start=True, stop=False)
                m = nc.tensor.matmul(out, q_low[0:HD + 2, i * P:(i + 1) * P], kc, start=False, stop=not diag)
                if diag:
                    m = nc.tensor.matmul(s_ps[n % 2][:, width - P:width], ident_r[:, :], mask[:, :], start=False, stop=True)
                m.then_inc(scored, 1)

            def turn(h, s, j):
                i = tiles[s]
                n = first[s] + j
                if j == 0:
                    pe.wait_ge(exped, h * NT + (s + 1))
                if not (isinstance(h, int) and h == 0 and n < 4):
                    pe.wait_ge(low, h * PER_HEAD + (n - 3))
                count = min(4, i + 1 - 4 * j)
                for q in range(count):
                    k = 4 * j + q
                    m = nc.tensor.transpose(t_ps[n % 4][:, q, :], probs[s % 2][:, k * P:(k + 1) * P], ident[:, :])
                m.then_inc(turned, 1)

            def weigh(h, s, j):
                i = tiles[s]
                n = first[s] + j
                pe.wait_ge(low, h * PER_HEAD + (n + 1))
                if j == 0 and not (isinstance(h, int) and h == 0 and s < 2):
                    pe.wait_ge(y_done, h * NT + (s - 1))
                count = min(4, i + 1 - 4 * j)
                b = h % 2
                for q in range(count):
                    k = 4 * j + q
                    v = v_both[:, bass.ds(b, 1), k, :].rearrange("p a d -> p (a d)")
                    nc.tensor.matmul(o_ps[s % 2][:, 0:2 * HD], turned_hi[n % 4][:, q, :], v, start=(k == 0), stop=False)
                    m = nc.tensor.matmul(o_ps[s % 2][:, 0:2 * HD], turned_lo[n % 4][:, q, :], v, start=False, stop=(k == i))
                m.then_inc(weighed, 1)

            def head(h, last):
                pending = [] if isinstance(h, int) and h == 0 else [(h - 1, NT - DEPTH + d, 0) for d in range(DEPTH)]
                for s in range(NT):
                    i = tiles[s]
                    ahead = None
                    if s + AHEAD_Q < NT:
                        ahead = (h, s + AHEAD_Q)
                    elif not last:
                        ahead = (h + 1, s + AHEAD_Q - NT)
                    na = groups_of(tiles[ahead[1]]) if ahead else 0
                    for j in range(max(na, groups_of(i))):
                        if j < na:
                            score(*ahead, j)
                        if j < groups_of(i):
                            turn(h, s, j)
                            pending.append((h, s, j))
                        if len(pending) > DEPTH:
                            weigh(*pending.pop(0))
                while last and pending:
                    weigh(*pending.pop(0))

            pe.wait_ge(ones_set, 4)
            for s in range(AHEAD_Q):
                for j in range(groups_of(tiles[s])):
                    score(0, s, j)
            head(0, False)
            with pe.Fori(1, HEADS - 1) as h:
                head(h, False)
            head(HEADS - 1, True)
            for n in range(Y_TILES * NCH):
                f, c = divmod(n, NCH)
                if n == 0:
                    pe.wait_ge(y_done, HEADS * NT)
                if n >= 4:
                    pe.wait_ge(yT_copied[n % 2], (n - 4) // 2 + 1)
                for q in range(4):
                    m = nc.tensor.transpose(t_ps[n % 4][:, q, :], y[:, c * 4 + q, f * P:(f + 1) * P], ident[:, :])
                m.then_inc(y_turned, 1)

        @block.scalar
        def _(act):
            def exponent(h, s):
                i = tiles[s]
                act.wait_ge(moved, h * PER_HEAD + (first[s] + groups_of(i)))
                if not (isinstance(h, int) and h == 0 and s < 2):
                    before = first[s - 2] + groups_of(tiles[s - 2]) if s >= 2 else first[s - 2 + NT] + groups_of(tiles[s - 2 + NT]) - PER_HEAD
                    act.wait_ge(turned, h * PER_HEAD + before)
                    act.wait_ge(y_done, h * NT + (s - 3)) if (s >= 4 or not isinstance(h, int) or h > 0) else None
                width = (i + 1) * P
                nc.scalar.activation(probs[s % 2][:, 0:width], scores[s % RING][:, 0:width], ACT.Exp,
                                     bias=least[:, s % RING, groups_of(i) - 1:groups_of(i)], scale=-1.0,
                                     accum_out=row_sum[:, s % 4:s % 4 + 1]).then_inc(exped, 1)

            def high_part(h, s, j):
                n = first[s] + j
                act.wait_ge(turned, h * PER_HEAD + (n + 1))
                if not (isinstance(h, int) and h == 0 and n < 4):
                    act.wait_ge(weighed, h * PER_HEAD + (n - 3))
                count = min(4, tiles[s] + 1 - 4 * j)
                nc.scalar.copy(turned_hi[n % 4][:, 0:count, :], t_ps[n % 4][:, 0:count, :]).then_inc(high, 1)

            def head(h, last):
                for s in range(NT):
                    for j in range(groups_of(tiles[s])):
                        high_part(h, s, j)
                        if j == 0:
                            if s + 1 < NT:
                                exponent(h, s + 1)
                            elif not last:
                                exponent(h + 1, 0)

            exponent(0, 0)
            head(0, False)
            with act.Fori(1, HEADS - 1) as h:
                head(h, False)
            head(HEADS - 1, True)
            for n in range(1, Y_TILES * NCH, 2):
                f, c = divmod(n, NCH)
                act.wait_ge(y_turned, n + 1)
                nc.scalar.copy(scores[f][:, c * CH:(c + 1) * CH], t_ps[n % 4][:, :, :].rearrange("p a b -> p (a b)")).then_inc(yT_copied[1], 1)

        @block.vector
        def _(dve):
            dve.wait_ge(consts, 3)
            dve.tensor_copy(mask[:, :], mask_f[:, :]).then_inc(ones_set, 1)
            dve.tensor_copy(ident_r[:, :], ident[:, :]).then_inc(ones_set, 1)
            dve.tensor_copy(q_low[HD:HD + 2, :], ones_f[HD:HD + 2, :]).then_inc(ones_set, 1)
            dve.memset(least[:, :, :], 0.0).then_inc(ones_set, 1)

            def move(h, s, j):
                i = tiles[s]
                n = first[s] + j
                dve.wait_ge(scored, h * PER_HEAD + (n + 1))
                if j == 0 and not (isinstance(h, int) and h == 0 and s < RING):
                    dve.wait_ge(exped, h * NT + (s + 1 - RING))
                if j > 0:
                    dve.wait_ge(moved, h * PER_HEAD + n)
                width = min(CH, (i + 1) * P - j * CH)
                dve.tensor_scalar(scores[s % RING][:, j * CH:j * CH + width], s_ps[n % 2][:, 0:width], 1.0,
                                  3e38 if j == 0 else least[:, s % RING, j - 1:j], ALU.mult, ALU.min,
                                  accum_out=least[:, s % RING, j:j + 1]).then_inc(moved, 1)

            def low_part(h, s, j):
                n = first[s] + j
                dve.wait_ge(high, h * PER_HEAD + (n + 1))
                count = min(4, tiles[s] + 1 - 4 * j)
                dve.tensor_tensor(turned_lo[n % 4][:, 0:count, :], t_ps[n % 4][:, 0:count, :], turned_hi[n % 4][:, 0:count, :],
                                  ALU.subtract).then_inc(low, 1)

            def finish_a(h, s):
                dve.reciprocal(row_inv[:, s % 2:s % 2 + 1], row_sum[:, s % 4:s % 4 + 1]).then_inc(inverted, 1)

            def finish_b(h, s):
                dve.wait_ge(weighed, h * PER_HEAD + (first[s] + groups_of(tiles[s])))
                dve.wait_ge(inverted, h * NT + (s + 1))
                dve.tensor_scalar(y_part[:, s % 2, :], o_ps[s % 2][:, 0:HD], row_inv[:, s % 2:s % 2 + 1], None, ALU.mult).then_inc(half, 1)

            def finish_c(h, s):
                dve.wait_ge(half, h * NT + (s + 1))
                dve.scalar_tensor_tensor(out=y[:, tiles[s], bass.ds(h * HD, HD)], in0=o_ps[s % 2][:, HD:2 * HD], scalar=row_inv[:, s % 2:s % 2 + 1],
                                         in1=y_part[:, s % 2, :], op0=ALU.mult, op1=ALU.add).then_inc(y_done, 1)

            def head(h, last):
                begun = isinstance(h, int) and h == 0
                for s in range(NT):
                    i = tiles[s]
                    ahead = (h, s + AHEAD_Q) if s + AHEAD_Q < NT else (None if last else (h + 1, s + AHEAD_Q - NT))
                    na = groups_of(tiles[ahead[1]]) if ahead else 0
                    done = (h, s - 2) if s >= 2 else (None if begun else (h - 1, NT - 2 + s))
                    for j in range(max(na, groups_of(i))):
                        finishing = j == 0 and done
                        if finishing:
                            finish_a(*done)
                        if j < na:
                            move(*ahead, j)
                        if finishing:
                            finish_b(*done)
                        if j < groups_of(i):
                            low_part(h, s, j)
                        if finishing:
                            finish_c(*done)
                if last:
                    for s in (NT - 2, NT - 1):
                        finish_a(h, s)
                        finish_b(h, s)
                        finish_c(h, s)

            for s in range(AHEAD_Q):
                for j in range(groups_of(tiles[s])):
                    move(0, s, j)
            head(0, False)
            with dve.Fori(1, HEADS - 1) as h:
                head(h, False)
            head(HEADS - 1, True)
            for n in range(0, Y_TILES * NCH, 2):
                f, c = divmod(n, NCH)
                dve.wait_ge(y_turned, n + 1)
                dve.tensor_copy(scores[f][:, c * CH:(c + 1) * CH], t_ps[n % 4][:, :, :].rearrange("p a b -> p (a b)")).then_inc(yT_copied[0], 1)


BR_K = 4
N_BR = 3


def merge(nc, ones_col, w_branch, scratch):
    YT = N_BR * BR_K
    NF = KD
    with ExitStack() as ctx:
        def sb(name, shape, dt=F32):
            return ctx.enter_context(nc.sbuf_tensor("me_" + name, shape, dt))

        def sem(name):
            return ctx.enter_context(nc.semaphore("me_" + name))

        y_hi = [sb(f"y_hi{s}", [P, YT, CH], F32R) for s in range(3)]
        y_lo = [sb(f"y_lo{s}", [P, YT, CH], F32R) for s in range(3)]
        y_raw = [sb(f"y_raw{b}", [P, CH]) for b in range(2)]
        raw = [sb(f"w_raw{b}", [P, YT, P]) for b in range(2)]
        w_hi = [sb(f"w_hi{b}", [P, YT, P], F32R) for b in range(2)]
        w_lo = [sb(f"w_lo{b}", [P, YT, P], F32R) for b in range(2)]
        gate = [sb(f"gate{c}", [P, N_BR, CH]) for c in range(2)]
        part = sb("part", [P, CH])
        total = [sb(f"total{c}", [P, CH]) for c in range(2)]
        ps = [ctx.enter_context(nc.psum_tensor(f"me_ps{i}", [P, CH], F32)) for i in range(2 * N_BR)]
        w_loaded = [sem(f"w_loaded{b}") for b in range(2)]
        y_loaded = [sem(f"y_loaded{b}") for b in range(2)]
        g_loaded = [sem(f"g_loaded{c}") for c in range(2)]
        stored = [sem(f"stored{c}") for c in range(2)]
        w_split_hi, w_split, y_high, y_low = sem("w_split_hi"), sem("w_split"), sem("y_high"), sem("y_low")
        product, gated, added = sem("product"), sem("gated"), sem("added")
        block = ctx.enter_context(nc.Block())
        w_view = w_branch.rearrange("o b (k p) n -> p (o b k) n", p=P)
        g_view = scratch["gates"].rearrange("(b f) p s -> p f b s", b=N_BR)
        y_view = scratch["y"].rearrange("b k p s -> p (b k) s")

        @block.sync
        def _(sp):
            def load_y(c, j, b):
                r = j + c * YT
                if not (isinstance(r, int) and r < 2):
                    sp.wait_ge(y_low, r - 1)
                sp.dma_start(y_raw[b][:, :], y_view[:, bass.ds(j, 1), c * CH:(c + 1) * CH].rearrange("p a s -> p (a s)")).then_inc(y_loaded[b], 16)

            def load_w(half, f, b):
                t = f + half * NF
                if not (isinstance(t, int) and t < 2):
                    sp.wait_ge(w_split, t - 1)
                sp.dma_start(raw[b][:, :, :], w_view[:, :, bass.ds(f * P, P)]).then_inc(w_loaded[b], 16)

            def load_gates(half, f, c):
                n = (f + half * NF) * 2 + c
                if not (isinstance(n, int) and n < 2):
                    sp.wait_ge(gated, (n - 1) * N_BR)
                sp.dma_start(gate[c][:, :, :], g_view[:, bass.ds(f, 1), :, (2 * half + c) * CH:(2 * half + c + 1) * CH]
                             .rearrange("p f b s -> p (f b) s")).then_inc(g_loaded[c], 16)

            def store(half, f, c):
                n = (f + half * NF) * 2 + c
                sp.wait_ge(added, n * 2 + 2)
                sp.dma_start(scratch["merged"][bass.ds(f, 1), :, (2 * half + c) * CH:(2 * half + c + 1) * CH].rearrange("a p s -> (a p) s"),
                             total[c][:, :]).then_inc(stored[c], 16)

            load_w(0, 0, 0)
            for c in range(2):
                for j in range(YT):
                    load_y(c, j, j % 2)
                    if c == 0 and j == 3:
                        load_w(0, 1, 1)
                        load_gates(0, 0, 0)
                        load_gates(0, 0, 1)

            def features(half, i, last):
                for u in range(2):
                    f = i * 2 + u
                    if not last:
                        load_w(half, f + 2, u)
                    for c in range(2):
                        store(half, f, c)
                        if not (last and u == 1):
                            load_gates(half, f + 1, c)

            for half in range(2):
                if half == 1:
                    for j in range(YT):
                        load_y(3, j, j % 2)
                with sp.Fori(0, NF // 2 - 1) as i:
                    features(half, i, False)
                    if half == 0:
                        for j in range(4):
                            load_y(2, i * 4 + j, j % 2)
                if half == 0:
                    load_w(1, 0, 0)
                    load_w(1, 1, 1)
                    for u in range(2):
                        for c in range(2):
                            store(0, NF - 2 + u, c)
                            if u == 0:
                                load_gates(0, NF - 1, c)
                            else:
                                load_gates(1, 0, c)
                else:
                    features(1, NF // 2 - 1, True)
            for c in range(2):
                sp.wait_ge(stored[c], 16 * 2 * NF)

        @block.gpsimd
        def _(pool):
            def split(b, t):
                if isinstance(t, int):
                    pool.wait_ge(w_loaded[b], 16 * (t // 2 + 1))
                else:
                    pool.wait_ge(w_loaded[b], t * 8 + (16 - 8 * b))
                if not (isinstance(t, int) and t < 2):
                    pool.wait_ge(product, (t - 1) * (2 * N_BR))
                pool.tensor_tensor(w_hi[b][:, :, :], raw[b][:, :, :], ones_col[:, 0:1, None].broadcast_to(list(raw[b].shape)), ALU.mult).then_inc(w_split_hi, 1)
                pool.wait_ge(w_split_hi, t + 1)
                pool.tensor_tensor(w_lo[b][:, :, :], raw[b][:, :, :], w_hi[b][:, :, :], ALU.subtract).then_inc(w_split, 1)

            split(0, 0)
            split(1, 1)
            with pool.Fori(1, NF) as i:
                split(0, i * 2)
                split(1, i * 2 + 1)

        @block.tensor
        def _(pe):
            def features(half, i):
                for u in range(2):
                    t = i * 2 + (half * NF + u)
                    for c in range(2):
                        slot = (2 * half + c) % 3
                        for b in range(N_BR):
                            n = t * (2 * N_BR) + (c * N_BR + b)
                            if b == 0 and c == 0:
                                pe.wait_ge(w_split, t + 1)
                            if not (isinstance(t, int) and t == 0):
                                pe.wait_ge(gated, n - (2 * N_BR - 1))
                            elif half == 0:
                                pe.wait_ge(y_low, (c * YT) + BR_K * (b + 1))
                            if half == 1:
                                pe.wait_ge(y_low, (2 + c) * YT + BR_K * (b + 1))
                            q = 0
                            for k in range(b * BR_K, (b + 1) * BR_K):
                                for w, y in ((w_hi, y_hi), (w_hi, y_lo), (w_lo, y_hi)):
                                    m = nc.tensor.matmul(ps[c * N_BR + b][:, :], w[u][:, k, :], y[slot][:, k, :], start=(q == 0), stop=(q == 3 * BR_K - 1))
                                    q += 1
                            m.then_inc(product, 1)

            features(0, 0)
            with pe.Fori(1, NF // 2) as i:
                features(0, i)
            with pe.Fori(0, NF // 2) as i:
                features(1, i)

        def y_count(c, j):
            return j + c * YT

        @block.scalar
        def _(act):
            def high(c, j, b):
                r = y_count(c, j)
                if isinstance(r, int):
                    act.wait_ge(y_loaded[b], 16 * (r // 2 + 1))
                else:
                    act.wait_ge(y_loaded[b], r * 8 + (16 - 8 * b))
                nc.scalar.copy(y_hi[c % 3][:, bass.ds(j, 1), :].rearrange("p a s -> p (a s)"), y_raw[b][:, :]).then_inc(y_high, 1)

            for c in range(2):
                for j in range(YT):
                    high(c, j, j % 2)
            with act.Fori(0, 3) as i:
                for j in range(4):
                    high(2, i * 4 + j, j % 2)
            act.wait_ge(product, (NF - 1) * 2 * N_BR + N_BR)
            for j in range(YT):
                high(3, j, j % 2)

        @block.vector
        def _(dve):
            def low(c, j, b):
                r = y_count(c, j)
                dve.wait_ge(y_high, r + 1)
                view = lambda t: t[c % 3][:, bass.ds(j, 1), :].rearrange("p a s -> p (a s)")
                dve.tensor_tensor(view(y_lo), y_raw[b][:, :], view(y_hi), ALU.subtract).then_inc(y_low, 1)

            def gate_and_add(t, c):
                for b in range(N_BR):
                    n = t * (2 * N_BR) + (c * N_BR + b)
                    dve.wait_ge(product, n + 1)
                    if b == 0:
                        dve.wait_ge(g_loaded[c], t * 16 + 16)
                        if not (isinstance(t, int) and t == 0):
                            dve.wait_ge(stored[c], t * 16)
                    else:
                        dve.wait_ge(added, t * 4 + (2 * c + b - 1)) if not (isinstance(t, int) and t == 0 and c == 0 and b == 1) else None
                    dst = total[c] if b == 0 else part
                    dve.tensor_tensor(dst[:, :], ps[c * N_BR + b][:, :], gate[c][:, b, :], ALU.mult).then_inc(gated, 1)
                    if b > 0:
                        dve.wait_ge(gated, n + 1)
                        dve.tensor_tensor(total[c][:, :], total[c][:, :], part[:, :], ALU.add).then_inc(added, 1)

            for c in range(2):
                for j in range(YT):
                    low(c, j, j % 2)
            for u in range(2):
                for c in range(2):
                    gate_and_add(u, c)
            for j in range(4):
                low(2, j, j % 2)
            with dve.Fori(1, 3) as i:
                for u in range(2):
                    for c in range(2):
                        gate_and_add(i * 2 + u, c)
                for j in range(4):
                    low(2, i * 4 + j, j % 2)
            for u in range(2):
                for c in range(2):
                    gate_and_add(6 + u, c)
            for j in range(YT):
                low(3, j, j % 2)
            with dve.Fori(NF // 2, NF) as i:
                for u in range(2):
                    for c in range(2):
                        gate_and_add(i * 2 + u, c)


N_GROUP, PER_GROUP = 4, 8
N_EXP = N_GROUP * PER_GROUP
N_LOGIT = N_GROUP + N_EXP
TOP = 2
BLOCKS = (S * TOP) // P + N_EXP
AHEAD = 4
TABLE = BLOCKS + AHEAD
PAD = 16384


def project_out(nc, ones_col, x, w_out, g_ffn, w_rg, b_rg, w_re, b_re, ident, logits, scratch):
    with ExitStack() as ctx:
        def sb(name, shape, dt=F32):
            return ctx.enter_context(nc.sbuf_tensor("po_" + name, shape, dt))

        def sem(name):
            return ctx.enter_context(nc.semaphore("po_" + name))

        w_raw = [sb(f"w_raw{b}", [P, D]) for b in range(2)]
        w_hi, w_lo = sb("w_hi", [P, KD, D], F32R), sb("w_lo", [P, KD, D], F32R)
        m_raw = [sb(f"m_raw{b}", [P, KD, P]) for b in range(2)]
        m_hi = [sb(f"m_hi{b}", [P, KD, P], F32R) for b in range(2)]
        m_lo = [sb(f"m_lo{b}", [P, KD, P], F32R) for b in range(2)]
        xt = [sb(f"x{b}", [P, D]) for b in range(2)]
        x2 = [sb(f"x2{b}", [P, D]) for b in range(2)]
        h2 = [sb(f"h2{b}", [P, D]) for b in range(2)]
        h2T = [sb(f"h2T{b}", [P, KD, P]) for b in range(2)]
        squares = sb("squares", [P, D])
        gain = sb("gain", [P, D])
        w_route = sb("w_route", [P, KD, N_LOGIT])
        b_route = sb("b_route", [P, N_LOGIT])
        sums, rms, rstd = sb("sums", [P, 2]), sb("rms", [P, 2]), sb("rstd", [P, 2])
        eps = sb("eps", [P, 1])
        o_ps = [[ctx.enter_context(nc.psum_tensor(f"po_o{b}{j}", [P, CH], F32)) for j in range(2)] for b in range(2)]
        t_ps = [ctx.enter_context(nc.psum_tensor(f"po_t{j}", [P, 4, P], F32)) for j in range(2)]
        r_ps = [ctx.enter_context(nc.psum_tensor(f"po_r{b}", [P, CH], F32)) for b in range(2)]
        params, eps_set = sem("params"), sem("eps_set")
        w_loaded = [sem(f"w_loaded{b}") for b in range(2)]
        m_loaded = [sem(f"m_loaded{b}") for b in range(2)]
        x2_stored = [sem(f"x2_stored{b}") for b in range(2)]
        h2_stored = [sem(f"h2_stored{b}") for b in range(2)]
        w_high, w_low, m_high, m_low = sem("w_high"), sem("w_low"), sem("m_high"), sem("m_low")
        product, x2_half, squared, rooted, inverted, h2_done = (sem("product"), sem("x2_half"), sem("squared"), sem("rooted"),
                                                                sem("inverted"), sem("h2_done"))
        turned, copied, routed, logged = sem("turned"), sem("copied"), sem("routed"), sem("logged")
        block = ctx.enter_context(nc.Block())
        m_view = scratch["merged"].rearrange("f p s -> p f s")

        def rows(ap, i):
            return ap[bass.ds(i * P, P), :]

        @block.sync
        def _(sp):
            def load_tile(i, b):
                if not isinstance(i, int) or i >= 2:
                    sp.wait_ge(x2_half, i * 2 - 2)
                    sp.wait_ge(m_low, i - 1)
                sp.dma_start(m_raw[b][:, :, :], m_view[:, :, bass.ds(i * P, P)]).then_inc(m_loaded[b], 16)
                sp.dma_start(xt[b][:, :], rows(x, i)).then_inc(m_loaded[b], 16)

            def store_tile(i, b):
                sp.wait_ge(x2_half, i * 2 + 2)
                sp.dma_start(rows(scratch["x2"], i), x2[b][:, :]).then_inc(x2_stored[b], 16)
                sp.wait_ge(h2_done, i + 1)
                sp.dma_start(rows(scratch["h2"], i), h2[b][:, :]).then_inc(h2_stored[b], 16)

            load_tile(0, 0)
            for k in range(KD):
                if k >= 2:
                    sp.wait_ge(w_low, k - 1)
                sp.dma_start(w_raw[k % 2][:, :], w_out[0, k * P:(k + 1) * P, :]).then_inc(w_loaded[k % 2], 16)
            with nc.allow_non_contiguous_dma("small parameters"):
                sp.dma_start(gain[:, :], g_ffn.rearrange("o d -> (o d)").partition_broadcast(P)).then_inc(params, 16)
                sp.dma_start(b_route[:, 0:N_GROUP], b_rg.rearrange("o d -> (o d)").partition_broadcast(P)).then_inc(params, 16)
                sp.dma_start(b_route[:, N_GROUP:N_LOGIT], b_re.rearrange("o d -> (o d)").partition_broadcast(P)).then_inc(params, 16)
                sp.dma_start(w_route[:, :, 0:N_GROUP], w_rg.rearrange("o (k p) n -> p (o k) n", p=P)).then_inc(params, 16)
                sp.dma_start(w_route[:, :, N_GROUP:N_LOGIT], w_re.rearrange("o (k p) n -> p (o k) n", p=P)).then_inc(params, 16)
            load_tile(1, 1)
            with sp.Fori(0, NT // 2 - 1) as i:
                for b in range(2):
                    store_tile(i * 2 + b, b)
                    load_tile(i * 2 + (b + 2), b)
            for b in range(2):
                store_tile(NT - 2 + b, b)
            for b in range(2):
                sp.wait_ge(x2_stored[b], 16 * NT // 2)
                sp.wait_ge(h2_stored[b], 16 * NT // 2)

        @block.gpsimd
        def _(pool):
            pool.memset(eps[:, :], EPS).then_inc(eps_set, 1)

            def split(i, b):
                if isinstance(i, int):
                    pool.wait_ge(m_loaded[b], 32 * (i // 2 + 1))
                else:
                    pool.wait_ge(m_loaded[b], i * 16 + (32 - 16 * b))
                if not isinstance(i, int) or i >= 2:
                    pool.wait_ge(product, i * 2 - 2)
                pool.tensor_tensor(m_hi[b][:, :, :], m_raw[b][:, :, :], ones_col[:, 0:1, None].broadcast_to([P, KD, P]), ALU.mult).then_inc(m_high, 1)
                pool.wait_ge(m_high, i + 1)
                pool.tensor_tensor(m_lo[b][:, :, :], m_raw[b][:, :, :], m_hi[b][:, :, :], ALU.subtract).then_inc(m_low, 1)

            split(0, 0)
            split(1, 1)
            with pool.Fori(1, NT // 2) as i:
                split(i * 2, 0)
                split(i * 2 + 1, 1)

        @block.tensor
        def _(pe):
            def out_product(i, b):
                pe.wait_ge(m_low, i + 1)
                if not isinstance(i, int) or i >= 2:
                    pe.wait_ge(x2_half, i * 2 - 2)
                for j in range(2):
                    cols = slice(j * CH, (j + 1) * CH)
                    n = 0
                    for k in range(KD):
                        if isinstance(i, int) and i == 0 and j == 0:
                            pe.wait_ge(w_low, k + 1)
                        for m, w in ((m_hi, w_hi), (m_hi, w_lo), (m_lo, w_hi)):
                            q = nc.tensor.matmul(o_ps[b][j][:, :], m[b][:, k, :], w[:, k, cols], start=(n == 0), stop=(n == 3 * KD - 1))
                            n += 1
                    q.then_inc(product, 1)

            def route(i, b):
                pe.wait_ge(h2_done, i + 1)
                for j in range(2):
                    if not (isinstance(i, int) and i == 0):
                        pe.wait_ge(copied, i * 2 + (j - 1))
                    for q in range(4):
                        k = 4 * j + q
                        m = nc.tensor.transpose(t_ps[j][:, q, :], h2[b][:, k * P:(k + 1) * P], ident[:, :])
                    m.then_inc(turned, 1)
                pe.wait_ge(copied, i * 2 + 2)
                if not isinstance(i, int) or i >= 2:
                    pe.wait_ge(logged, i - 1)
                for k in range(KD):
                    m = nc.tensor.matmul(r_ps[b][:, 0:N_LOGIT], h2T[b][:, k, :], w_route[:, k, :], start=(k == 0), stop=(k == KD - 1))
                m.then_inc(routed, 1)

            out_product(0, 0)
            out_product(1, 1)
            route(0, 0)
            pe.wait_ge(params, 80)
            with pe.Fori(1, NT // 2) as i:
                for b in range(2):
                    out_product(i * 2 + b, b)
                    route(i * 2 + (b - 1), 1 - b)
            route(NT - 1, 1)

        @block.scalar
        def _(act):
            for k in range(KD):
                act.wait_ge(w_loaded[k % 2], 16 * (k // 2 + 1))
                nc.scalar.copy(w_hi[:, k, :], w_raw[k % 2][:, :]).then_inc(w_high, 1)
            act.wait_ge(eps_set, 1)

            def root(i, b):
                act.wait_ge(x2_half, i * 2 + 2)
                if not (isinstance(i, int) and i == 0):
                    act.wait_ge(rooted, i)
                nc.scalar.activation(squares[:, :], x2[b][:, :], ACT.Square, accum_out=sums[:, b:b + 1]).then_inc(squared, 1)
                act.wait_ge(squared, i + 1)
                if not isinstance(i, int) or i >= 2:
                    act.wait_ge(inverted, i - 1)
                nc.scalar.activation(rms[:, b:b + 1], sums[:, b:b + 1], ACT.Sqrt, bias=eps[:, 0:1], scale=1.0 / D).then_inc(rooted, 1)

            def copy_turned(i, b):
                for j in range(2):
                    act.wait_ge(turned, i * 2 + (j + 1))
                    if not isinstance(i, int) or i >= 2:
                        act.wait_ge(routed, i - 1)
                    nc.scalar.copy(h2T[b][:, 4 * j:4 * j + 4, :], t_ps[j][:, :, :]).then_inc(copied, 1)

            root(0, 0)
            root(1, 1)
            copy_turned(0, 0)
            with act.Fori(1, NT // 2) as i:
                for b in range(2):
                    root(i * 2 + b, b)
                    copy_turned(i * 2 + (b - 1), 1 - b)
            copy_turned(NT - 1, 1)

        @block.vector
        def _(dve):
            for k in range(KD):
                dve.wait_ge(w_high, k + 1)
                dve.tensor_tensor(w_lo[:, k, :], w_raw[k % 2][:, :], w_hi[:, k, :], ALU.subtract).then_inc(w_low, 1)
            dve.wait_ge(params, 80)

            def residual(i, b):
                for j in range(2):
                    dve.wait_ge(product, i * 2 + (j + 1))
                    if j == 0:
                        if isinstance(i, int):
                            dve.wait_ge(m_loaded[b], 32 * (i // 2 + 1))
                        else:
                            dve.wait_ge(m_loaded[b], i * 16 + (32 - 16 * b))
                        if isinstance(i, int) and i < 2:
                            pass
                        elif isinstance(i, int):
                            dve.wait_ge(x2_stored[b], 16 * (i // 2))
                        else:
                            dve.wait_ge(x2_stored[b], i * 8 - 8 * b)
                    cols = slice(j * CH, (j + 1) * CH)
                    dve.tensor_tensor(x2[b][:, cols], o_ps[b][j][:, :], xt[b][:, cols], ALU.add).then_inc(x2_half, 1)
                dve.wait_ge(rooted, i + 1)
                dve.reciprocal(rstd[:, b:b + 1], rms[:, b:b + 1]).then_inc(inverted, 1)
                dve.wait_ge(inverted, i + 1)
                if not isinstance(i, int) or i >= 2:
                    dve.wait_ge(h2_stored[b], i * 8 - 8 * b)
                    dve.wait_ge(turned, i * 2 - 2)
                dve.scalar_tensor_tensor(out=h2[b][:, :], in0=x2[b][:, :], scalar=rstd[:, b:b + 1], in1=gain[:, :],
                                         op0=ALU.mult, op1=ALU.mult).then_inc(h2_done, 1)

            def log(i, b):
                dve.wait_ge(routed, i + 1)
                dve.tensor_tensor(logits[:, bass.ds(i, 1), :].rearrange("p a n -> p (a n)"), r_ps[b][:, 0:N_LOGIT], b_route[:, :], ALU.add).then_inc(logged, 1)

            residual(0, 0)
            residual(1, 1)
            log(0, 0)
            with dve.Fori(1, NT // 2) as i:
                for b in range(2):
                    residual(i * 2 + b, b)
                    log(i * 2 + (b - 1), 1 - b)
            log(NT - 1, 1)
            dve.wait_ge(logged, NT)


def route(nc, logits, gates, slots, plan, scratch=None):
    with ExitStack() as ctx:
        def sb(name, shape, dt=F32):
            return ctx.enter_context(nc.sbuf_tensor("ro_" + name, shape, dt))

        def sem(name):
            return ctx.enter_context(nc.semaphore("ro_" + name))

        g_max, g_sum, pick = sb("g_max", [P, NT, 1]), sb("g_sum", [P, NT, 1]), sb("pick", [P, NT, 1])
        g_rel, g_exp, g_cand, g_one = (sb(n, [P, NT, N_GROUP]) for n in ("g_rel", "g_exp", "g_cand", "g_one"))
        masked = sb("masked", [P, NT, N_GROUP, PER_GROUP])
        le, le_rest, cand = (sb(n, [P, NT, PER_GROUP]) for n in ("le", "le_rest", "cand"))
        best = [sb(f"best{c}", [P, NT, 1]) for c in range(TOP)]
        one = [sb(f"one{c}", [P, NT, PER_GROUP]) for c in range(TOP)]
        onehot = [sb(f"onehot{c}", [P, NT, N_EXP]) for c in range(TOP)]
        both = sb("both", [P, NT, N_EXP])
        ratio, total = sb("ratio", [P, NT, 1]), sb("total", [P, NT, 1])
        run_a, run_b = sb("run_a", [P, NT, N_EXP]), sb("run_b", [P, NT, N_EXP])
        tile_totals = sb("tile_totals", [P, NT, N_EXP])
        place = sb("place", [P, NT, N_EXP])
        count_i, blocks_f, ends, starts = sb("count_i", [P, N_EXP], I32), sb("blocks_f", [P, N_EXP]), sb("ends", [P, N_EXP]), sb("starts", [P, N_EXP])
        zeros32 = sb("zeros32", [P, N_EXP])
        dest = sb("dest", [P, TOP, NT])
        dest_i, row_i, block_i = (sb(n, [P, TOP, NT], I32) for n in ("dest_i", "row_i", "block_i"))
        row_f, block_f = sb("row_f", [P, TOP, NT]), sb("block_f", [P, TOP, NT])
        index8 = sb("index8", [P, 1, PER_GROUP])
        index_row, index_block = sb("index_row", [P, P]), sb("index_block", [P, TABLE, 1])
        name = sb("name", [P, TOP, NT])
        before = sb("before", [P, P])
        ones = sb("ones", [P, P])
        cmp = sb("cmp", [P, TABLE, N_EXP])
        expert, fresh, runs = sb("expert", [P, TABLE, 1]), sb("fresh", [P, TABLE]), sb("runs", [P, TABLE])
        zeros_b = sb("zeros_b", [P, TABLE])
        runs_i = sb("runs_i", [P, TABLE], I32)
        row_hot = [sb(f"row_hot{b}", [P, P]) for b in range(4)]
        block_hot = [sb(f"block_hot{b}", [P, TABLE]) for b in range(4)]
        slot_f, slot_pad = sb("slot_f", [P, TABLE]), sb("slot_pad", [P, TABLE])
        ps_before = ctx.enter_context(nc.psum_tensor("ro_ps_before", [P, NT, N_EXP], F32))
        ps_total = ctx.enter_context(nc.psum_tensor("ro_ps_total", [P, NT, N_EXP], F32))
        ps_slot = ctx.enter_context(nc.psum_tensor("ro_ps_slot", [P, CH], F32))
        consts, chain, asked, counted, exped = sem("consts"), sem("chain"), sem("asked"), sem("counted"), sem("exped")
        hot, placed = sem("hot"), sem("placed")
        block = ctx.enter_context(nc.Block())

        @block.gpsimd
        def _(pool):
            n = [0]

            def step(m):
                m.then_inc(consts, 1)
                n[0] += 1
                pool.wait_ge(consts, n[0])

            kw = dict(channel_multiplier=0, allow_small_or_imprecise_dtypes=True)
            step(pool.iota(index8[:, :, :], pattern=[[1, PER_GROUP]], base=0, **kw))
            step(pool.iota(index_row[:, :], pattern=[[1, P]], base=0, **kw))
            step(pool.iota(index_block[:, :, :], pattern=[[1, TABLE]], base=0, **kw))
            kw["channel_multiplier"] = 1
            step(pool.iota(name[:, :, :], pattern=[[S, TOP], [P, NT]], base=1, **kw))
            step(pool.memset(ones[:, :], 1.0))
            step(pool.memset(zeros32[:, :], 0.0))
            step(pool.memset(zeros_b[:, :], 0.0))
            step(pool.memset(before[:, :], 1.0))
            step(pool.affine_select(out=before[:, :], in_=before[:, :], compare_op=ALU.is_gt, fill=0.0, base=0,
                                    pattern=[[1, P]], channel_multiplier=-1))

        @block.scalar
        def _(act):
            act.wait_ge(asked, 1)
            nc.scalar.activation(g_exp[:, :, :], g_rel[:, :, :], ACT.Exp).then_inc(exped, 1)
            act.wait_ge(asked, 2)
            nc.scalar.activation(ratio[:, :, :], ratio[:, :, :], ACT.Exp).then_inc(exped, 1)

        @block.vector
        def _(dve):
            n = [0]

            def step(m):
                m.then_inc(chain, 1)
                n[0] += 1
                dve.wait_ge(chain, n[0])

            lg = logits[:, :, 0:N_GROUP]
            lexp = logits[:, :, N_GROUP:N_LOGIT].rearrange("p t (g e) -> p t g e", g=N_GROUP)
            dve.wait_ge(consts, 9)
            step(dve.tensor_reduce(g_max[:, :, :], lg, AX.X, ALU.max))
            dve.tensor_tensor(g_rel[:, :, :], lg, g_max[:, :, :].broadcast_to([P, NT, N_GROUP]), ALU.subtract).then_inc(asked, 1)
            dve.wait_ge(asked, 1)
            step(dve.tensor_scalar(g_cand[:, :, :], g_rel[:, :, :], 0.0, -64.0, ALU.is_ge, ALU.mult))
            step(dve.tensor_tensor(g_cand[:, :, :], g_cand[:, :, :], index8[:, :, 0:N_GROUP].broadcast_to([P, NT, N_GROUP]), ALU.add))
            step(dve.tensor_reduce(pick[:, :, :], g_cand[:, :, :], AX.X, ALU.min))
            step(dve.tensor_tensor(g_one[:, :, :], g_cand[:, :, :], pick[:, :, :].broadcast_to([P, NT, N_GROUP]), ALU.is_equal))
            for g in range(N_GROUP):
                step(dve.tensor_tensor(masked[:, :, g, :], lexp[:, :, g, :], g_one[:, :, g:g + 1].broadcast_to([P, NT, PER_GROUP]), ALU.mult))
            step(dve.tensor_reduce(le[:, :, :], masked[:, :, :, :].rearrange("p t g e -> p t e g"), AX.X, ALU.add))
            src = le
            for c in range(TOP):
                step(dve.tensor_reduce(best[c][:, :, :], src[:, :, :], AX.X, ALU.max))
                step(dve.tensor_tensor(cand[:, :, :], src[:, :, :], best[c][:, :, :].broadcast_to([P, NT, PER_GROUP]), ALU.is_ge))
                step(dve.scalar_tensor_tensor(out=cand[:, :, :], in0=cand[:, :, :], scalar=-64.0, in1=index8[:, :, :].broadcast_to([P, NT, PER_GROUP]),
                                              op0=ALU.mult, op1=ALU.add))
                step(dve.tensor_reduce(pick[:, :, :], cand[:, :, :], AX.X, ALU.min))
                step(dve.tensor_tensor(one[c][:, :, :], cand[:, :, :], pick[:, :, :].broadcast_to([P, NT, PER_GROUP]), ALU.is_equal))
                if c == 0:
                    step(dve.scalar_tensor_tensor(out=le_rest[:, :, :], in0=one[c][:, :, :], scalar=-1e30, in1=le[:, :, :],
                                                  op0=ALU.mult, op1=ALU.add))
                    src = le_rest
                for g in range(N_GROUP):
                    step(dve.tensor_tensor(onehot[c][:, :, g * PER_GROUP:(g + 1) * PER_GROUP], one[c][:, :, :],
                                           g_one[:, :, g:g + 1].broadcast_to([P, NT, PER_GROUP]), ALU.mult))
            dve.tensor_tensor(both[:, :, :], onehot[0][:, :, :], onehot[1][:, :, :], ALU.add).then_inc(hot, 1)
            dve.tensor_tensor(ratio[:, :, :], best[1][:, :, :], best[0][:, :, :], ALU.subtract).then_inc(asked, 1)
            dve.wait_ge(exped, 2)
            step(dve.tensor_reduce(g_sum[:, :, :], g_exp[:, :, :], AX.X, ALU.add))
            step(dve.tensor_scalar(total[:, :, :], ratio[:, :, :], 1.0, None, ALU.add))
            step(dve.tensor_tensor(total[:, :, :], total[:, :, :], g_sum[:, :, :], ALU.mult))
            step(dve.reciprocal(gates[:, :, 0:1], total[:, :, :]))
            step(dve.tensor_tensor(gates[:, :, 1:2], gates[:, :, 0:1], ratio[:, :, :], ALU.mult))
            dve.wait_ge(counted, 2)
            step(dve.tensor_copy(tile_totals[:, :, :], ps_total[:, :, :]))
            src, dst, gap = tile_totals, run_a, 1
            while gap < NT:
                step(dve.tensor_copy(dst[:, 0:gap, :], src[:, 0:gap, :]))
                step(dve.tensor_tensor(dst[:, gap:NT, :], src[:, gap:NT, :], src[:, 0:NT - gap, :], ALU.add))
                src, dst, gap = dst, (run_b if dst is run_a else run_a), gap * 2
            step(dve.tensor_scalar(blocks_f[:, :], src[:, NT - 1, :], float(P - 1), None, ALU.add))
            step(dve.tensor_copy(count_i[:, :], blocks_f[:, :]))
            step(dve.tensor_scalar(count_i[:, :], count_i[:, :], P.bit_length() - 1, None, ALU.arith_shift_right))
            step(dve.tensor_copy(blocks_f[:, :], count_i[:, :]))
            step(dve.tensor_tensor_scan(ends[:, :], blocks_f[:, :], zeros32[:, :], 0.0, ALU.add, ALU.add))
            step(dve.tensor_tensor(starts[:, :], ends[:, :], blocks_f[:, :], ALU.subtract))
            step(dve.tensor_tensor(place[:, :, :], src[:, :, :], tile_totals[:, :, :], ALU.subtract))
            step(dve.tensor_tensor(place[:, :, :], place[:, :, :], ps_before[:, :, :], ALU.add))
            step(dve.tensor_scalar(starts[:, :], starts[:, :], float(P), None, ALU.mult))
            for t in range(NT):
                m = dve.tensor_tensor(place[:, t, :], place[:, t, :], starts[:, :], ALU.add)
            step(m)
            for c in range(TOP):
                step(dve.tensor_tensor(both[:, :, :], onehot[c][:, :, :], place[:, :, :], ALU.mult))
                step(dve.tensor_reduce(dest[:, c, :].rearrange("p (t a) -> p t a", a=1), both[:, :, :], AX.X, ALU.add))
            step(dve.tensor_copy(dest_i[:, :, :], dest[:, :, :]))
            step(dve.tensor_scalar(row_i[:, :, :], dest_i[:, :, :], P - 1, None, ALU.bitwise_and))
            step(dve.tensor_scalar(block_i[:, :, :], dest_i[:, :, :], P.bit_length() - 1, None, ALU.arith_shift_right))
            step(dve.tensor_copy(row_f[:, :, :], row_i[:, :, :]))
            step(dve.tensor_copy(block_f[:, :, :], block_i[:, :, :]))
            for q in range(TOP * NT):
                c, t = divmod(q, NT)
                if q >= 4:
                    dve.wait_ge(placed, q - 3)
                dve.tensor_scalar(row_hot[q % 4][:, :], index_row[:, :], row_f[:, c, t:t + 1], None, ALU.is_equal)
                dve.tensor_scalar(block_hot[q % 4][:, :], index_block[:, :, :].rearrange("p b a -> p (b a)"), block_f[:, c, t:t + 1],
                                  name[:, c, t:t + 1], ALU.is_equal, ALU.mult).then_inc(hot, 1)
            for e in range(N_EXP):
                m = dve.tensor_scalar(cmp[:, :, e], index_block[:, :, :].rearrange("p b a -> p (b a)"), ends[:, e:e + 1], None, ALU.is_ge)
            step(m)
            step(dve.tensor_reduce(expert[:, :, :], cmp[:, :, :], AX.X, ALU.add))
            ex = expert[:, :, :].rearrange("p b a -> p (b a)")
            step(dve.tensor_scalar(ex, ex, float(N_EXP - 1), None, ALU.min))
            step(dve.memset(fresh[:, 0:1], 1.0))
            step(dve.tensor_tensor(fresh[:, 1:TABLE], ex[:, 1:TABLE], ex[:, 0:TABLE - 1], ALU.not_equal))
            step(dve.tensor_tensor_scan(runs[:, :], fresh[:, :], zeros_b[:, :], 1.0, ALU.add, ALU.add))
            step(dve.tensor_copy(runs_i[:, :], runs[:, :]))
            step(dve.tensor_scalar(plan[:, 1, :], runs_i[:, :], 1, None, ALU.bitwise_and))
            step(dve.tensor_copy(plan[:, 0, :], ex))
            step(dve.tensor_copy(plan[:, 2, :], fresh[:, :]))
            step(dve.tensor_copy(plan[:, 3, :], ends[:, N_EXP - 1:N_EXP].broadcast_to([P, TABLE])))
            step(dve.tensor_scalar(plan[:, 3, :], plan[:, 3, :], 1, None, ALU.add))
            step(dve.tensor_scalar(plan[:, 3, :], plan[:, 3, :], 1, None, ALU.arith_shift_right))
            dve.wait_ge(placed, TOP * NT)
            step(dve.tensor_scalar(slot_pad[:, :], ps_slot[:, 0:TABLE], 0.0, float(PAD), ALU.is_equal, ALU.mult))
            step(dve.scalar_tensor_tensor(out=slot_f[:, :], in0=ps_slot[:, 0:TABLE], scalar=-1.0, in1=slot_pad[:, :], op0=ALU.add, op1=ALU.add))
            step(dve.tensor_copy(slots[:, 0, :], slot_f[:, :]))
            step(dve.tensor_scalar(slots[:, 1, :], slots[:, 0, :], S - 1, None, ALU.bitwise_and))

        @block.tensor
        def _(pe):
            pe.wait_ge(consts, 9)
            pe.wait_ge(hot, 1)
            flat = both[:, :, :].rearrange("p t e -> p (t e)")
            nc.tensor.matmul(ps_before[:, :, :].rearrange("p t e -> p (t e)"), before[:, :], flat, start=True, stop=True).then_inc(counted, 1)
            nc.tensor.matmul(ps_total[:, :, :].rearrange("p t e -> p (t e)"), ones[:, :], flat, start=True, stop=True).then_inc(counted, 1)
            for q in range(TOP * NT):
                pe.wait_ge(hot, q + 2)
                nc.tensor.matmul(ps_slot[:, 0:TABLE], row_hot[q % 4][:, :], block_hot[q % 4][:, :],
                                 start=(q == 0), stop=(q == TOP * NT - 1)).then_inc(placed, 1)


FE = 256
FK = FE // P


def experts(nc, w1, w3, w2, ident, slots, plan, scratch):
    with ExitStack() as ctx:
        def sb(name, shape, dt=F32):
            return ctx.enter_context(nc.sbuf_tensor("ex_" + name, shape, dt))

        def sem(name):
            return ctx.enter_context(nc.semaphore("ex_" + name))

        raw_in = sb("raw_in", [P, 2, KD, 2 * FE])
        raw_out = sb("raw_out", [P, 2, FK, D])
        in_hi = [sb(f"in_hi{b}", [P, KD, 2 * FE], F32R) for b in range(2)]
        in_lo = [sb(f"in_lo{b}", [P, KD, 2 * FE], F32R) for b in range(2)]
        out_hi = [sb(f"out_hi{b}", [P, FK, D], F32R) for b in range(2)]
        out_lo = [sb(f"out_lo{b}", [P, FK, D], F32R) for b in range(2)]
        x = [sb(f"x{b}", [P, D]) for b in range(2)]
        xT_hi = [sb(f"xT_hi{b}", [P, KD, P], F32R) for b in range(2)]
        xT_lo = [sb(f"xT_lo{b}", [P, KD, P], F32R) for b in range(2)]
        act_part, inner = sb("act_part", [P, FE]), sb("inner", [P, FE])
        iT_hi = [sb(f"iT_hi{b}", [P, FK, P], F32R) for b in range(2)]
        iT_lo = [sb(f"iT_lo{b}", [P, FK, P], F32R) for b in range(2)]
        y = [sb(f"y{b}", [P, D]) for b in range(2)]
        fetch = [sb(f"fetch{b}", [P, 1], I32) for b in range(2)]
        put = [sb(f"put{b}", [P, 1], I32) for b in range(2)]
        x_ps = [ctx.enter_context(nc.psum_tensor(f"ex_ps_x{j}", [P, 4, P], F32)) for j in range(2)]
        h_ps = [ctx.enter_context(nc.psum_tensor(f"ex_ps_h{b}", [P, 2 * FE], F32)) for b in range(2)]
        i_ps = ctx.enter_context(nc.psum_tensor("ex_ps_i", [P, 4, P], F32))
        y_ps = [ctx.enter_context(nc.psum_tensor(f"ex_ps_y{j}", [P, CH], F32)) for j in range(2)]
        w_loaded = [sem(f"w_loaded{b}") for b in range(2)]
        fetched = [sem(f"fetched{b}") for b in range(2)]
        stored = [sem(f"stored{b}") for b in range(2)]
        fetch_set, put_set, may_move = sem("fetch_set"), sem("put_set"), sem("may_move")
        in_high, in_low, out_high, out_low = sem("in_high"), sem("in_low"), sem("out_high"), sem("out_low")
        x_turned, x_high, x_low = sem("x_turned"), sem("x_high"), sem("x_low")
        inner_done, silu_done, inner_set, i_turned, i_high, i_low = (sem("inner_done"), sem("silu_done"), sem("inner_set"),
                                                                     sem("i_turned"), sem("i_high"), sem("i_low"))
        y_product, y_copied = sem("y_product"), sem("y_copied")
        block = ctx.enter_context(nc.Block())
        w1_v = w1.rearrange("o e (k p) f -> (o e) p k f", p=P)
        w3_v = w3.rearrange("o e (k p) f -> (o e) p k f", p=P)
        w2_v = w2.rearrange("o e (k p) n -> (o e) p k n", p=P)
        LOADS = 3 * 16

        def past(b, first):
            return b >= first if isinstance(b, int) else True

        def wait_pair(eng, sems, b, u, each):
            if isinstance(b, int):
                eng.wait_ge(sems[u], each * (b // 2 + 1))
            else:
                eng.wait_ge(sems[u], b * (each // 2) + (each - each // 2 * u))

        def pairs_of(eng):
            return eng.value_load(plan[0:1, 3, 0:1], min_val=S * TOP // P // 2, max_val=BLOCKS // 2)

        def buffer_of(eng, b):
            return eng.value_load(plan[0:1, 1, bass.ds(b, 1)], min_val=0, max_val=1)

        @block.sync
        def _(sp):
            def load(b, u):
                e = sp.value_load(plan[0:1, 0, bass.ds(b, 1)], min_val=0, max_val=N_EXP - 1)
                r = buffer_of(sp, b)
                new = sp.value_load(plan[0:1, 2, bass.ds(b, 1)], min_val=0, max_val=1)
                if not isinstance(b, int) or b >= 2:
                    sp.wait_ge(in_low, b * KD - KD)
                kw = dict(cond=(new > 0), bounds_check="skip_entire_dma")
                flat = lambda ap: ap.rearrange("p a k n -> p (a k) n")
                src = lambda w: w[bass.ds(e, 1)].rearrange("a p k n -> p (a k) n")
                sp.dma_start(flat(raw_in[:, bass.ds(r, 1), :, 0:FE]), src(w1_v), **kw).then_inc(w_loaded[u], 16)
                sp.dma_start(flat(raw_in[:, bass.ds(r, 1), :, FE:2 * FE]), src(w3_v), **kw).then_inc(w_loaded[u], 16)
                if not isinstance(b, int) or b >= 2:
                    sp.wait_ge(out_low, b - 1)
                sp.dma_start(flat(raw_out[:, bass.ds(r, 1), :, :]), src(w2_v), **kw).then_inc(w_loaded[u], 16)

            pairs = pairs_of(sp)
            load(0, 0)
            load(1, 1)
            with sp.Fori(1, BLOCKS // 2) as i:
                with sp.If(i < pairs):
                    for u in range(2):
                        load(i * 2 + u, u)

        @block.gpsimd
        def _(pool):
            def fetch_rows(b, u):
                if not isinstance(b, int) or b >= 2:
                    wait_pair(pool, fetched, b - 2, u, 16)
                    pool.wait_ge(x_turned, b * 2 - 2)
                pool.tensor_copy(fetch[u][:, :], slots[:, 1, bass.ds(b, 1)]).then_inc(fetch_set, 1)
                pool.wait_ge(fetch_set, b + 1)
                pool.sem_inc(may_move)
                pool.indirect_dma_start(x[u][:, :], None, scratch["h2"], bass.IndirectOffsetOnAxis(ap=fetch[u][:, :], axis=0)).then_inc(fetched[u], 16)

            def out_low_part(b, u):
                wait_pair(pool, w_loaded, b, u, LOADS)
                r = buffer_of(pool, b)
                pool.wait_ge(out_high, b + 1)
                pool.tensor_tensor(out_lo[u][:, :, :], raw_out[:, bass.ds(r, 1), :, :].rearrange("p a k n -> p (a k) n"),
                                   out_hi[u][:, :, :], ALU.subtract).then_inc(out_low, 1)

            def store_rows(b, u):
                if not isinstance(b, int) or b >= 2:
                    wait_pair(pool, stored, b - 2, u, 16)
                pool.tensor_copy(put[u][:, :], slots[:, 0, bass.ds(b, 1)]).then_inc(put_set, 1)
                pool.wait_ge(put_set, b + 1)
                pool.wait_ge(y_copied, b * 2 + 2)
                pool.sem_inc(may_move)
                pool.indirect_dma_start(scratch["y_slots"], bass.IndirectOffsetOnAxis(ap=put[u][:, :], axis=0), y[u][:, :], None,
                                        bounds_check=S * TOP - 1, oob_is_err=False).then_inc(stored[u], 16)

            pairs = pairs_of(pool)
            fetch_rows(0, 0)
            fetch_rows(1, 1)
            fetch_rows(2, 0)
            out_low_part(0, 0)
            fetch_rows(3, 1)
            out_low_part(1, 1)
            fetch_rows(4, 0)
            store_rows(0, 0)
            out_low_part(2, 0)
            with pool.Fori(1, BLOCKS // 2) as i:
                with pool.If(i < pairs - 1):
                    for u in (0, 1):
                        b = i * 2 + u
                        fetch_rows(b + 3, 1 - u)
                        store_rows(b - 1, 1 - u)
                        out_low_part(b + 1, 1 - u)
                with pool.If(i == pairs - 1):
                    b = i * 2
                    store_rows(b - 1, 1)
                    out_low_part(b + 1, 1)
                    store_rows(b, 0)
                    store_rows(b + 1, 1)
                    for u in range(2):
                        pool.wait_ge(stored[u], i * 16 + 16)
                    pool.wait_ge(fetched[0], i * 16 + 32)

        @block.tensor
        def _(pe):
            def turn_rows(b, u):
                wait_pair(pe, fetched, b, u, 16)
                for j in range(2):
                    if not (isinstance(b, int) and b == 0):
                        pe.wait_ge(x_low, b * 2 + (j - 1))
                    for q in range(4):
                        k = 4 * j + q
                        m = nc.tensor.transpose(x_ps[j][:, q, :], x[u][:, k * P:(k + 1) * P], ident[:, :])
                    m.then_inc(x_turned, 1)

            def into(b, u):
                pe.wait_ge(x_low, b * 2 + 2)
                if not isinstance(b, int) or b >= 2:
                    pe.wait_ge(inner_set, b - 1)
                n = 0
                for k in range(KD):
                    pe.wait_ge(in_low, b * KD + (k + 1))
                    for xs, ws in ((xT_hi, in_hi), (xT_hi, in_lo), (xT_lo, in_hi)):
                        m = nc.tensor.matmul(h_ps[u][:, :], xs[u][:, k, :], ws[u][:, k, :], start=(n == 0), stop=(n == 3 * KD - 1))
                        n += 1
                m.then_inc(inner_done, 1)

            def turn_inner(b, u):
                pe.wait_ge(inner_set, b + 1)
                if not (isinstance(b, int) and b == 0):
                    pe.wait_ge(i_low, b)
                for q in range(FK):
                    m = nc.tensor.transpose(i_ps[:, q, :], inner[:, q * P:(q + 1) * P], ident[:, :])
                m.then_inc(i_turned, 1)

            def out_of(b, u):
                pe.wait_ge(i_low, b + 1)
                pe.wait_ge(out_low, b + 1)
                for j in range(2):
                    if not (isinstance(b, int) and b == 0):
                        pe.wait_ge(y_copied, b * 2 + (j - 1))
                    n = 0
                    for k in range(FK):
                        for s, w in ((iT_hi, out_hi), (iT_hi, out_lo), (iT_lo, out_hi)):
                            m = nc.tensor.matmul(y_ps[j][:, :], s[u][:, k, :], w[u][:, k, j * CH:(j + 1) * CH], start=(n == 0), stop=(n == 3 * FK - 1))
                            n += 1
                    m.then_inc(y_product, 1)

            pairs = pairs_of(pe)
            turn_rows(0, 0)
            into(0, 0)
            turn_rows(1, 1)
            turn_inner(0, 0)
            into(1, 1)
            turn_rows(2, 0)
            out_of(0, 0)
            turn_inner(1, 1)
            with pe.Fori(1, BLOCKS // 2) as i:
                with pe.If(i < pairs - 1):
                    for u in range(2):
                        b = i * 2 + u
                        into(b, u)
                        turn_rows(b + 1, 1 - u)
                        out_of(b - 1, 1 - u)
                        turn_inner(b, u)
                with pe.If(i == pairs - 1):
                    for u in range(2):
                        b = i * 2 + u
                        into(b, u)
                        if u == 0:
                            turn_rows(b + 1, 1)
                        out_of(b - 1, 1 - u)
                        turn_inner(b, u)
                    out_of(i * 2 + 1, 1)

        @block.scalar
        def _(act):
            def in_high_part(b, u):
                wait_pair(act, w_loaded, b, u, LOADS)
                r = buffer_of(act, b)
                if not isinstance(b, int) or b >= 2:
                    act.wait_ge(inner_done, b - 1)
                for k in range(KD):
                    nc.scalar.copy(in_hi[u][:, k, :], raw_in[:, bass.ds(r, 1), k, :].rearrange("p a n -> p (a n)")).then_inc(in_high, 1)
                return r

            def out_high_part(b, u, r):
                if not isinstance(b, int) or b >= 2:
                    act.wait_ge(y_product, b * 2 - 2)
                nc.scalar.copy(out_hi[u][:, :, :], raw_out[:, bass.ds(r, 1), :, :].rearrange("p a k n -> p (a k) n")).then_inc(out_high, 1)

            def x_high_part(b, u):
                for j in range(2):
                    act.wait_ge(x_turned, b * 2 + (j + 1))
                    if not isinstance(b, int) or b >= 2:
                        act.wait_ge(inner_done, b - 1)
                    nc.scalar.copy(xT_hi[u][:, 4 * j:4 * j + 4, :], x_ps[j][:, :, :]).then_inc(x_high, 1)

            def silu(b, u):
                act.wait_ge(inner_done, b + 1)
                if not (isinstance(b, int) and b == 0):
                    act.wait_ge(inner_set, b)
                nc.scalar.activation(act_part[:, :], h_ps[u][:, 0:FE], ACT.Silu).then_inc(silu_done, 1)

            def i_high_part(b, u):
                act.wait_ge(i_turned, b + 1)
                if not isinstance(b, int) or b >= 2:
                    act.wait_ge(y_product, b * 2 - 2)
                nc.scalar.copy(iT_hi[u][:, :, :], i_ps[:, 0:FK, :]).then_inc(i_high, 1)

            def step(b, u, last):
                if not last:
                    r = in_high_part(b + 1, 1 - u)
                silu(b, u)
                if not last:
                    x_high_part(b + 1, 1 - u)
                i_high_part(b, u)
                if not last:
                    out_high_part(b + 1, 1 - u, r)

            pairs = pairs_of(act)
            r = in_high_part(0, 0)
            x_high_part(0, 0)
            out_high_part(0, 0, r)
            step(0, 0, False)
            step(1, 1, False)
            with act.Fori(1, BLOCKS // 2) as i:
                with act.If(i < pairs - 1):
                    for u in range(2):
                        step(i * 2 + u, u, False)
                with act.If(i == pairs - 1):
                    step(i * 2, 0, False)
                    step(i * 2 + 1, 1, True)

        @block.vector
        def _(dve):
            def in_low_part(b, u):
                r = buffer_of(dve, b)
                for k in range(KD):
                    dve.wait_ge(in_high, b * KD + (k + 1))
                    dve.tensor_tensor(in_lo[u][:, k, :], raw_in[:, bass.ds(r, 1), k, :].rearrange("p a n -> p (a n)"), in_hi[u][:, k, :],
                                      ALU.subtract).then_inc(in_low, 1)

            def x_low_part(b, u):
                for j in range(2):
                    dve.wait_ge(x_high, b * 2 + (j + 1))
                    dve.tensor_tensor(xT_lo[u][:, 4 * j:4 * j + 4, :], x_ps[j][:, :, :], xT_hi[u][:, 4 * j:4 * j + 4, :], ALU.subtract).then_inc(x_low, 1)

            def set_inner(b, u):
                dve.wait_ge(silu_done, b + 1)
                if not (isinstance(b, int) and b == 0):
                    dve.wait_ge(i_turned, b)
                dve.tensor_tensor(inner[:, :], act_part[:, :], h_ps[u][:, FE:2 * FE], ALU.mult).then_inc(inner_set, 1)

            def i_low_part(b, u):
                dve.wait_ge(i_high, b + 1)
                dve.tensor_tensor(iT_lo[u][:, :, :], i_ps[:, 0:FK, :], iT_hi[u][:, :, :], ALU.subtract).then_inc(i_low, 1)

            def copy_y(b, u):
                for j in range(2):
                    dve.wait_ge(y_product, b * 2 + (j + 1))
                    if j == 0 and (not isinstance(b, int) or b >= 2):
                        wait_pair(dve, stored, b - 2, u, 16)
                    dve.tensor_copy(y[u][:, j * CH:(j + 1) * CH], y_ps[j][:, :]).then_inc(y_copied, 1)

            def step(b, u, last, first=False):
                if not last:
                    in_low_part(b + 1, 1 - u)
                set_inner(b, u)
                if not last:
                    x_low_part(b + 1, 1 - u)
                if not first:
                    copy_y(b - 1, 1 - u)
                i_low_part(b, u)

            pairs = pairs_of(dve)
            in_low_part(0, 0)
            x_low_part(0, 0)
            step(0, 0, False, True)
            step(1, 1, False)
            with dve.Fori(1, BLOCKS // 2) as i:
                with dve.If(i < pairs - 1):
                    for u in range(2):
                        step(i * 2 + u, u, False)
                with dve.If(i == pairs - 1):
                    step(i * 2, 0, False)
                    step(i * 2 + 1, 1, True)
                    copy_y(i * 2 + 1, 1)


def combine(nc, gates, out, scratch):
    RING = 4
    with ExitStack() as ctx:
        def sb(name, shape, dt=F32):
            return ctx.enter_context(nc.sbuf_tensor("co_" + name, shape, dt))

        def sem(name):
            return ctx.enter_context(nc.semaphore("co_" + name))

        x2 = [sb(f"x2{b}", [P, D]) for b in range(RING)]
        y = [sb(f"y{b}", [P, TOP, D]) for b in range(RING)]
        loaded = [sem(f"loaded{b}") for b in range(RING)]
        stored = [sem(f"stored{b}") for b in range(RING)]
        first, second = sem("first"), sem("second")
        block = ctx.enter_context(nc.Block())
        y_view = scratch["y_slots"].rearrange("(c s) d -> s c d", c=TOP)

        @block.sync
        def _(sp):
            for t in range(NT):
                b, rows = t % RING, slice(t * P, (t + 1) * P)
                if t >= RING:
                    sp.wait_ge(stored[b], 16 * (t // RING))
                sp.dma_start(x2[b][:, :], scratch["x2"][rows, :]).then_inc(loaded[b], 16)
                sp.dma_start(y[b][:, :, :], y_view[rows, :, :]).then_inc(loaded[b], 16)

        @block.vector
        def _(dve):
            for t in range(NT):
                b = t % RING
                dve.wait_ge(loaded[b], 32 * (t // RING + 1))
                dve.scalar_tensor_tensor(out=x2[b][:, :], in0=y[b][:, 0, :], scalar=gates[:, t, 0:1], in1=x2[b][:, :],
                                         op0=ALU.mult, op1=ALU.add).then_inc(first, 1)
                dve.wait_ge(first, t + 1)
                dve.scalar_tensor_tensor(out=x2[b][:, :], in0=y[b][:, 1, :], scalar=gates[:, t, 1:2], in1=x2[b][:, :],
                                         op0=ALU.mult, op1=ALU.add).then_inc(second, 1)

        @block.scalar
        def _(act):
            for t in range(NT):
                b = t % RING
                act.wait_ge(second, t + 1)
                act.dma_start(out[t * P:(t + 1) * P, :], x2[b][:, :]).then_inc(stored[b], 16)
            for b in range(RING):
                act.wait_ge(stored[b], 16 * NT // RING)


def hybrid_layer(nc, x, g_mix, w_in, b_fgate, b_gate, g_q, g_k, w_pool, s_pool, g_sgu, w_sgu, b_sgu, w_branch, w_out,
                 g_ffn, w_rg, b_rg, w_re, b_re, w1, w3, w2, out):
    x, out = x.rearrange("o s d -> (o s) d"), out.rearrange("o s d -> (o s) d")

    def dram(name, shape):
        return nc.dram_tensor(name, shape, F32, kind="Internal").ap()

    scratch = {
        "qk_hi": dram("qk_hi", (QK_TILES, P, S)),
        "qk_lo": dram("qk_lo", (QK_TILES, P, S)),
        "v": dram("v_parts", (NCH, P, TPC, HEADS, 2, HD)),
        "cum": dram("cum_parts", (HEADS, 2, S)),
        "y": dram("branch_out", (N_BR, BR_K, P, S)),
        "gates": dram("branch_gates", (GATE_TILES, P, S)),
        "merged": dram("merged", (KD, P, S)),
        "x2": dram("x2", (S, D)),
        "h2": dram("h2", (S, D)),
        "y_slots": dram("y_slots", (S * TOP, D)),
    }
    half = QK_TILES // 2
    flat = [scratch[n].rearrange("t p s -> (t p) s") for n in ("qk_hi", "qk_lo")]
    scratch["q_rows"] = [f[0:half * P] for f in flat]
    scratch["k_rows"] = [f[half * P:QK_TILES * P] for f in flat]

    with nc.sbuf_tensor("ident", [P, P], F32) as ident, nc.sbuf_tensor("ones_col", [P, 1], F32) as ones_col:
        with nc.sbuf_tensor("head_ones", [P, P], F32) as head_ones, nc.sbuf_tensor("hT_hi", [P, KD, S], F32R) as hT_hi, \
                nc.sbuf_tensor("hT_lo", [P, KD, S], F32R) as hT_lo:
            spent = build_constants(nc, ident, head_ones, ones_col)
            spent += norm_and_transpose(nc, x, g_mix, ident, hT_hi, hT_lo)
            spent += project(nc, hT_hi, hT_lo, ident, head_ones, ones_col, w_in, b_fgate, b_gate, g_q, g_k, w_pool, s_pool, g_sgu, w_sgu,
                    b_sgu, scratch)
        attend(nc, ident, scratch, spent)
        merge(nc, ones_col, w_branch, scratch)
        with nc.sbuf_tensor("gates", [P, NT, TOP], F32) as gates, nc.sbuf_tensor("slots", [P, 2, TABLE], I32) as slots, \
                nc.sbuf_tensor("plan", [P, 4, TABLE], I32) as plan:
            with nc.sbuf_tensor("logits", [P, NT, N_LOGIT], F32) as logits:
                project_out(nc, ones_col, x, w_out, g_ffn, w_rg, b_rg, w_re, b_re, ident, logits, scratch)
                route(nc, logits, gates, slots, plan)
            experts(nc, w1, w3, w2, ident, slots, plan, scratch)
            combine(nc, gates, out, scratch)


_INS = ["x", "g_mix", "w_in", "b_fgate", "b_gate", "g_q", "g_k", "w_pool", "s_pool", "g_sgu", "w_sgu", "b_sgu",
        "w_branch", "w_out", "g_ffn", "w_rg", "b_rg", "w_re", "b_re", "w1", "w3", "w2"]
_OUTS = [((1, S, D), "float32")]


def kernel(**inputs):
    import numpy as _np
    import concourse.bacc as _bacc
    from concourse import mybir as _mybir
    from concourse.bass_utils import run_bass_kernel_spmd as _run

    nc = _bacc.Bacc("TRN2", target_bir_lowering=False, num_devices=1)
    arrays, args = {}, []
    for name in _INS:
        a = _np.ascontiguousarray(inputs[name])
        arrays[f"in_{name}_dram"] = a
        args.append(nc.dram_tensor(f"in_{name}_dram", a.shape, _mybir.dt.from_np(a.dtype), kind="ExternalInput").ap())
    for i, (shape, dtype) in enumerate(_OUTS):
        dt = _mybir.dt.from_np(_np.dtype(dtype))
        args.append(nc.dram_tensor(f"out_{i}_dram", shape, dt, kind="ExternalOutput").ap())
    hybrid_layer(nc, *args)
    r = _run(nc, [arrays], core_ids=[0])
    got = tuple(r.results[0][f"out_{i}_dram"] for i in range(len(_OUTS)))
    return got[0]
```

```python
from contextlib import ExitStack

import concourse.bass as bass
from concourse import mybir

F32 = mybir.dt.float32
F32R = mybir.dt.float32r
I32 = mybir.dt.int32
ALU = mybir.AluOpType
ACT = mybir.ActivationFunctionType
AX = mybir.AxisListType

P = 128
S, D = 2048, 1024
NT = S // P
KD = D // P
CH = 512
NCH = S // CH
TPC = CH // P
EPS = 1e-6
HEADS, HD = 8, 64
GROUPS = 4
WINDOWS = (2, 4, 8, 16)
HALO = 16
OFF_F, OFF_P, OFF_U, OFF_SV, OFF_G = 1536, 1544, 2056, 2568, 3080
QK_TILES, V_TILES, GATE_TILES = 8, 4, 24
T_F, T_QK = 0, 1
T_V = T_QK + QK_TILES
T_P = T_V + V_TILES
T_SU = T_P + GROUPS
T_G = T_SU + 2 * GROUPS
T_END = T_G + GATE_TILES


def w_in_offset(t):
    if t == T_F:
        return OFF_F
    if t < T_P:
        return P * (t - T_QK)
    if t < T_SU:
        return OFF_P + P * (t - T_P)
    if t < T_G:
        g, is_u = divmod(t - T_SU, 2)
        return (OFF_U if is_u else OFF_SV) + P * g
    return OFF_G + P * (t - T_G)


def build_constants(nc, ident, head_ones, ones_col):
    with nc.semaphore("const_zeroed") as zeroed, nc.semaphore("const_made") as made, \
            nc.semaphore("const_cleared") as cleared, nc.Block() as block:
        @block.gpsimd
        def _(pool):
            pool.memset(ident[:, :], 0.0).then_inc(zeroed, 1)
            pool.memset(ones_col[:, :], 1.0).then_inc(made, 1)
            pool.wait_ge(zeroed, 1)
            pool.affine_select(out=ident[:, :], in_=ident[:, :], compare_op=ALU.not_equal, fill=1.0, base=0,
                               pattern=[[-1, P]], channel_multiplier=1).then_inc(made, 1)
            pool.wait_ge(made, 2)

        @block.vector
        def _(dve):
            dve.memset(head_ones[:, :], 0.0).then_inc(cleared, 1)
            dve.wait_ge(cleared, 1)
            dve.memset(head_ones[0:HD, 0:HD], 1.0).then_inc(cleared, 1)
            dve.memset(head_ones[HD:P, HD:P], 1.0).then_inc(cleared, 1)
            dve.wait_ge(cleared, 3)
    return [zeroed, made, cleared]


def projection_weights(nc, ctx):
    def sb(name, dt=F32):
        return [ctx.enter_context(nc.sbuf_tensor(f"p1_{name}{i}", [P, KD, P], dt)) for i in range(2)]

    def sem(name):
        return ctx.enter_context(nc.semaphore("p1_" + name))

    return {"raw": sb("w_raw"), "hi": sb("w_hi", F32R), "lo": sb("w_lo", F32R), "loaded": [sem(f"w_loaded{i}") for i in range(2)],
            "split_hi": sem("split_hi"), "split_done": sem("split_done")}


def load_feature_tile(sp, w_in, weights, offset, b):
    view = w_in.rearrange("o (k p) n -> p (o k) n", p=P)
    sp.dma_start(weights["raw"][b][:, :, :], view[:, :, bass.ds(offset, P)]).then_inc(weights["loaded"][b], 16)


def split_feature_tile(pool, weights, ones_col, b, tr):
    raw, hi, lo = (weights[n][b] for n in ("raw", "hi", "lo"))
    pool.tensor_tensor(hi[:, :, :], raw[:, :, :], ones_col[:, 0:1, None].broadcast_to([P, KD, P]), ALU.mult).then_inc(weights["split_hi"], 1)
    pool.wait_ge(weights["split_hi"], tr + 1)
    pool.tensor_tensor(lo[:, :, :], raw[:, :, :], hi[:, :, :], ALU.subtract).then_inc(weights["split_done"], 1)


def norm_and_transpose(nc, x, gain, ident, ones_col, w_in, weights, hT_hi, hT_lo):
    used = []
    with ExitStack() as ctx:
        def sb(name, shape, dt=F32):
            return ctx.enter_context(nc.sbuf_tensor(name, shape, dt))

        def sem(name):
            used.append(ctx.enter_context(nc.semaphore(name)))
            return used[-1]

        XB = 4
        xt = sb("p0_x", [P, XB, D])
        hh = sb("p0_h", [P, 2, D])
        squares = sb("p0_squares", [P, D])
        gain_rows = sb("p0_gain", [P, D])
        sums = sb("p0_sums", [P, NT])
        rms = sb("p0_rms", [P, NT])
        rstd = sb("p0_rstd", [P, NT])
        ps = ctx.enter_context(nc.psum_tensor("p0_turned", [P, 4, 4, P], F32))
        x_loaded = [sem(f"p0_x_loaded{i}") for i in range(XB)]
        gain_loaded = sem("p0_gain_loaded")
        eps_col = sb("p0_eps", [P, 1])
        eps_set = sem("p0_eps_set")
        summed, rooted, inverted = sem("p0_summed"), sem("p0_rooted"), sem("p0_inverted")
        scaled, turned, hi_done, lo_done = sem("p0_scaled"), sem("p0_turned_s"), sem("p0_hi"), sem("p0_lo")
        block = ctx.enter_context(nc.Block())

        @block.sync
        def _(sp):
            sp.dma_start(gain_rows[:, :], gain.rearrange("o d -> (o d)").partition_broadcast(P)).then_inc(gain_loaded, 16)
            for i in range(NT):
                if i >= XB:
                    sp.wait_ge(scaled, i - XB + 1)
                sp.dma_start(xt[:, i % XB, :], x[i * P:(i + 1) * P, :]).then_inc(x_loaded[i % XB], 16)
            for t in range(2):
                load_feature_tile(sp, w_in, weights, w_in_offset(t), t)

        @block.scalar
        def _(act):
            def square(i):
                act.wait_ge(x_loaded[i % XB], 16 * (i // XB + 1))
                if i >= 1:
                    act.wait_ge(summed, i)
                nc.scalar.activation(squares[:, :], xt[:, i % XB, :], ACT.Square,
                                     accum_out=sums[:, i:i + 1]).then_inc(summed, 1)
                act.wait_ge(summed, i + 1)
                nc.scalar.activation(rms[:, i:i + 1], sums[:, i:i + 1], ACT.Sqrt, bias=eps_col[:, 0:1],
                                     scale=1.0 / D).then_inc(rooted, 1)

            def high_parts(i):
                for j in range(2):
                    act.wait_ge(turned, 2 * i + j + 1)
                    nc.scalar.copy(hT_hi[:, 4 * j:4 * j + 4, i * P:(i + 1) * P],
                                   ps[:, (2 * i + j) % 4, :, :]).then_inc(hi_done, 1)

            act.wait_ge(eps_set, 1)
            for i in range(NT + 1):
                if i < NT:
                    square(i)
                if i >= 1:
                    high_parts(i - 1)

        @block.gpsimd
        def _(pool):
            pool.memset(eps_col[:, :], EPS).then_inc(eps_set, 1)
            for t in range(2):
                pool.wait_ge(weights["loaded"][t], 16)
                split_feature_tile(pool, weights, ones_col, t, t)
            pool.wait_ge(weights["split_done"], 2)

        @block.vector
        def _(dve):
            dve.wait_ge(gain_loaded, 16)
            def scale(i):
                dve.wait_ge(rooted, i + 1)
                dve.reciprocal(rstd[:, i:i + 1], rms[:, i:i + 1]).then_inc(inverted, 1)
                dve.wait_ge(inverted, i + 1)
                if i >= 2:
                    dve.wait_ge(turned, 2 * (i - 1))
                dve.scalar_tensor_tensor(out=hh[:, i % 2, :], in0=xt[:, i % XB, :], scalar=rstd[:, i:i + 1],
                                         in1=gain_rows[:, :], op0=ALU.mult, op1=ALU.mult).then_inc(scaled, 1)

            def low_parts(i):
                for j in range(2):
                    dve.wait_ge(hi_done, 2 * i + j + 1)
                    cols = slice(i * P, (i + 1) * P)
                    dve.tensor_tensor(hT_lo[:, 4 * j:4 * j + 4, cols], ps[:, (2 * i + j) % 4, :, :],
                                      hT_hi[:, 4 * j:4 * j + 4, cols], ALU.subtract).then_inc(lo_done, 1)

            for i in range(NT + 1):
                if i < NT:
                    scale(i)
                if i >= 1:
                    low_parts(i - 1)

        @block.tensor
        def _(pe):
            for i in range(NT):
                pe.wait_ge(scaled, i + 1)
                for j in range(2):
                    if i >= 2:
                        pe.wait_ge(lo_done, 2 * (i - 2) + j + 1)
                    for q in range(4):
                        m = nc.tensor.transpose(ps[:, (2 * i + j) % 4, q, :],
                                                hh[:, i % 2, (4 * j + q) * P:(4 * j + q + 1) * P], ident[:, :])
                    m.then_inc(turned, 1)
    return used


def project(nc, hT_hi, hT_lo, ident, head_ones, ones_col, weights, w_in, b_fgate, b_gate, g_q, g_k, w_pool, s_pool, g_sgu, w_sgu,
            b_sgu, scratch):
    used = []
    with ExitStack() as ctx:
        def sb(name, shape, dt=F32):
            return ctx.enter_context(nc.sbuf_tensor("p1_" + name, shape, dt))

        def sem(name):
            used.append(ctx.enter_context(nc.semaphore("p1_" + name)))
            return used[-1]

        w_hi, w_lo, w_loaded, split_done = (weights[n] for n in ("hi", "lo", "loaded", "split_done"))
        work = [sb(f"work{i}", [P, HALO + CH]) for i in range(6)]
        out = [sb(f"out{i}", [P, 2, CH], F32R) for i in range(2)]
        out_a, out_b = [o[:, 0, :] for o in out], [o[:, 1, :] for o in out]
        out_v = [o[:, :, :].rearrange("p a b -> p (a b)").rearrange("p (n h l d) -> p n h l d", n=TPC, h=2, l=2) for o in out]
        long_a = sb("long_a", [P, S])
        gates = [sb(f"gate{i}", [P, CH]) for i in range(3)]
        cum_chunk = [work[3 + i][0:HEADS, 0:CH] for i in range(2)]
        cum_parts = [sb(f"cum_parts{i}", [HEADS, 2, CH], F32R) for i in range(2)]
        qk_gain = sb("qk_gain", [P, 2])
        f_bias = sb("f_bias", [HEADS, 1])
        gate_bias = sb("gate_bias", [P, GATE_TILES])
        pool_w = sb("pool_w", [P, GROUPS, P])
        pool_scale = sb("pool_scale", [P, GROUPS])
        pool_count = sb("pool_count", [P, GROUPS, HALO])
        pool_inverse = sb("pool_inverse", [P, GROUPS, HALO])
        sgu_gain = sb("sgu_gain", [P, GROUPS])
        sgu_w = sb("sgu_w", [P, GROUPS, P])
        sgu_wT = sb("sgu_wT", [P, GROUPS, P])
        sgu_bias = sb("sgu_bias", [P, GROUPS, P])
        square_sums = sb("square_sums", [P, NT])
        square_roots = sb("square_roots", [P, NT])
        inverse_roots = sb("inverse_roots", [P, NT])
        ones8 = work[5][0:HEADS, 0:CH]
        eps = sb("eps", [P, 1])
        qk_gain8 = sb("qk_gain8", [P, QK_TILES])
        gate_bias_now = [sb(f"gate_bias_now{i}", [P, 1]) for i in range(2)]
        sgu_now = sb("sgu_now", [P, P])
        main = [ctx.enter_context(nc.psum_tensor(f"p1_main{i}", [P, CH], F32)) for i in range(NCH)]
        aux = [ctx.enter_context(nc.psum_tensor(f"p1_aux{i}", [P, CH], F32)) for i in range(4)]

        main_done = sem("main_done")
        bank_free = [sem(f"bank_free{i}") for i in range(NCH)]
        params_loaded, consts, f_chain, cum_stored = sem("params_loaded"), sem("consts"), sem("f_chain"), [sem(f"cum_stored{i}") for i in range(2)]
        turned_w, sgu_w_ready = sem("turned_w"), sem("sgu_w_ready")
        sq_done, ssq_done, root_done, inv_done = sem("sq_done"), sem("ssq_done"), sem("root_done"), sem("inv_done")
        hi_done, lo_done = sem("hi_done"), sem("lo_done")
        hi_stored = [sem(f"hi_stored{i}") for i in range(2)]
        lo_stored = [sem(f"lo_stored{i}") for i in range(2)]
        v_turned, v_hi, v_lo = sem("v_turned"), sem("v_hi"), sem("v_lo")
        v_stored = [sem(f"v_stored{i}") for i in range(2)]
        halo_done, sum_step, pooled_done, pool_mm = sem("halo_done"), sem("sum_step"), sem("pooled_done"), sem("pool_mm")
        yb_done, yb_stored = sem("yb_done"), [sem(f"yb_stored{i}") for i in range(2)]
        sv_turned, sv_copied, sv_squared, sv_summed = sem("sv_turned"), sem("sv_copied"), sem("sv_squared"), sem("sv_summed")
        sv_rooted, sv_inverted, sv_scaled, mixed = sem("sv_rooted"), sem("sv_inverted"), sem("sv_scaled"), sem("mixed")
        gained, biased, yc_done = sem("gained"), sem("biased"), sem("yc_done")
        yc_stored = [sem(f"yc_stored{i}") for i in range(2)]
        gains_ready, sgu_now_set, gate_bias_set = sem("gains_ready"), sem("sgu_now_set"), sem("gate_bias_set")
        cum_high, cum_split = sem("cum_high"), sem("cum_split")
        gate_stored = [sem(f"gate_stored{i}") for i in range(4)]
        gates.append(work[5][:, 0:CH])
        gate_buf = lambda j: gates[j] if j == 3 else gates[j][:, :]

        block = ctx.enter_context(nc.Block())

        @block.sync
        def _(sp):
            def load(offset, t, tr):
                if not (isinstance(tr, int) and tr < 2):
                    sp.wait_ge(split_done, tr - 1)
                load_feature_tile(sp, w_in, weights, offset, t % 2)

            with nc.allow_non_contiguous_dma("small parameters"):
                for half in range(2):
                    rows = slice(half * HD, half * HD + HD)
                    sp.dma_start(qk_gain[rows, 0:1], g_q.rearrange("o d -> d o")).then_inc(params_loaded, 16)
                    sp.dma_start(qk_gain[rows, 1:2], g_k.rearrange("o d -> d o")).then_inc(params_loaded, 16)
                sp.dma_start(f_bias[:, :], b_fgate.rearrange("o h -> h o")).then_inc(params_loaded, 16)
                sp.dma_start(gate_bias[:, :], b_gate.rearrange("o b (k p) -> p (o b k)", p=P)).then_inc(params_loaded, 16)
                sp.dma_start(pool_w[:, :, :], w_pool.rearrange("o g c d -> c (o g) d")).then_inc(params_loaded, 16)
                sp.dma_start(pool_scale[:, :], s_pool.rearrange("o (g p) -> p (o g)", p=P)).then_inc(params_loaded, 16)
                sp.dma_start(sgu_gain[:, :], g_sgu.rearrange("o (g p) -> p (o g)", p=P)).then_inc(params_loaded, 16)
                sp.dma_start(sgu_w[:, :, :], w_sgu.rearrange("o g t s -> t (o g) s")).then_inc(params_loaded, 16)
                sp.dma_start(sgu_bias[:, :, :], b_sgu.rearrange("o g t -> (o g) t").partition_broadcast(P)).then_inc(params_loaded, 16)
            load(w_in_offset(2), 2, 2)
            for c in range(NCH):
                sp.wait_ge(cum_split, c + 1)
                sp.dma_start(scratch["cum"][:, :, c * CH:(c + 1) * CH], cum_parts[c % 2][:, :, :].bitcast(F32)).then_inc(cum_stored[c % 2], 16)

            def store_qk(t, k, c):
                cols = slice(c * CH, (c + 1) * CH)
                sp.wait_ge(hi_done, k + 1)
                sp.dma_start(scratch["qk_hi"][t - T_QK, :, cols], out_a[c % 2].bitcast(F32)).then_inc(hi_stored[c % 2], 16)
                sp.wait_ge(lo_done, k + 1)
                sp.dma_start(scratch["qk_lo"][t - T_QK, :, cols], out_b[c % 2].bitcast(F32)).then_inc(lo_stored[c % 2], 16)

            with sp.Fori(0, QK_TILES // 2) as i:
                for u in range(2):
                    t = i * 2 + (T_QK + u)
                    load(i * (2 * P) + P * (u + 1 + 1), T_QK + u + 2, t + 2)
                    for c in range(NCH):
                        store_qk(t, i * (2 * NCH) + (u * NCH + c), c)
            for t in range(T_V, T_P):
                load(w_in_offset(t + 2), t + 2, t + 2)
                for c in range(NCH):
                    k = (t - T_V) * NCH + c
                    dst = scratch["v"][c, :, :, 2 * (t - T_V):2 * (t - T_V) + 2]
                    sp.wait_ge(v_lo, k + 1)
                    sp.dma_start(dst, out_v[c % 2].bitcast(F32)).then_inc(v_stored[c % 2], 16)
            for t in range(T_P, T_SU):
                load(w_in_offset(t + 2), t + 2, t + 2)
                for c in range(NCH):
                    sp.wait_ge(yb_done, (t - T_P) * NCH + c + 1)
                    sp.dma_start(scratch["y"][1, t - T_P, :, c * CH:(c + 1) * CH], out_b[c % 2].bitcast(F32)).then_inc(yb_stored[c % 2], 16)

            def pair(g, load_u_offset, load_sv_offset, t):
                load(load_sv_offset, T_SU, t + 2)
                load(load_u_offset, T_SU + 1, t + 3)
                for c in range(NCH):
                    sp.wait_ge(yc_done, g * NCH + (c + 1))
                    sp.dma_start(scratch["y"][2, g, :, c * CH:(c + 1) * CH], out_b[c % 2].bitcast(F32)).then_inc(yc_stored[c % 2], 16)

            with sp.Fori(0, GROUPS - 1) as g:
                pair(g, g * P + (OFF_U + P), g * P + (OFF_SV + P), g * 2 + T_SU)
            pair(GROUPS - 1, w_in_offset(T_G + 1), w_in_offset(T_G), T_G - 2)

            def gate_pair(i, last):
                for u in range(2):
                    t = i * 2 + (T_G + u)
                    if not last:
                        load(i * (2 * P) + (OFF_G + P * (u + 2)), T_G + u + 2, t + 2)
                    for c in range(NCH):
                        sp.wait_ge(bank_free[c], t + 1)
                        sp.dma_start(scratch["gates"][t - T_G, :, c * CH:(c + 1) * CH], gate_buf(c)).then_inc(gate_stored[c], 16)

            with sp.Fori(0, GATE_TILES // 2 - 1) as i:
                gate_pair(i, False)
            gate_pair(GATE_TILES // 2 - 1, True)
            for j in range(2):
                sp.wait_ge(cum_stored[j], 16 * NCH // 2)
                sp.wait_ge(hi_stored[j], 16 * QK_TILES * NCH // 2)
                sp.wait_ge(lo_stored[j], 16 * QK_TILES * NCH // 2)
                sp.wait_ge(v_stored[j], 16 * V_TILES * NCH // 2)
                sp.wait_ge(yb_stored[j], 16 * GROUPS * NCH // 2)
                sp.wait_ge(yc_stored[j], 16 * GROUPS * NCH // 2)
            for j in range(4):
                sp.wait_ge(gate_stored[j], 16 * GATE_TILES)

        @block.gpsimd
        def _(pool):
            pool.memset(eps[:, :], EPS).then_inc(consts, 1)
            pool.memset(ones8, 1.0).then_inc(consts, 1)
            pool.iota(pool_count[:, :, :], pattern=[[0, GROUPS], [1, HALO]], base=1, channel_multiplier=0,
                      allow_small_or_imprecise_dtypes=True).then_inc(consts, 1)
            pool.wait_ge(consts, 3)
            for g, w in enumerate(WINDOWS):
                pool.tensor_scalar(pool_count[:, g, :], pool_count[:, g, :], float(w), None, ALU.min).then_inc(consts, 1)
            pool.wait_ge(params_loaded, 16 * 11)
            for g in range(GROUPS):
                pool.affine_select(out=sgu_w[:, g, :], in_=sgu_w[:, g, :], compare_op=ALU.is_ge, fill=0.0, base=0,
                                   pattern=[[-1, P]], channel_multiplier=1).then_inc(consts, 1)

            def split(t, tr):
                b = t % 2
                if isinstance(tr, int):
                    pool.wait_ge(w_loaded[b], 16 * (tr // 2 + 1))
                else:
                    pool.wait_ge(w_loaded[b], tr * 8 + (8 if b else 16))
                if not (isinstance(tr, int) and tr < 2):
                    pool.wait_ge(main_done, tr * NCH - NCH)
                split_feature_tile(pool, weights, ones_col, b, tr)

            split(2, 2)
            with pool.Fori(0, (T_END - 3) // 2) as i:
                split(3, i * 2 + 3)
                split(4, i * 2 + 4)

        @block.tensor
        def _(pe):
            def chunk(t, tr, c):
                if c == 0:
                    pe.wait_ge(split_done, tr + 1)
                if not (isinstance(tr, int) and tr == 0):
                    pe.wait_ge(bank_free[c], tr)
                b = t % 2
                cols = slice(c * CH, (c + 1) * CH)
                n = 0
                for k in range(KD):
                    for w, h in ((w_hi, hT_hi), (w_hi, hT_lo), (w_lo, hT_hi)):
                        m = nc.tensor.matmul(main[c][:, :], w[b][:, k, :], h[:, k, cols], start=(n == 0), stop=(n == 3 * KD - 1))
                        n += 1
                m.then_inc(main_done, 1)

            for c in range(NCH):
                chunk(0, 0, c)
            pe.wait_ge(consts, 7 + GROUPS)
            for g in range(GROUPS):
                m = nc.tensor.transpose(aux[3][:, g * P:(g + 1) * P], sgu_w[:, g, :], ident[:, :])
            m.then_inc(turned_w, 1)

            def head_sums(c, k):
                pe.wait_ge(sq_done, k + 1)
                if not (isinstance(k, int) and k < 2):
                    pe.wait_ge(root_done, k - 1)
                nc.tensor.matmul(aux[c % 2][:, :], head_ones[:, :], work[c % 2][:, 0:CH], start=True, stop=True).then_inc(ssq_done, 1)

            def qk_pair(i):
                for s in range(2 * NCH + 1):
                    if s < 2 * NCH:
                        u, c = divmod(s, NCH)
                        chunk(T_QK + u, i * 2 + (T_QK + u), c)
                    if s >= 1:
                        head_sums(s - 1, i * (2 * NCH) + (s - 1))

            qk_pair(0)
            with pe.Fori(1, QK_TILES // 2) as i:
                qk_pair(i)

            def v_turn(k):
                c = k % NCH
                pe.wait_ge(bank_free[c], T_V + k // NCH + 1)
                if k < 2:
                    pe.wait_ge(root_done, QK_TILES * NCH - 1 + k)
                else:
                    pe.wait_ge(v_lo, k - 1)
                for n in range(TPC):
                    m = nc.tensor.transpose(aux[c % 2][:, n * P:(n + 1) * P], work[c % 2][:, n * P:(n + 1) * P], ident[:, :])
                m.then_inc(v_turned, 1)

            for k in range(V_TILES * NCH + 1):
                if k < V_TILES * NCH:
                    chunk(T_V + k // NCH, T_V + k // NCH, k % NCH)
                if k >= 1:
                    v_turn(k - 1)

            def pool_product(k):
                g, c = divmod(k, NCH)
                pe.wait_ge(pooled_done, k + 1)
                if k < 2:
                    pe.wait_ge(v_lo, V_TILES * NCH - 1 + k)
                else:
                    pe.wait_ge(yb_done, k - 1)
                nc.tensor.matmul(aux[c % 2][:, :], pool_w[:, g, :], work[4 + c % 2][:, 0:CH], start=True, stop=True).then_inc(pool_mm, 1)

            for k in range(GROUPS * NCH + 1):
                if k < GROUPS * NCH:
                    chunk(T_P + k // NCH, T_P + k // NCH, k % NCH)
                if k >= 1:
                    pool_product(k - 1)

            def su_pair(g):
                t = g * 2 + T_SU
                for s in range(NCH + 1):
                    if s < NCH:
                        chunk(T_SU, t, s)
                    else:
                        chunk(T_SU + 1, t + 1, 0)
                    if s >= 1:
                        c = s - 1
                        pe.wait_ge(bank_free[c], t + 1)
                        if c >= 2:
                            pe.wait_ge(sv_copied, g * NCH + (c - 1))
                        elif not isinstance(g, int):
                            pe.wait_ge(sv_copied, g * NCH + (c - 1))
                        else:
                            pe.wait_ge(yb_done, GROUPS * NCH - 1 + c)
                        for n in range(TPC):
                            m = nc.tensor.transpose(aux[c % 2][:, n * P:(n + 1) * P], work[c % 2][:, n * P:(n + 1) * P], ident[:, :])
                        m.then_inc(sv_turned, 1)
                for s in range(1, NCH + 1):
                    if s < NCH:
                        chunk(T_SU + 1, t + 1, s)
                    c = s - 1
                    pe.wait_ge(sv_scaled, g * NCH + s)
                    if c >= 2 or not isinstance(g, int):
                        pe.wait_ge(gained, g * NCH + (c - 1))
                    for n in range(TPC):
                        cols = slice((c * TPC + n) * P, (c * TPC + n + 1) * P)
                        m = nc.tensor.matmul(aux[2 + c % 2][:, n * P:(n + 1) * P], long_a[:, cols], sgu_now[:, :], start=True, stop=True)
                    m.then_inc(mixed, 1)

            su_pair(0)
            with pe.Fori(1, GROUPS) as g:
                su_pair(g)
            with pe.Fori(0, GATE_TILES // 2) as i:
                for u in range(2):
                    for c in range(NCH):
                        chunk(T_G + u, i * 2 + (T_G + u), c)

        @block.scalar
        def _(act):
            act.wait_ge(params_loaded, 16 * 11)
            act.wait_ge(consts, 3)
            for c in range(NCH):
                act.wait_ge(f_chain, 6 * c + 2)
                nc.scalar.activation(work[1][0:HEADS, 0:CH], work[1][0:HEADS, 0:CH], ACT.Exp).then_inc(f_chain, 1)
                act.wait_ge(f_chain, 6 * c + 3)
                nc.scalar.activation(work[1][0:HEADS, 0:CH], work[1][0:HEADS, 0:CH], ACT.Ln, bias=1.0).then_inc(f_chain, 1)

            def square(u, c, i):
                k = i * (2 * NCH) + (u * NCH + c)
                act.wait_ge(main_done, k + (T_QK * NCH + 1))
                if isinstance(k, int) and k < 2:
                    act.wait_ge(f_chain, 6 * NCH)
                else:
                    act.wait_ge(ssq_done, k - 1)
                nc.scalar.activation(work[c % 2][:, 0:CH], main[c][:, :], ACT.Square).then_inc(sq_done, 1)

            def root(u, c, i):
                k = i * (2 * NCH) + (u * NCH + c)
                act.wait_ge(ssq_done, k + 1)
                if not (isinstance(k, int) and k < 2):
                    act.wait_ge(inv_done, k - 1)
                else:
                    act.wait_ge(cum_split, NCH)
                nc.scalar.activation(work[2 + c % 2][:, 0:CH], aux[c % 2][:, :], ACT.Sqrt, bias=eps[:, 0:1], scale=1.0 / HD).then_inc(root_done, 1)

            def high(u, c, i):
                k = i * (2 * NCH) + (u * NCH + c)
                act.wait_ge(bank_free[c], i * 2 + (T_QK + u + 1))
                if not (isinstance(k, int) and k < 2):
                    stored = (k - (c % 2)) * 8
                    act.wait_ge(hi_stored[c % 2], stored)
                nc.scalar.copy(out_a[c % 2], gates[c % 2][:, :]).then_inc(hi_done, 1)

            def qk_pair(i):
                for s in range(2 * NCH + 2):
                    if s < 2 * NCH:
                        square(s // NCH, s % NCH, i)
                    if 1 <= s <= 2 * NCH:
                        root((s - 1) // NCH, (s - 1) % NCH, i)
                    if s >= 2:
                        high((s - 2) // NCH, (s - 2) % NCH, i)

            qk_pair(0)
            with act.Fori(1, QK_TILES // 2) as i:
                qk_pair(i)

            def v_copy(k):
                c = k % NCH
                act.wait_ge(main_done, T_V * NCH + k + 1)
                if k >= 2:
                    act.wait_ge(v_turned, k - 1)
                else:
                    act.wait_ge(ssq_done, QK_TILES * NCH)
                nc.scalar.copy(work[c % 2][:, 0:CH], main[c][:, :]).then_inc(bank_free[c], 1)

            def v_high(k):
                c = k % NCH
                act.wait_ge(v_turned, k + 1)
                if k < 2:
                    act.wait_ge(hi_stored[c], 16 * QK_TILES * NCH // 2)
                    act.wait_ge(lo_stored[c], 16 * QK_TILES * NCH // 2)
                else:
                    act.wait_ge(v_stored[c % 2], 16 * (k // 2))
                nc.scalar.copy(out_v[c % 2][:, :, :, 0, :], aux[c % 2][:, :].rearrange("p (n h d) -> p n h d", n=TPC, h=2)).then_inc(v_hi, 1)

            for k in range(V_TILES * NCH + 1):
                if k < V_TILES * NCH:
                    v_copy(k)
                if k >= 1:
                    v_high(k - 1)

            def p_copy(k):
                c = k % NCH
                act.wait_ge(main_done, T_P * NCH + k + 1)
                if k < 2:
                    act.wait_ge(v_turned, V_TILES * NCH)
                else:
                    act.wait_ge(pooled_done, k - 1)
                    act.wait_ge(halo_done, k)
                nc.scalar.copy(work[c % 2][:, HALO:HALO + CH], main[c][:, :]).then_inc(bank_free[c], 1)

            def yb_scale(k):
                g, c = divmod(k, NCH)
                act.wait_ge(pool_mm, k + 1)
                if k < 2:
                    act.wait_ge(v_stored[c], 16 * V_TILES * NCH // 2)
                else:
                    act.wait_ge(yb_stored[c % 2], 16 * (k // 2))
                nc.scalar.activation(out_b[c % 2].bitcast(F32), aux[c % 2][:, :], ACT.Copy, scale=pool_scale[:, g:g + 1]).then_inc(yb_done, 1)

            for k in range(GROUPS * NCH + 2):
                if k < GROUPS * NCH:
                    p_copy(k)
                if k >= 2:
                    yb_scale(k - 2)

            def su_pair(g):
                t = g * 2 + T_SU
                for s in range(NCH + 1):
                    if s < NCH:
                        act.wait_ge(main_done, t * NCH + (s + 1))
                        if s >= 2 or not isinstance(g, int):
                            act.wait_ge(sv_turned, g * NCH + (s - 1))
                        else:
                            act.wait_ge(pooled_done, GROUPS * NCH)
                        nc.scalar.activation(work[s % 2][:, 0:CH], main[s][:, :], ACT.Gelu_apprx_tanh).then_inc(bank_free[s], 1)
                    if s >= 1:
                        c = s - 1
                        act.wait_ge(sv_turned, g * NCH + s)
                        if c == 0 and not isinstance(g, int):
                            act.wait_ge(mixed, g * NCH)
                        nc.scalar.copy(long_a[:, c * CH:(c + 1) * CH], aux[c % 2][:, :]).then_inc(sv_copied, 1)
                act.wait_ge(sv_summed, g * NCH + NCH)
                nc.scalar.activation(square_roots[:, :], square_sums[:, :], ACT.Sqrt, bias=eps[:, 0:1], scale=1.0 / P).then_inc(sv_rooted, 1)
                for c in range(NCH):
                    act.wait_ge(main_done, t * NCH + (NCH + c + 1))
                    if c >= 2 or not isinstance(g, int):
                        act.wait_ge(yc_done, g * NCH + (c - 1))
                    else:
                        act.wait_ge(pool_mm, GROUPS * NCH)
                    nc.scalar.activation(work[4 + c % 2][:, 0:CH], main[c][:, :], ACT.Gelu_apprx_tanh).then_inc(bank_free[c], 1)

            su_pair(0)
            with act.Fori(1, GROUPS) as g:
                su_pair(g)

            def gate_pair(i):
                for u in range(2):
                    for c in range(NCH):
                        tile = i * 2 + u
                        if c == 0:
                            act.wait_ge(gate_bias_set, tile + 1)
                        act.wait_ge(main_done, i * (2 * NCH) + ((T_G + u) * NCH + c + 1))
                        if not (isinstance(tile, int) and tile == 0):
                            act.wait_ge(gate_stored[c], tile * 16)
                        elif c < 3:
                            act.wait_ge(lo_done, QK_TILES * NCH)
                        else:
                            act.wait_ge(yc_done, GROUPS * NCH)
                        nc.scalar.activation(gate_buf(c), main[c][:, :], ACT.Sigmoid, bias=gate_bias_now[u][:, 0:1]).then_inc(bank_free[c], 1)

            gate_pair(0)
            with act.Fori(1, GATE_TILES // 2) as i:
                gate_pair(i)

        @block.vector
        def _(dve):
            dve.wait_ge(params_loaded, 16 * 11)
            dve.wait_ge(consts, 7)
            for c in range(NCH):
                low, mag = work[0][0:HEADS, 0:CH], work[1][0:HEADS, 0:CH]
                dve.wait_ge(main_done, c + 1)
                dve.tensor_scalar(low, main[c][0:HEADS, :], f_bias[:, 0:1], 0.0, ALU.add, ALU.min).then_inc(f_chain, 1)
                dve.tensor_scalar(mag, main[c][0:HEADS, :], f_bias[:, 0:1], 0.0, ALU.add, ALU.max).then_inc(bank_free[c], 1)
                dve.wait_ge(f_chain, 6 * c + 1)
                dve.wait_ge(bank_free[c], 1)
                dve.tensor_tensor(mag, low, mag, ALU.subtract).then_inc(f_chain, 1)
                dve.wait_ge(f_chain, 6 * c + 4)
                dve.tensor_tensor(low, low, mag, ALU.subtract).then_inc(f_chain, 1)
                dve.wait_ge(f_chain, 6 * c + 5)
                dve.tensor_tensor_scan(cum_chunk[c % 2], ones8, low,
                                       0.0 if c == 0 else cum_chunk[(c - 1) % 2][:, CH - 1:CH],
                                       ALU.mult, ALU.add).then_inc(f_chain, 1)
                dve.wait_ge(f_chain, 6 * c + 6)
                if c >= 2:
                    dve.wait_ge(cum_stored[c % 2], 16)
                dve.tensor_copy(cum_parts[c % 2][:, 0, :], cum_chunk[c % 2]).then_inc(cum_high, 1)
                dve.wait_ge(cum_high, c + 1)
                dve.tensor_tensor(cum_parts[c % 2][:, 1, :], cum_chunk[c % 2], cum_parts[c % 2][:, 0, :], ALU.subtract).then_inc(cum_split, 1)
            dve.wait_ge(turned_w, 1)
            dve.tensor_copy(sgu_wT[:, :, :], aux[3][:, :].rearrange("p (g t) -> p g t", g=GROUPS)).then_inc(sgu_w_ready, 1)
            dve.reciprocal(pool_inverse[:, :, :], pool_count[:, :, :]).then_inc(sgu_w_ready, 1)

            def normalise(u, c, i):
                k = i * (2 * NCH) + (u * NCH + c)
                dve.wait_ge(root_done, k + 1)
                dve.reciprocal(work[4 + c % 2][:, 0:CH], work[2 + c % 2][:, 0:CH]).then_inc(inv_done, 1)
                dve.wait_ge(inv_done, k + 1)
                if not (isinstance(k, int) and k < 2):
                    dve.wait_ge(lo_done, k - 1)
                tile = i * 2 + u
                gain = qk_gain_of(tile)
                dve.scalar_tensor_tensor(out=gates[c % 2][:, :], in0=main[c][:, :], scalar=gain,
                                         in1=work[4 + c % 2][:, 0:CH], op0=ALU.mult, op1=ALU.mult).then_inc(bank_free[c], 1)

            def low_part(u, c, i):
                k = i * (2 * NCH) + (u * NCH + c)
                dve.wait_ge(hi_done, k + 1)
                if not (isinstance(k, int) and k < 2):
                    dve.wait_ge(lo_stored[c % 2], (k - (c % 2)) * 8)
                dve.tensor_tensor(out_b[c % 2], gates[c % 2][:, :], out_a[c % 2], ALU.subtract).then_inc(lo_done, 1)

            def qk_gain_of(tile):
                return qk_gain8[:, bass.ds(tile, 1)]

            for j in range(QK_TILES):
                src = qk_gain[:, 0:1] if j < QK_TILES // 2 else qk_gain[:, 1:2]
                dve.tensor_scalar(qk_gain8[:, j:j + 1], src, -HD ** -0.5 if j < QK_TILES // 2 else 1.0, None, ALU.mult).then_inc(gains_ready, 1)
            dve.wait_ge(gains_ready, QK_TILES)

            def qk_pair(i):
                for s in range(2 * NCH + 1):
                    if s < 2 * NCH:
                        normalise(s // NCH, s % NCH, i)
                    if s >= 1:
                        low_part((s - 1) // NCH, (s - 1) % NCH, i)

            qk_pair(0)
            with dve.Fori(1, QK_TILES // 2) as i:
                qk_pair(i)

            for k in range(V_TILES * NCH):
                c = k % NCH
                dve.wait_ge(v_hi, k + 1)
                dve.tensor_tensor(out_v[c % 2][:, :, :, 1, :], aux[c % 2][:, :].rearrange("p (n h d) -> p n h d", n=TPC, h=2),
                                  out_v[c % 2][:, :, :, 0, :], ALU.subtract).then_inc(v_lo, 1)

            steps = 0
            E_ = HALO + CH
            for k in range(GROUPS * NCH):
                g, c = divmod(k, NCH)
                w = WINDOWS[g]
                p = work[c % 2]
                dve.wait_ge(bank_free[c], T_P + g + 1)
                if c == 0:
                    dve.memset(p[:, 0:HALO], 0.0).then_inc(halo_done, 1)
                else:
                    dve.tensor_copy(p[:, 0:HALO], work[(c - 1) % 2][:, CH:CH + HALO]).then_inc(halo_done, 1)
                dve.wait_ge(halo_done, k + 1)
                src, reach, b = p, 1, 0
                while reach < w:
                    dst = work[2 + b]
                    first = 2 * reach - 1
                    dve.tensor_tensor(dst[:, first:E_], src[:, first:E_], src[:, first - reach:E_ - reach], ALU.add).then_inc(sum_step, 1)
                    steps += 1
                    dve.wait_ge(sum_step, steps)
                    src, reach, b = dst, reach * 2, 1 - b
                if k >= 2:
                    dve.wait_ge(pool_mm, k - 1)
                pooled = work[4 + c % 2]
                if c == 0:
                    dve.tensor_tensor(work[2 + b][:, HALO:2 * HALO], src[:, HALO:2 * HALO], pool_inverse[:, g, :], ALU.mult).then_inc(sum_step, 1)
                    steps += 1
                    dve.wait_ge(sum_step, steps)
                    dve.tensor_tensor(pooled[:, 0:HALO], work[2 + b][:, HALO:2 * HALO], p[:, HALO:2 * HALO], ALU.subtract).then_inc(sum_step, 1)
                    steps += 1
                    dve.wait_ge(sum_step, steps)
                lo = HALO if c == 0 else 0
                dve.scalar_tensor_tensor(out=pooled[:, lo:CH], in0=src[:, HALO + lo:E_], scalar=1.0 / w, in1=p[:, HALO + lo:E_],
                                         op0=ALU.mult, op1=ALU.subtract).then_inc(pooled_done, 1)

            def su_pair(g):
                for c in range(NCH):
                    dve.wait_ge(sv_copied, g * NCH + (c + 1))
                    part = long_a[:, c * CH:(c + 1) * CH]
                    if c >= 1 or not isinstance(g, int):
                        dve.wait_ge(sv_summed, g * NCH + c)
                    dve.tensor_tensor(work[2][:, 0:CH], part, part, ALU.mult).then_inc(sv_squared, 1)
                    dve.wait_ge(sv_squared, g * NCH + (c + 1))
                    dve.tensor_reduce(square_sums[:, c * TPC:(c + 1) * TPC], work[2][:, 0:CH].rearrange("p (n d) -> p n d", n=TPC),
                                      AX.X, ALU.add).then_inc(sv_summed, 1)
                dve.tensor_copy(sgu_now[:, :], sgu_wT[:, bass.ds(g, 1), :].rearrange("p a t -> p (a t)")).then_inc(sgu_now_set, 1)
                dve.wait_ge(sv_rooted, g + 1)
                dve.reciprocal(inverse_roots[:, :], square_roots[:, :]).then_inc(sv_inverted, 1)
                dve.wait_ge(sv_inverted, g + 1)
                dve.wait_ge(sgu_now_set, g + 1)
                for c in range(NCH):
                    for n in range(TPC):
                        j = c * TPC + n
                        m = dve.tensor_scalar(long_a[:, j * P:(j + 1) * P], long_a[:, j * P:(j + 1) * P], inverse_roots[:, j:j + 1], None, ALU.mult)
                    m.then_inc(sv_scaled, 1)
                for c in range(NCH):
                    dve.wait_ge(mixed, g * NCH + (c + 1))
                    if c >= 1 or not isinstance(g, int):
                        dve.wait_ge(yc_done, g * NCH + c)
                    dve.tensor_scalar(work[2][:, 0:CH], aux[2 + c % 2][:, :], sgu_gain[:, bass.ds(g, 1)], None, ALU.mult).then_inc(gained, 1)
                    dve.wait_ge(gained, g * NCH + (c + 1))
                    bias = sgu_bias[:, bass.ds(g, 1), :].broadcast_to([P, TPC, P])
                    dve.tensor_tensor(work[3][:, 0:CH].rearrange("p (n t) -> p n t", n=TPC), work[2][:, 0:CH].rearrange("p (n t) -> p n t", n=TPC),
                                      bias, ALU.add).then_inc(biased, 1)
                    dve.wait_ge(biased, g * NCH + (c + 1))
                    dve.wait_ge(bank_free[c], g * 2 + (T_SU + 2))
                    if c >= 2:
                        dve.wait_ge(yc_stored[c % 2], g * 32 + 16 * (c // 2))
                    elif isinstance(g, int):
                        dve.wait_ge(yb_stored[c % 2], 16 * GROUPS * NCH // 2)
                    else:
                        dve.wait_ge(yc_stored[c % 2], g * 32)
                    dve.tensor_tensor(out_b[c % 2].bitcast(F32), work[3][:, 0:CH], work[4 + c % 2][:, 0:CH], ALU.mult).then_inc(yc_done, 1)

            su_pair(0)
            with dve.Fori(1, GROUPS) as g:
                su_pair(g)

            def gate_bias_columns(i):
                for u in range(2):
                    if not isinstance(i, int):
                        dve.wait_ge(bank_free[NCH - 1], i * 2 + (T_G + u - 1))
                    dve.tensor_copy(gate_bias_now[u][:, :], gate_bias[:, bass.ds(i * 2 + u, 1)]).then_inc(gate_bias_set, 1)

            gate_bias_columns(0)
            with dve.Fori(1, GATE_TILES // 2) as i:
                gate_bias_columns(i)
    return used


def groups_of(i):
    return i // 4 + 1


def attend(nc, ident, scratch, spent=()):
    PER_HEAD = sum(groups_of(i) for i in range(NT))
    RING = 4
    AHEAD_Q = 2
    Y_TILES = HEADS * HD // P
    DEPTH = 2
    with ExitStack() as ctx:
        def sb(name, shape, dt=F32):
            return ctx.enter_context(nc.sbuf_tensor("at_" + name, shape, dt))

        def sem(name):
            return ctx.enter_context(nc.semaphore("at_" + name))

        q_high = sb("q_high", [P, S], F32R)
        q_low = sb("q_low", [P, S], F32R)
        k_both = sb("k_both", [P, 2, S], F32R)
        k_cum = sb("k_cum", [P, 2, S], F32R)
        v_both = sb("v_both", [P, 2, NT, 2 * HD], F32R)
        scores = [sb(f"scores{b}", [P, S]) for b in range(RING)]
        probs = [sb(f"probs{b}", [P, S]) for b in range(2)]
        turned_hi = [sb(f"turned_hi{b}", [P, 4, P], F32R) for b in range(4)]
        turned_lo = [sb(f"turned_lo{b}", [P, 4, P], F32R) for b in range(4)]
        y = sb("y", [P, NT, HEADS * HD])
        least = sb("least", [P, RING, 4])
        row_sum = sb("row_sum", [P, 4])
        row_inv = sb("row_inv", [P, 2])
        y_part = sb("y_part", [P, 2, HD])
        ones_f = sb("ones_f", [P, S])
        mask_f = sb("mask_f", [P, P])
        mask = sb("mask", [P, P], F32R)
        ident_r = sb("ident_r", [P, P], F32R)
        s_ps = [ctx.enter_context(nc.psum_tensor(f"at_s{b}", [P, CH], F32)) for b in range(2)]
        t_ps = [ctx.enter_context(nc.psum_tensor(f"at_t{b}", [P, 4, P], F32)) for b in range(4)]
        o_ps = [ctx.enter_context(nc.psum_tensor(f"at_o{b}", [P, CH], F32)) for b in range(2)]

        consts, ones_set = sem("consts"), sem("ones_set")
        q_loaded = [sem(f"q_loaded{c}") for c in range(4)]
        k_loaded, v_loaded = sem("k_loaded"), sem("v_loaded")
        KV_INC = 16 * 4
        q_free, scored, moved, exped = sem("q_free"), sem("scored"), sem("moved"), sem("exped")
        turned, high, low = sem("turned"), sem("high"), sem("low")
        weighed, inverted, half, y_done = sem("weighed"), sem("inverted"), sem("half"), sem("y_done")
        y_turned, yT_copied = sem("y_turned"), [sem(f"yT_copied{b}") for b in range(2)]
        yT_stored = sem("yT_stored")
        block = ctx.enter_context(nc.Block())

        tiles = list(range(NT - 1, -1, -1))
        first = {}
        n = 0
        for s, i in enumerate(tiles):
            first[s] = n
            n += groups_of(i)

        @block.gpsimd
        def _(pool):
            if spent:
                pool.sem_clear(range(min(s.num for s in spent), max(s.num for s in spent) + 1))
            pool.memset(ones_f[:, :], 1.0).then_inc(consts, 1)
            pool.memset(mask_f[:, :], 0.0).then_inc(consts, 1)
            pool.wait_ge(consts, 2)
            pool.affine_select(out=mask_f[:, :], in_=mask_f[:, :], compare_op=ALU.is_ge, fill=1e30, base=0,
                               pattern=[[-1, P]], channel_multiplier=1).then_inc(consts, 1)

        @block.sync
        def _(sp):
            def load_q(h, c):
                if not isinstance(h, int) or h > 0:
                    sp.wait_ge(scored, h * PER_HEAD + (first[NT - 1 - 4 * c] + groups_of(4 * c) - PER_HEAD))
                    sp.sem_inc(q_free)
                cols = slice(c * CH, (c + 1) * CH)
                rows = bass.ds(h * HD, HD)
                sp.dma_start(q_high[0:HD, cols].bitcast(F32), scratch["q_rows"][0][rows, cols]).then_inc(q_loaded[c], 16)
                sp.dma_start(q_high[HD:P, cols].bitcast(F32), scratch["q_rows"][0][rows, cols]).then_inc(q_loaded[c], 16)
                sp.dma_start(q_low[0:HD, cols].bitcast(F32), scratch["q_rows"][1][rows, cols]).then_inc(q_loaded[c], 16)

            def load_k(h):
                b = h % 2
                if not isinstance(h, int):
                    sp.wait_ge(y_done, h * NT - NT)
                if not isinstance(h, int) or h > 0:
                    sp.wait_ge(scored, (h - 1) * PER_HEAD + (first[2] + 1))
                rows = bass.ds(h * HD, HD)
                hi, lo = scratch["k_rows"][0][rows, :], scratch["k_rows"][1][rows, :]
                for dst, src in ((k_both[0:HD, bass.ds(b, 1), :], hi), (k_both[HD:P, bass.ds(b, 1), :], lo), (k_cum[0:HD, bass.ds(b, 1), :], hi),
                                 (k_cum[HD:HD + 2, bass.ds(b, 1), :], scratch["cum"][bass.ds(h, 1), :, :].rearrange("a l s -> (a l) s"))):
                    sp.dma_start(dst.rearrange("p a s -> p (a s)").bitcast(F32), src).then_inc(k_loaded, 16)

            def load_v(h):
                b = h % 2
                if not isinstance(h, int) or h > 0:
                    sp.wait_ge(weighed, (h - 1) * PER_HEAD + 1)
                src = scratch["v"][:, :, :, bass.ds(h, 1), :, :].rearrange("c p n h l d -> p c n (h l d)")
                for c in range(NCH):
                    sp.dma_start(v_both[:, bass.ds(b, 1), c * TPC:(c + 1) * TPC, :].rearrange("p a n d -> p (a n) d").bitcast(F32),
                                 src[:, c]).then_inc(v_loaded, 16)

            load_k(0)
            load_q(0, 3)
            load_v(0)
            for c in range(2, -1, -1):
                load_q(0, c)
            load_k(1)
            load_v(1)
            for c in range(3, -1, -1):
                load_q(1, c)
            with sp.Fori(2, HEADS) as h:
                load_k(h)
                load_v(h)
                for c in range(3, -1, -1):
                    load_q(h, c)
            for f in range(Y_TILES):
                for by in range(2):
                    sp.wait_ge(yT_copied[by], (f + 1) * NCH // 2)
                sp.dma_start(scratch["y"][0, f, :, :], scores[f][:, :]).then_inc(yT_stored, 16)
            sp.wait_ge(yT_stored, 16 * Y_TILES)

        @block.tensor
        def _(pe):
            def score(h, s, j):
                i = tiles[s]
                n = first[s] + j
                if j == 0:
                    if s == 0:
                        pe.wait_ge(k_loaded, h * KV_INC + KV_INC)
                    if i % 4 == 3:
                        pe.wait_ge(q_loaded[i // 4], h * 48 + 48)
                if not (isinstance(h, int) and h == 0 and n < 2):
                    pe.wait_ge(moved, h * PER_HEAD + (n - 1))
                width = min(CH, (i + 1) * P - j * CH)
                cols = slice(j * CH, j * CH + width)
                b = h % 2
                diag = j == groups_of(i) - 1
                out = s_ps[n % 2][:, 0:width]
                kb = k_both[:, bass.ds(b, 1), cols].rearrange("p a s -> p (a s)")
                kc = k_cum[0:HD + 2, bass.ds(b, 1), cols].rearrange("p a s -> p (a s)")
                nc.tensor.matmul(out, q_high[:, i * P:(i + 1) * P], kb, start=True, stop=False)
                m = nc.tensor.matmul(out, q_low[0:HD + 2, i * P:(i + 1) * P], kc, start=False, stop=not diag)
                if diag:
                    m = nc.tensor.matmul(s_ps[n % 2][:, width - P:width], ident_r[:, :], mask[:, :], start=False, stop=True)
                m.then_inc(scored, 1)

            def turn(h, s, j):
                i = tiles[s]
                n = first[s] + j
                if j == 0:
                    pe.wait_ge(exped, h * NT + (s + 1))
                if not (isinstance(h, int) and h == 0 and n < 4):
                    pe.wait_ge(low, h * PER_HEAD + (n - 3))
                count = min(4, i + 1 - 4 * j)
                for q in range(count):
                    k = 4 * j + q
                    m = nc.tensor.transpose(t_ps[n % 4][:, q, :], probs[s % 2][:, k * P:(k + 1) * P], ident[:, :])
                m.then_inc(turned, 1)

            def weigh(h, s, j):
                i = tiles[s]
                n = first[s] + j
                pe.wait_ge(low, h * PER_HEAD + (n + 1))
                if j == 0 and not (isinstance(h, int) and h == 0 and s < 2):
                    pe.wait_ge(y_done, h * NT + (s - 1))
                if s == 0 and j == 0:
                    pe.wait_ge(v_loaded, h * KV_INC + KV_INC)
                count = min(4, i + 1 - 4 * j)
                b = h % 2
                for q in range(count):
                    k = 4 * j + q
                    v = v_both[:, bass.ds(b, 1), k, :].rearrange("p a d -> p (a d)")
                    nc.tensor.matmul(o_ps[s % 2][:, 0:2 * HD], turned_hi[n % 4][:, q, :], v, start=(k == 0), stop=False)
                    m = nc.tensor.matmul(o_ps[s % 2][:, 0:2 * HD], turned_lo[n % 4][:, q, :], v, start=False, stop=(k == i))
                m.then_inc(weighed, 1)

            def head(h, last):
                pending = [] if isinstance(h, int) and h == 0 else [(h - 1, NT - DEPTH + d, 0) for d in range(DEPTH)]
                for s in range(NT):
                    i = tiles[s]
                    ahead = None
                    if s + AHEAD_Q < NT:
                        ahead = (h, s + AHEAD_Q)
                    elif not last:
                        ahead = (h + 1, s + AHEAD_Q - NT)
                    na = groups_of(tiles[ahead[1]]) if ahead else 0
                    for j in range(max(na, groups_of(i))):
                        if j < na:
                            score(*ahead, j)
                        if j < groups_of(i):
                            turn(h, s, j)
                            pending.append((h, s, j))
                        if len(pending) > DEPTH:
                            weigh(*pending.pop(0))
                while last and pending:
                    weigh(*pending.pop(0))

            pe.wait_ge(ones_set, 4)
            for s in range(AHEAD_Q):
                for j in range(groups_of(tiles[s])):
                    score(0, s, j)
            head(0, False)
            with pe.Fori(1, HEADS - 1) as h:
                head(h, False)
            head(HEADS - 1, True)
            for n in range(Y_TILES * NCH):
                f, c = divmod(n, NCH)
                if n == 0:
                    pe.wait_ge(y_done, HEADS * NT)
                if n >= 4:
                    pe.wait_ge(yT_copied[n % 2], (n - 4) // 2 + 1)
                for q in range(4):
                    m = nc.tensor.transpose(t_ps[n % 4][:, q, :], y[:, c * 4 + q, f * P:(f + 1) * P], ident[:, :])
                m.then_inc(y_turned, 1)

        @block.scalar
        def _(act):
            def exponent(h, s):
                i = tiles[s]
                act.wait_ge(moved, h * PER_HEAD + (first[s] + groups_of(i)))
                if not (isinstance(h, int) and h == 0 and s < 2):
                    before = first[s - 2] + groups_of(tiles[s - 2]) if s >= 2 else first[s - 2 + NT] + groups_of(tiles[s - 2 + NT]) - PER_HEAD
                    act.wait_ge(turned, h * PER_HEAD + before)
                    if s >= 4 or not isinstance(h, int) or h > 0:
                        act.wait_ge(y_done, h * NT + (s - 3))
                width = (i + 1) * P
                nc.scalar.activation(probs[s % 2][:, 0:width], scores[s % RING][:, 0:width], ACT.Exp,
                                     bias=least[:, s % RING, groups_of(i) - 1:groups_of(i)], scale=-1.0,
                                     accum_out=row_sum[:, s % 4:s % 4 + 1]).then_inc(exped, 1)

            def high_part(h, s, j):
                n = first[s] + j
                act.wait_ge(turned, h * PER_HEAD + (n + 1))
                if not (isinstance(h, int) and h == 0 and n < 4):
                    act.wait_ge(weighed, h * PER_HEAD + (n - 3))
                count = min(4, tiles[s] + 1 - 4 * j)
                nc.scalar.copy(turned_hi[n % 4][:, 0:count, :], t_ps[n % 4][:, 0:count, :]).then_inc(high, 1)

            def head(h, last):
                for s in range(NT):
                    for j in range(groups_of(tiles[s])):
                        high_part(h, s, j)
                        if j == 0:
                            if s + 1 < NT:
                                exponent(h, s + 1)
                            elif not last:
                                exponent(h + 1, 0)

            exponent(0, 0)
            head(0, False)
            with act.Fori(1, HEADS - 1) as h:
                head(h, False)
            head(HEADS - 1, True)
            for n in range(1, Y_TILES * NCH, 2):
                f, c = divmod(n, NCH)
                act.wait_ge(y_turned, n + 1)
                nc.scalar.copy(scores[f][:, c * CH:(c + 1) * CH], t_ps[n % 4][:, :, :].rearrange("p a b -> p (a b)")).then_inc(yT_copied[1], 1)

        @block.vector
        def _(dve):
            dve.wait_ge(consts, 3)
            dve.tensor_copy(mask[:, :], mask_f[:, :]).then_inc(ones_set, 1)
            dve.tensor_copy(ident_r[:, :], ident[:, :]).then_inc(ones_set, 1)
            dve.tensor_copy(q_low[HD:HD + 2, :], ones_f[HD:HD + 2, :]).then_inc(ones_set, 1)
            dve.memset(least[:, :, :], 0.0).then_inc(ones_set, 1)

            def move(h, s, j):
                i = tiles[s]
                n = first[s] + j
                dve.wait_ge(scored, h * PER_HEAD + (n + 1))
                if j == 0 and not (isinstance(h, int) and h == 0 and s < RING):
                    dve.wait_ge(exped, h * NT + (s + 1 - RING))
                if j > 0:
                    dve.wait_ge(moved, h * PER_HEAD + n)
                width = min(CH, (i + 1) * P - j * CH)
                dve.tensor_scalar(scores[s % RING][:, j * CH:j * CH + width], s_ps[n % 2][:, 0:width], 1.0,
                                  3e38 if j == 0 else least[:, s % RING, j - 1:j], ALU.mult, ALU.min,
                                  accum_out=least[:, s % RING, j:j + 1]).then_inc(moved, 1)

            def low_part(h, s, j):
                n = first[s] + j
                dve.wait_ge(high, h * PER_HEAD + (n + 1))
                count = min(4, tiles[s] + 1 - 4 * j)
                dve.tensor_tensor(turned_lo[n % 4][:, 0:count, :], t_ps[n % 4][:, 0:count, :], turned_hi[n % 4][:, 0:count, :],
                                  ALU.subtract).then_inc(low, 1)

            def finish_a(h, s):
                dve.reciprocal(row_inv[:, s % 2:s % 2 + 1], row_sum[:, s % 4:s % 4 + 1]).then_inc(inverted, 1)

            def finish_b(h, s):
                dve.wait_ge(weighed, h * PER_HEAD + (first[s] + groups_of(tiles[s])))
                dve.wait_ge(inverted, h * NT + (s + 1))
                dve.tensor_scalar(y_part[:, s % 2, :], o_ps[s % 2][:, 0:HD], row_inv[:, s % 2:s % 2 + 1], None, ALU.mult).then_inc(half, 1)

            def finish_c(h, s):
                dve.wait_ge(half, h * NT + (s + 1))
                dve.scalar_tensor_tensor(out=y[:, tiles[s], bass.ds(h * HD, HD)], in0=o_ps[s % 2][:, HD:2 * HD], scalar=row_inv[:, s % 2:s % 2 + 1],
                                         in1=y_part[:, s % 2, :], op0=ALU.mult, op1=ALU.add).then_inc(y_done, 1)

            def head(h, last):
                begun = isinstance(h, int) and h == 0
                for s in range(NT):
                    i = tiles[s]
                    ahead = (h, s + AHEAD_Q) if s + AHEAD_Q < NT else (None if last else (h + 1, s + AHEAD_Q - NT))
                    na = groups_of(tiles[ahead[1]]) if ahead else 0
                    done = (h, s - 2) if s >= 2 else (None if begun else (h - 1, NT - 2 + s))
                    for j in range(max(na, groups_of(i))):
                        finishing = j == 0 and done
                        if finishing:
                            finish_a(*done)
                        if j < na:
                            move(*ahead, j)
                        if finishing:
                            finish_b(*done)
                        if j < groups_of(i):
                            low_part(h, s, j)
                        if finishing:
                            finish_c(*done)
                if last:
                    for s in (NT - 2, NT - 1):
                        finish_a(h, s)
                        finish_b(h, s)
                        finish_c(h, s)

            for s in range(AHEAD_Q):
                for j in range(groups_of(tiles[s])):
                    move(0, s, j)
            head(0, False)
            with dve.Fori(1, HEADS - 1) as h:
                head(h, False)
            head(HEADS - 1, True)
            for n in range(0, Y_TILES * NCH, 2):
                f, c = divmod(n, NCH)
                dve.wait_ge(y_turned, n + 1)
                dve.tensor_copy(scores[f][:, c * CH:(c + 1) * CH], t_ps[n % 4][:, :, :].rearrange("p a b -> p (a b)")).then_inc(yT_copied[0], 1)


BR_K = 4
N_BR = 3


def merge(nc, ones_col, w_branch, scratch):
    YT = N_BR * BR_K
    NF = KD
    with ExitStack() as ctx:
        def sb(name, shape, dt=F32):
            return ctx.enter_context(nc.sbuf_tensor("me_" + name, shape, dt))

        def sem(name):
            return ctx.enter_context(nc.semaphore("me_" + name))

        y_hi = [sb(f"y_hi{s}", [P, YT, CH], F32R) for s in range(3)]
        y_lo = [sb(f"y_lo{s}", [P, YT, CH], F32R) for s in range(3)]
        raw = [sb(f"w_raw{b}", [P, YT, P]) for b in range(2)]
        w_hi = [sb(f"w_hi{b}", [P, YT, P], F32R) for b in range(2)]
        w_lo = [sb(f"w_lo{b}", [P, YT, P], F32R) for b in range(2)]
        gate = [sb(f"gate{c}", [P, N_BR, CH]) for c in range(2)]
        part = sb("part", [P, CH])
        total = [sb(f"total{c}", [P, CH]) for c in range(2)]
        ps = [ctx.enter_context(nc.psum_tensor(f"me_ps{i}", [P, CH], F32)) for i in range(2 * N_BR)]
        w_loaded = [sem(f"w_loaded{b}") for b in range(2)]
        y_loaded = [[sem(f"y_loaded{c}{b}") for b in range(N_BR)] for c in range(NCH)]
        g_loaded = [sem(f"g_loaded{c}") for c in range(2)]
        stored = [sem(f"stored{c}") for c in range(2)]
        w_split_hi, w_split, y_high, y_low = sem("w_split_hi"), sem("w_split"), sem("y_high"), sem("y_low")
        product, gated, added = sem("product"), sem("gated"), sem("added")
        block = ctx.enter_context(nc.Block())
        w_view = w_branch.rearrange("o b (k p) n -> p (o b k) n", p=P)
        g_view = scratch["gates"].rearrange("(b f) p s -> p f b s", b=N_BR)
        y_view = scratch["y"].rearrange("b k p s -> p (b k) s")

        @block.sync
        def _(sp):
            def load_y(c, b):
                if c == 3:
                    sp.wait_ge(product, (NF - 1) * 2 * N_BR + N_BR)
                k = slice(b * BR_K, (b + 1) * BR_K)
                sp.dma_start(y_lo[c % 3][:, k, :].bitcast(F32), y_view[:, k, c * CH:(c + 1) * CH]).then_inc(y_loaded[c][b], 16)

            def load_w(half, f, b):
                t = f + half * NF
                if not (isinstance(t, int) and t < 2):
                    sp.wait_ge(w_split, t - 1)
                sp.dma_start(raw[b][:, :, :], w_view[:, :, bass.ds(f * P, P)]).then_inc(w_loaded[b], 16)

            def load_step_gates(n, u, f, chunk):
                if not (isinstance(n, int) and n < 2):
                    sp.wait_ge(gated, (n - 1) * N_BR)
                sp.dma_start(gate[u][:, :, :], g_view[:, bass.ds(f, 1), :, chunk * CH:(chunk + 1) * CH]
                             .rearrange("p f b s -> p (f b) s")).then_inc(g_loaded[u], 16)

            def store_step(n, u, f, chunk):
                sp.wait_ge(added, n * 2 + 2)
                sp.dma_start(scratch["merged"][bass.ds(f, 1), :, chunk * CH:(chunk + 1) * CH].rearrange("a p s -> (a p) s"),
                             total[u][:, :]).then_inc(stored[u], 16)

            def load_gates(half, f, c):
                load_step_gates((f + half * NF) * 2 + c, c, f, 2 * half + c)

            def store(half, f, c):
                store_step((f + half * NF) * 2 + c, c, f, 2 * half + c)

            load_w(0, 0, 0)
            load_y(0, 0)
            load_y(0, 1)
            load_w(0, 1, 1)
            load_y(0, 2)
            load_y(1, 0)
            load_step_gates(0, 0, 0, 0)
            load_y(1, 1)
            load_y(1, 2)
            load_step_gates(1, 1, 1, 0)
            load_step_gates(2, 0, 0, 1)
            load_y(2, 0)
            load_step_gates(3, 1, 1, 1)
            load_w(0, 2, 0)
            load_w(0, 3, 1)
            store_step(0, 0, 0, 0)
            store_step(1, 1, 1, 0)
            load_y(2, 1)
            store_step(2, 0, 0, 1)
            load_gates(0, 2, 0)
            store_step(3, 1, 1, 1)
            load_gates(0, 2, 1)
            load_y(2, 2)

            def features(half, i, last):
                for u in range(2):
                    f = i * 2 + u
                    if not last:
                        load_w(half, f + 2, u)
                    for c in range(2):
                        store(half, f, c)
                        if not (last and u == 1):
                            load_gates(half, f + 1, c)

            for half in range(2):
                with sp.Fori(1 - half, NF // 2 - 1) as i:
                    features(half, i, False)
                if half == 0:
                    load_w(1, 0, 0)
                    load_w(1, 1, 1)
                    for u in range(2):
                        for c in range(2):
                            store(0, NF - 2 + u, c)
                            if u == 0:
                                load_gates(0, NF - 1, c)
                            else:
                                load_gates(1, 0, c)
                                if c == 0:
                                    for b in range(N_BR):
                                        load_y(3, b)
                else:
                    features(1, NF // 2 - 1, True)
            for c in range(2):
                sp.wait_ge(stored[c], 16 * 2 * NF)

        @block.gpsimd
        def _(pool):
            def split(b, t, used=None):
                if isinstance(t, int):
                    pool.wait_ge(w_loaded[b], 16 * (t // 2 + 1))
                else:
                    pool.wait_ge(w_loaded[b], t * 8 + (16 - 8 * b))
                if not (isinstance(t, int) and t < 2):
                    pool.wait_ge(product, used if used else (t - 1) * (2 * N_BR))
                pool.tensor_tensor(w_hi[b][:, :, :], raw[b][:, :, :], ones_col[:, 0:1, None].broadcast_to(list(raw[b].shape)), ALU.mult).then_inc(w_split_hi, 1)
                pool.wait_ge(w_split_hi, t + 1)
                pool.tensor_tensor(w_lo[b][:, :, :], raw[b][:, :, :], w_hi[b][:, :, :], ALU.subtract).then_inc(w_split, 1)

            split(0, 0)
            split(1, 1)
            split(0, 2, used=3 * N_BR)
            split(1, 3, used=4 * N_BR)
            with pool.Fori(2, NF) as i:
                split(0, i * 2)
                split(1, i * 2 + 1)

        @block.tensor
        def _(pe):
            def products(slot, u, bank, b):
                q = 0
                for k in range(b * BR_K, (b + 1) * BR_K):
                    for w, y in ((w_hi, y_hi), (w_hi, y_lo), (w_lo, y_hi)):
                        m = nc.tensor.matmul(ps[bank][:, :], w[u][:, k, :], y[slot][:, k, :], start=(q == 0), stop=(q == 3 * BR_K - 1))
                        q += 1
                m.then_inc(product, 1)

            def first_features():
                for n in range(4):
                    u, c = n % 2, n // 2
                    for b in range(N_BR):
                        if b == 0:
                            pe.wait_ge(w_split, u + 1)
                        if n >= 2:
                            pe.wait_ge(gated, (n - 2) * N_BR + b + 1)
                        pe.wait_ge(y_low, c * N_BR + b + 1)
                        products(c, u, u * N_BR + b, b)

            def features(half, i):
                for u in range(2):
                    t = i * 2 + (half * NF + u)
                    for c in range(2):
                        slot = (2 * half + c) % 3
                        for b in range(N_BR):
                            n = t * (2 * N_BR) + (c * N_BR + b)
                            if b == 0 and c == 0:
                                pe.wait_ge(w_split, t + 1)
                            pe.wait_ge(gated, n - (2 * N_BR - 1))
                            if half == 1:
                                pe.wait_ge(y_low, (2 + c) * N_BR + b + 1)
                            products(slot, u, c * N_BR + b, b)

            first_features()
            with pe.Fori(1, NF // 2) as i:
                features(0, i)
            with pe.Fori(0, NF // 2) as i:
                features(1, i)

        def branch(c, b):
            return b + c * N_BR

        def part_of(y, c, b):
            return y[c % 3][:, bass.ds(b * BR_K, BR_K), :]

        @block.scalar
        def _(act):
            for c in range(NCH):
                for b in range(N_BR):
                    act.wait_ge(y_loaded[c][b], 16)
                    nc.scalar.copy(part_of(y_hi, c, b), part_of(y_lo, c, b).bitcast(F32)).then_inc(y_high, 1)

        @block.vector
        def _(dve):
            def low(c, b):
                dve.wait_ge(y_high, branch(c, b) + 1)
                dve.tensor_tensor(part_of(y_lo, c, b), part_of(y_lo, c, b).bitcast(F32), part_of(y_hi, c, b), ALU.subtract).then_inc(y_low, 1)

            def gate_and_add(t, c):
                for b in range(N_BR):
                    n = t * (2 * N_BR) + (c * N_BR + b)
                    dve.wait_ge(product, n + 1)
                    if b == 0:
                        dve.wait_ge(g_loaded[c], t * 16 + 16)
                        if not (isinstance(t, int) and t == 0):
                            dve.wait_ge(stored[c], t * 16)
                    elif not (isinstance(t, int) and t == 0 and c == 0 and b == 1):
                        dve.wait_ge(added, t * 4 + (2 * c + b - 1))
                    dst = total[c] if b == 0 else part
                    dve.tensor_tensor(dst[:, :], ps[c * N_BR + b][:, :], gate[c][:, b, :], ALU.mult).then_inc(gated, 1)
                    if b > 0:
                        dve.wait_ge(gated, n + 1)
                        dve.tensor_tensor(total[c][:, :], total[c][:, :], part[:, :], ALU.add).then_inc(added, 1)

            for b in range(N_BR):
                low(0, b)
            low(1, 0)
            gate_and_add(0, 0)
            low(1, 1)
            low(1, 2)
            gate_and_add(0, 1)
            for c in range(2):
                gate_and_add(1, c)
            low(2, 0)
            with dve.Fori(1, 3) as i:
                for u in range(2):
                    for c in range(2):
                        gate_and_add(i * 2 + u, c)
                low(2, i)
            for u in range(2):
                for c in range(2):
                    gate_and_add(6 + u, c)
            for b in range(N_BR):
                low(3, b)
            with dve.Fori(NF // 2, NF) as i:
                for u in range(2):
                    for c in range(2):
                        gate_and_add(i * 2 + u, c)


N_GROUP, PER_GROUP = 4, 8
N_EXP = N_GROUP * PER_GROUP
N_LOGIT = N_GROUP + N_EXP
FE = 256
FK = FE // P
LOADED = 3
TOP = 2
BLOCKS = (S * TOP) // P + N_EXP
AHEAD = 4
TABLE = BLOCKS + AHEAD
PAD = 16384


def project_out(nc, ones_col, staging, x, w_out, g_ffn, w_rg, b_rg, w_re, b_re, ident, logits, scratch):
    with ExitStack() as ctx:
        def sb(name, shape, dt=F32):
            return ctx.enter_context(nc.sbuf_tensor("po_" + name, shape, dt))

        def sem(name):
            return ctx.enter_context(nc.semaphore("po_" + name))

        w_raw = [staging[:, k * D // (KD * CH), (k * D // CH) % KD:(k * D // CH) % KD + D // CH, :].rearrange("p a n -> p (a n)")
                 for k in range(KD)]
        w_hi, w_lo = sb("w_hi", [P, KD, D], F32R), sb("w_lo", [P, KD, D], F32R)
        m_raw = [sb(f"m_raw{b}", [P, KD, P]) for b in range(2)]
        m_hi = [sb(f"m_hi{b}", [P, KD, P], F32R) for b in range(2)]
        m_lo = [sb(f"m_lo{b}", [P, KD, P], F32R) for b in range(2)]
        xt = [sb(f"x{b}", [P, D]) for b in range(2)]
        x2 = [sb(f"x2{b}", [P, D]) for b in range(2)]
        h2 = [sb(f"h2{b}", [P, D]) for b in range(2)]
        h2T = [sb(f"h2T{b}", [P, KD, P]) for b in range(2)]
        squares = sb("squares", [P, D])
        gain = sb("gain", [P, D])
        w_route = sb("w_route", [P, KD, N_LOGIT])
        b_route = sb("b_route", [P, N_LOGIT])
        sums, rms, rstd = sb("sums", [P, 2]), sb("rms", [P, 2]), sb("rstd", [P, 2])
        eps = sb("eps", [P, 1])
        o_ps = [[ctx.enter_context(nc.psum_tensor(f"po_o{b}{j}", [P, CH], F32)) for j in range(2)] for b in range(2)]
        t_ps = [ctx.enter_context(nc.psum_tensor(f"po_t{j}", [P, 4, P], F32)) for j in range(2)]
        r_ps = [ctx.enter_context(nc.psum_tensor(f"po_r{b}", [P, CH], F32)) for b in range(2)]
        params, eps_set = sem("params"), sem("eps_set")
        w_loaded = [sem(f"w_loaded{k}") for k in range(KD)]
        m_loaded = [sem(f"m_loaded{b}") for b in range(2)]
        x_loaded = [sem(f"x_loaded{b}") for b in range(2)]
        x2_stored = [sem(f"x2_stored{b}") for b in range(2)]
        h2_stored = [sem(f"h2_stored{b}") for b in range(2)]
        w_high, w_low, m_high, m_low = sem("w_high"), sem("w_low"), sem("m_high"), sem("m_low")
        product, x2_half, squared, rooted, inverted, h2_done = (sem("product"), sem("x2_half"), sem("squared"), sem("rooted"),
                                                                sem("inverted"), sem("h2_done"))
        turned, copied, routed, logged = sem("turned"), sem("copied"), sem("routed"), sem("logged")
        block = ctx.enter_context(nc.Block())
        m_view = scratch["merged"].rearrange("f p s -> p f s")

        def rows(ap, i):
            return ap[bass.ds(i * P, P), :]

        @block.sync
        def _(sp):
            def load_merged(i, b):
                if not isinstance(i, int) or i >= 2:
                    sp.wait_ge(m_low, i - 1)
                sp.dma_start(m_raw[b][:, :, :], m_view[:, :, bass.ds(i * P, P)]).then_inc(m_loaded[b], 16)

            def load_x(i, b):
                if not isinstance(i, int) or i >= 2:
                    sp.wait_ge(x2_half, i * 2 - 2)
                sp.dma_start(xt[b][:, :], rows(x, i)).then_inc(x_loaded[b], 16)

            def store_tile(i, b):
                sp.wait_ge(x2_half, i * 2 + 2)
                sp.dma_start(rows(scratch["x2"], i), x2[b][:, :]).then_inc(x2_stored[b], 16)
                sp.wait_ge(h2_done, i + 1)
                sp.dma_start(rows(scratch["h2"], i), h2[b][:, :]).then_inc(h2_stored[b], 16)

            load_merged(0, 0)
            for k in range(KD):
                sp.dma_start(w_raw[k], w_out[0, k * P:(k + 1) * P, :]).then_inc(w_loaded[k], 16)
                if k == 0:
                    load_merged(1, 1)
            load_merged(2, 0)
            load_x(0, 0)
            load_merged(3, 1)
            load_x(1, 1)
            with nc.allow_non_contiguous_dma("small parameters"):
                sp.dma_start(gain[:, :], g_ffn.rearrange("o d -> (o d)").partition_broadcast(P)).then_inc(params, 16)
                sp.dma_start(b_route[:, 0:N_GROUP], b_rg.rearrange("o d -> (o d)").partition_broadcast(P)).then_inc(params, 16)
                sp.dma_start(b_route[:, N_GROUP:N_LOGIT], b_re.rearrange("o d -> (o d)").partition_broadcast(P)).then_inc(params, 16)
                sp.dma_start(w_route[:, :, 0:N_GROUP], w_rg.rearrange("o (k p) n -> p (o k) n", p=P)).then_inc(params, 16)
                sp.dma_start(w_route[:, :, N_GROUP:N_LOGIT], w_re.rearrange("o (k p) n -> p (o k) n", p=P)).then_inc(params, 16)
            with sp.Fori(0, NT // 2 - 2) as i:
                for b in range(2):
                    load_merged(i * 2 + (b + 4), b)
                    store_tile(i * 2 + b, b)
                    load_x(i * 2 + (b + 2), b)
            for b in range(2):
                store_tile(NT - 4 + b, b)
                load_x(NT - 2 + b, b)
            for b in range(2):
                store_tile(NT - 2 + b, b)
            for b in range(2):
                sp.wait_ge(x2_stored[b], 16 * NT // 2)
                sp.wait_ge(h2_stored[b], 16 * NT // 2)

        @block.gpsimd
        def _(pool):
            pool.memset(eps[:, :], EPS).then_inc(eps_set, 1)

            def split(i, b):
                if isinstance(i, int):
                    pool.wait_ge(m_loaded[b], 16 * (i // 2 + 1))
                else:
                    pool.wait_ge(m_loaded[b], i * 8 + (16 - 8 * b))
                if not isinstance(i, int) or i >= 2:
                    pool.wait_ge(product, i * 2 - 2)
                pool.tensor_tensor(m_hi[b][:, :, :], m_raw[b][:, :, :], ones_col[:, 0:1, None].broadcast_to([P, KD, P]), ALU.mult).then_inc(m_high, 1)
                pool.wait_ge(m_high, i + 1)
                pool.tensor_tensor(m_lo[b][:, :, :], m_raw[b][:, :, :], m_hi[b][:, :, :], ALU.subtract).then_inc(m_low, 1)

            split(0, 0)
            split(1, 1)
            with pool.Fori(1, NT // 2) as i:
                split(i * 2, 0)
                split(i * 2 + 1, 1)

        @block.tensor
        def _(pe):
            def first_products():
                for k in range(KD):
                    pe.wait_ge(w_low, k + 1)
                    for i in range(2):
                        if k == 0:
                            pe.wait_ge(m_low, i + 1)
                        for j in range(2):
                            for n, (m, w) in enumerate(((m_hi, w_hi), (m_hi, w_lo), (m_lo, w_hi))):
                                q = nc.tensor.matmul(o_ps[i][j][:, :], m[i][:, k, :], w[:, k, j * CH:(j + 1) * CH],
                                                     start=(k == 0 and n == 0), stop=(k == KD - 1 and n == 2))
                            if k == KD - 1:
                                q.then_inc(product, 1)

            def out_product(i, b, j):
                if j == 0:
                    pe.wait_ge(m_low, i + 1)
                    pe.wait_ge(x2_half, i * 2 - 2)
                cols = slice(j * CH, (j + 1) * CH)
                n = 0
                for k in range(KD):
                    for m, w in ((m_hi, w_hi), (m_hi, w_lo), (m_lo, w_hi)):
                        q = nc.tensor.matmul(o_ps[b][j][:, :], m[b][:, k, :], w[:, k, cols], start=(n == 0), stop=(n == 3 * KD - 1))
                        n += 1
                q.then_inc(product, 1)

            def turn(i, b):
                pe.wait_ge(h2_done, i + 1)
                for j in range(2):
                    if not (isinstance(i, int) and i == 0):
                        pe.wait_ge(copied, i * 2 + (j - 1))
                    for q in range(4):
                        k = 4 * j + q
                        m = nc.tensor.transpose(t_ps[j][:, q, :], h2[b][:, k * P:(k + 1) * P], ident[:, :])
                    m.then_inc(turned, 1)

            def route_product(i, b):
                pe.wait_ge(copied, i * 2 + 2)
                if not isinstance(i, int) or i >= 2:
                    pe.wait_ge(logged, i - 1)
                for k in range(KD):
                    m = nc.tensor.matmul(r_ps[b][:, 0:N_LOGIT], h2T[b][:, k, :], w_route[:, k, :], start=(k == 0), stop=(k == KD - 1))
                m.then_inc(routed, 1)

            first_products()
            out_product(2, 0, 0)
            turn(0, 0)
            out_product(2, 0, 1)
            pe.wait_ge(params, 80)
            route_product(0, 0)
            turn(1, 1)
            out_product(3, 1, 0)
            route_product(1, 1)
            turn(2, 0)
            out_product(3, 1, 1)
            route_product(2, 0)
            with pe.Fori(2, NT // 2) as i:
                for b in range(2):
                    out_product(i * 2 + b, b, 0)
                    turn(i * 2 + (b - 1), 1 - b)
                    out_product(i * 2 + b, b, 1)
                    route_product(i * 2 + (b - 1), 1 - b)
            turn(NT - 1, 1)
            route_product(NT - 1, 1)

        @block.scalar
        def _(act):
            for k in range(KD):
                act.wait_ge(w_loaded[k], 16)
                nc.scalar.copy(w_hi[:, k, :], w_raw[k]).then_inc(w_high, 1)
            act.wait_ge(eps_set, 1)

            def root(i, b):
                act.wait_ge(x2_half, i * 2 + 2)
                if not (isinstance(i, int) and i == 0):
                    act.wait_ge(rooted, i)
                nc.scalar.activation(squares[:, :], x2[b][:, :], ACT.Square, accum_out=sums[:, b:b + 1]).then_inc(squared, 1)
                act.wait_ge(squared, i + 1)
                if not isinstance(i, int) or i >= 2:
                    act.wait_ge(inverted, i - 1)
                nc.scalar.activation(rms[:, b:b + 1], sums[:, b:b + 1], ACT.Sqrt, bias=eps[:, 0:1], scale=1.0 / D).then_inc(rooted, 1)

            def copy_turned(i, b):
                for j in range(2):
                    act.wait_ge(turned, i * 2 + (j + 1))
                    if not isinstance(i, int) or i >= 2:
                        act.wait_ge(routed, i - 1)
                    nc.scalar.copy(h2T[b][:, 4 * j:4 * j + 4, :], t_ps[j][:, :, :]).then_inc(copied, 1)

            root(0, 0)
            root(1, 1)
            copy_turned(0, 0)
            with act.Fori(1, NT // 2) as i:
                for b in range(2):
                    copy_turned(i * 2 + (b - 1), 1 - b)
                    root(i * 2 + b, b)
            copy_turned(NT - 1, 1)

        @block.vector
        def _(dve):
            for k in range(KD):
                dve.wait_ge(w_high, k + 1)
                dve.tensor_tensor(w_lo[:, k, :], w_raw[k], w_hi[:, k, :], ALU.subtract).then_inc(w_low, 1)
            dve.wait_ge(params, 80)

            def residual(i, b):
                for j in range(2):
                    dve.wait_ge(product, i * 2 + (j + 1))
                    if j == 0:
                        if isinstance(i, int):
                            dve.wait_ge(x_loaded[b], 16 * (i // 2 + 1))
                        else:
                            dve.wait_ge(x_loaded[b], i * 8 + (16 - 8 * b))
                        if isinstance(i, int) and i < 2:
                            pass
                        elif isinstance(i, int):
                            dve.wait_ge(x2_stored[b], 16 * (i // 2))
                        else:
                            dve.wait_ge(x2_stored[b], i * 8 - 8 * b)
                    cols = slice(j * CH, (j + 1) * CH)
                    dve.tensor_tensor(x2[b][:, cols], o_ps[b][j][:, :], xt[b][:, cols], ALU.add).then_inc(x2_half, 1)
                dve.wait_ge(rooted, i + 1)
                dve.reciprocal(rstd[:, b:b + 1], rms[:, b:b + 1]).then_inc(inverted, 1)
                dve.wait_ge(inverted, i + 1)
                if not isinstance(i, int) or i >= 2:
                    dve.wait_ge(h2_stored[b], i * 8 - 8 * b)
                    dve.wait_ge(turned, i * 2 - 2)
                dve.scalar_tensor_tensor(out=h2[b][:, :], in0=x2[b][:, :], scalar=rstd[:, b:b + 1], in1=gain[:, :],
                                         op0=ALU.mult, op1=ALU.mult).then_inc(h2_done, 1)

            def log(i, b):
                dve.wait_ge(routed, i + 1)
                dve.tensor_tensor(logits[:, bass.ds(i, 1), :].rearrange("p a n -> p (a n)"), r_ps[b][:, 0:N_LOGIT], b_route[:, :], ALU.add).then_inc(logged, 1)

            residual(0, 0)
            residual(1, 1)
            log(0, 0)
            with dve.Fori(1, NT // 2) as i:
                for b in range(2):
                    residual(i * 2 + b, b)
                    log(i * 2 + (b - 1), 1 - b)
            log(NT - 1, 1)
            dve.wait_ge(logged, NT)


def expert_weights(nc, ctx):
    def sb(name, shape):
        return ctx.enter_context(nc.sbuf_tensor("ex_" + name, shape, F32))

    return {"in": sb("raw_in", [P, LOADED, KD, 2 * FE]), "out": sb("raw_out", [P, LOADED, FK, D]),
            "loaded": [ctx.enter_context(nc.semaphore(f"ex_w_loaded{b}")) for b in range(2)]}


def load_expert(sp, weights, w1, w3, w2, plan, b, u, through=None, in_free=None, out_free=None):
    e = sp.value_load(plan[0:1, 0, bass.ds(b, 1)], min_val=0, max_val=N_EXP - 1)
    r = sp.value_load(plan[0:1, 1, bass.ds(b, 1)], min_val=0, max_val=LOADED - 1)
    new = sp.value_load(plan[0:1, 2, bass.ds(b, 1)], min_val=0, max_val=1)
    flat = lambda ap: ap.rearrange("p a k n -> p (a k) n")
    src = lambda w: w.rearrange("o e (k p) n -> (o e) p k n", p=P)[bass.ds(e, 1)].rearrange("a p k n -> p (a k) n")
    if through:
        sp.wait_ge(*through)
    if in_free:
        sp.wait_ge(*in_free)
    for half, w in enumerate((w1, w3)):
        sp.dma_start(flat(weights["in"][:, bass.ds(r, 1), :, half * FE:(half + 1) * FE]), src(w), cond=(new > 0),
                     bounds_check="skip_entire_dma").then_inc(weights["loaded"][u], 16)
    if out_free:
        sp.wait_ge(*out_free)
    sp.dma_start(flat(weights["out"][:, bass.ds(r, 1), :, :]), src(w2), cond=(new > 0),
                 bounds_check="skip_entire_dma").then_inc(weights["loaded"][u], 16)


def route(nc, logits, gates, slots, plan, w1, w3, w2, weights):
    with ExitStack() as ctx:
        def sb(name, shape, dt=F32):
            return ctx.enter_context(nc.sbuf_tensor("ro_" + name, shape, dt))

        def sem(name):
            return ctx.enter_context(nc.semaphore("ro_" + name))

        g_max, g_sum, pick = sb("g_max", [P, NT, 1]), sb("g_sum", [P, NT, 1]), sb("pick", [P, NT, 1])
        g_rel, g_exp, g_cand, g_one = (sb(n, [P, NT, N_GROUP]) for n in ("g_rel", "g_exp", "g_cand", "g_one"))
        masked = sb("masked", [P, NT, N_GROUP, PER_GROUP])
        le, le_rest, cand = (sb(n, [P, NT, PER_GROUP]) for n in ("le", "le_rest", "cand"))
        best = [sb(f"best{c}", [P, NT, 1]) for c in range(TOP)]
        one = [sb(f"one{c}", [P, NT, PER_GROUP]) for c in range(TOP)]
        onehot = [sb(f"onehot{c}", [P, NT, N_EXP]) for c in range(TOP)]
        both = sb("both", [P, NT, N_EXP])
        ratio, total = sb("ratio", [P, NT, 1]), sb("total", [P, NT, 1])
        running = sb("running", [P, N_EXP, NT])
        tile_totals = sb("tile_totals", [P, N_EXP, NT])
        place = sb("place", [P, NT, N_EXP])
        count_i, blocks_f, ends, starts = sb("count_i", [P, N_EXP], I32), sb("blocks_f", [P, N_EXP]), sb("ends", [P, N_EXP]), sb("starts", [P, N_EXP])
        zeros32 = sb("zeros32", [P, N_EXP])
        dest = sb("dest", [P, TOP, NT])
        dest_i, row_i, block_i = (sb(n, [P, TOP, NT], I32) for n in ("dest_i", "row_i", "block_i"))
        row_f, block_f = sb("row_f", [P, TOP, NT]), sb("block_f", [P, TOP, NT])
        index8 = sb("index8", [P, 1, PER_GROUP])
        index_row, index_block = sb("index_row", [P, P]), sb("index_block", [P, TABLE, 1])
        name = sb("name", [P, TOP, NT])
        before = sb("before", [P, P])
        ones = sb("ones", [P, P])
        cmp = sb("cmp", [P, TABLE, N_EXP])
        expert, fresh, runs = sb("expert", [P, TABLE, 1]), sb("fresh", [P, TABLE]), sb("runs", [P, TABLE])
        zeros_b = sb("zeros_b", [P, TABLE])
        not_first = sb("not_first", [P, N_EXP, NT])
        both_r, before_r, ones_r = (sb(n, s, F32R) for n, s in (("both_r", [P, NT * N_EXP]), ("before_r", [P, P]), ("ones_r", [P, P])))
        MULTIPLES = -(-(N_EXP + 2) // LOADED)
        multiples, passed = sb("multiples", [P, MULTIPLES]), sb("passed", [P, TABLE, MULTIPLES])
        row_hot = [sb(f"row_hot{b}", [P, P]) for b in range(4)]
        block_hot = [sb(f"block_hot{b}", [P, TABLE]) for b in range(4)]
        slot_f, slot_pad = sb("slot_f", [P, TABLE]), sb("slot_pad", [P, TABLE])
        ps_before = ctx.enter_context(nc.psum_tensor("ro_ps_before", [P, NT, N_EXP], F32))
        ps_total = ctx.enter_context(nc.psum_tensor("ro_ps_total", [P, NT, N_EXP], F32))
        ps_slot = ctx.enter_context(nc.psum_tensor("ro_ps_slot", [P, CH], F32))
        consts, chain, asked, counted, exped = sem("consts"), sem("chain"), sem("asked"), sem("counted"), sem("exped")
        plan_set = sem("plan_set")
        hot, placed, rows_known, row_set = sem("hot"), sem("placed"), sem("rows_known"), sem("row_set")
        block = ctx.enter_context(nc.Block())

        @block.sync
        def _(sp):
            sp.wait_ge(plan_set, 1)
            for b in range(2):
                load_expert(sp, weights, w1, w3, w2, plan, b, b)

        @block.gpsimd
        def _(pool):
            n = [0]

            def step(m):
                m.then_inc(consts, 1)
                n[0] += 1
                pool.wait_ge(consts, n[0])

            kw = dict(channel_multiplier=0, allow_small_or_imprecise_dtypes=True)
            step(pool.iota(index8[:, :, :], pattern=[[1, PER_GROUP]], base=0, **kw))
            step(pool.iota(index_row[:, :], pattern=[[1, P]], base=0, **kw))
            step(pool.iota(index_block[:, :, :], pattern=[[1, TABLE]], base=0, **kw))
            step(pool.iota(multiples[:, :], pattern=[[LOADED, MULTIPLES]], base=LOADED, **kw))
            kw["channel_multiplier"] = 1
            step(pool.iota(name[:, :, :], pattern=[[S, TOP], [P, NT]], base=1, **kw))
            step(pool.memset(ones[:, :], 1.0))
            step(pool.memset(zeros32[:, :], 0.0))
            step(pool.memset(zeros_b[:, :], 0.0))
            step(pool.memset(not_first[:, :, :], 1.0))
            step(pool.memset(not_first[:, :, 0:1], 0.0))
            step(pool.memset(before[:, :], 1.0))
            step(pool.affine_select(out=before[:, :], in_=before[:, :], compare_op=ALU.is_gt, fill=0.0, base=0,
                                    pattern=[[1, P]], channel_multiplier=-1))
            pool.wait_ge(rows_known, 1)
            for q in range(0, TOP * NT, 2):
                c, t = divmod(q, NT)
                if q >= 4:
                    pool.wait_ge(placed, q - 3)
                pool.tensor_scalar(row_hot[q % 4][:, :], index_row[:, :], row_f[:, c, t:t + 1], None, ALU.is_equal).then_inc(row_set, 1)

        @block.scalar
        def _(act):
            act.wait_ge(asked, 1)
            nc.scalar.activation(g_exp[:, :, :], g_rel[:, :, :], ACT.Exp).then_inc(exped, 1)
            act.wait_ge(asked, 2)
            nc.scalar.activation(ratio[:, :, :], ratio[:, :, :], ACT.Exp).then_inc(exped, 1)

        @block.vector
        def _(dve):
            n = [0]

            def step(m):
                m.then_inc(chain, 1)
                n[0] += 1
                dve.wait_ge(chain, n[0])

            lg = logits[:, :, 0:N_GROUP]
            lexp = logits[:, :, N_GROUP:N_LOGIT].rearrange("p t (g e) -> p t g e", g=N_GROUP)
            dve.wait_ge(consts, 1)
            step(dve.tensor_reduce(g_max[:, :, :], lg, AX.X, ALU.max))
            dve.tensor_tensor(g_rel[:, :, :], lg, g_max[:, :, :].broadcast_to([P, NT, N_GROUP]), ALU.subtract).then_inc(asked, 1)
            dve.wait_ge(asked, 1)
            step(dve.tensor_scalar(g_cand[:, :, :], g_rel[:, :, :], 0.0, -64.0, ALU.is_ge, ALU.mult))
            step(dve.tensor_tensor(g_cand[:, :, :], g_cand[:, :, :], index8[:, :, 0:N_GROUP].broadcast_to([P, NT, N_GROUP]), ALU.add))
            step(dve.tensor_reduce(pick[:, :, :], g_cand[:, :, :], AX.X, ALU.min))
            step(dve.tensor_tensor(g_one[:, :, :], g_cand[:, :, :], pick[:, :, :].broadcast_to([P, NT, N_GROUP]), ALU.is_equal))
            for g in range(N_GROUP):
                step(dve.tensor_tensor(masked[:, :, g, :], lexp[:, :, g, :], g_one[:, :, g:g + 1].broadcast_to([P, NT, PER_GROUP]), ALU.mult))
            step(dve.tensor_reduce(le[:, :, :], masked[:, :, :, :].rearrange("p t g e -> p t e g"), AX.X, ALU.add))
            src = le
            for c in range(TOP):
                step(dve.tensor_reduce(best[c][:, :, :], src[:, :, :], AX.X, ALU.max))
                step(dve.tensor_tensor(cand[:, :, :], src[:, :, :], best[c][:, :, :].broadcast_to([P, NT, PER_GROUP]), ALU.is_ge))
                step(dve.scalar_tensor_tensor(out=cand[:, :, :], in0=cand[:, :, :], scalar=-64.0, in1=index8[:, :, :].broadcast_to([P, NT, PER_GROUP]),
                                              op0=ALU.mult, op1=ALU.add))
                step(dve.tensor_reduce(pick[:, :, :], cand[:, :, :], AX.X, ALU.min))
                step(dve.tensor_tensor(one[c][:, :, :], cand[:, :, :], pick[:, :, :].broadcast_to([P, NT, PER_GROUP]), ALU.is_equal))
                if c == 0:
                    step(dve.scalar_tensor_tensor(out=le_rest[:, :, :], in0=one[c][:, :, :], scalar=-1e30, in1=le[:, :, :],
                                                  op0=ALU.mult, op1=ALU.add))
                    src = le_rest
                for g in range(N_GROUP):
                    step(dve.tensor_tensor(onehot[c][:, :, g * PER_GROUP:(g + 1) * PER_GROUP], one[c][:, :, :],
                                           g_one[:, :, g:g + 1].broadcast_to([P, NT, PER_GROUP]), ALU.mult))
            dve.wait_ge(consts, 12)
            dve.tensor_copy(before_r[:, :], before[:, :]).then_inc(hot, 1)
            dve.tensor_copy(ones_r[:, :], ones[:, :]).then_inc(hot, 1)
            dve.tensor_tensor(both_r[:, :].rearrange("p (t e) -> p t e", t=NT), onehot[0][:, :, :], onehot[1][:, :, :], ALU.add).then_inc(hot, 1)
            dve.tensor_tensor(ratio[:, :, :], best[1][:, :, :], best[0][:, :, :], ALU.subtract).then_inc(asked, 1)
            dve.wait_ge(exped, 2)
            step(dve.tensor_reduce(g_sum[:, :, :], g_exp[:, :, :], AX.X, ALU.add))
            step(dve.tensor_scalar(total[:, :, :], ratio[:, :, :], 1.0, None, ALU.add))
            step(dve.tensor_tensor(total[:, :, :], total[:, :, :], g_sum[:, :, :], ALU.mult))
            step(dve.reciprocal(gates[:, :, 0:1], total[:, :, :]))
            step(dve.tensor_tensor(gates[:, :, 1:2], gates[:, :, 0:1], ratio[:, :, :], ALU.mult))
            dve.wait_ge(counted, 2)
            step(dve.tensor_copy(tile_totals[:, :, :], ps_total[:, :, :].rearrange("p t e -> p e t")))
            flat = lambda ap: ap[:, :, :].rearrange("p e t -> p (e t)")
            by_tile = lambda ap: ap[:, :, :].rearrange("p e t -> p t e")
            step(dve.tensor_tensor_scan(flat(running), flat(not_first), flat(tile_totals), 0.0, ALU.mult, ALU.add))
            step(dve.tensor_scalar(blocks_f[:, :], by_tile(running)[:, NT - 1, :], float(P - 1), None, ALU.add))
            step(dve.tensor_copy(count_i[:, :], blocks_f[:, :]))
            step(dve.tensor_scalar(count_i[:, :], count_i[:, :], P.bit_length() - 1, None, ALU.arith_shift_right))
            step(dve.tensor_copy(blocks_f[:, :], count_i[:, :]))
            step(dve.tensor_tensor_scan(ends[:, :], blocks_f[:, :], zeros32[:, :], 0.0, ALU.add, ALU.add))
            step(dve.tensor_tensor(starts[:, :], ends[:, :], blocks_f[:, :], ALU.subtract))
            step(dve.tensor_tensor(place[:, :, :], by_tile(running), by_tile(tile_totals), ALU.subtract))
            step(dve.tensor_tensor(place[:, :, :], place[:, :, :], ps_before[:, :, :], ALU.add))
            step(dve.tensor_scalar(starts[:, :], starts[:, :], float(P), None, ALU.mult))
            step(dve.tensor_tensor(place[:, :, :], place[:, :, :], starts[:, None, :].broadcast_to([P, NT, N_EXP]), ALU.add))
            for c in range(TOP):
                step(dve.tensor_tensor(both[:, :, :], onehot[c][:, :, :], place[:, :, :], ALU.mult))
                step(dve.tensor_reduce(dest[:, c, :].rearrange("p (t a) -> p t a", a=1), both[:, :, :], AX.X, ALU.add))
            step(dve.tensor_copy(dest_i[:, :, :], dest[:, :, :]))
            step(dve.tensor_scalar(row_i[:, :, :], dest_i[:, :, :], P - 1, None, ALU.bitwise_and))
            step(dve.tensor_scalar(block_i[:, :, :], dest_i[:, :, :], P.bit_length() - 1, None, ALU.arith_shift_right))
            dve.tensor_copy(row_f[:, :, :], row_i[:, :, :]).then_inc(rows_known, 1)
            step(dve.tensor_copy(block_f[:, :, :], block_i[:, :, :]))
            step(dve.tensor_tensor(cmp[:, :, :], index_block[:, :, :].broadcast_to([P, TABLE, N_EXP]), ends[:, None, :].broadcast_to([P, TABLE, N_EXP]), ALU.is_ge))
            step(dve.tensor_reduce(expert[:, :, :], cmp[:, :, :], AX.X, ALU.add))
            ex = expert[:, :, :].rearrange("p b a -> p (b a)")
            step(dve.tensor_scalar(ex, ex, float(N_EXP - 1), None, ALU.min))
            step(dve.tensor_copy(plan[:, 0, :], ex))
            step(dve.memset(fresh[:, 0:1], 1.0))
            step(dve.tensor_tensor(fresh[:, 1:TABLE], ex[:, 1:TABLE], ex[:, 0:TABLE - 1], ALU.not_equal))
            step(dve.tensor_tensor_scan(runs[:, :], fresh[:, :], zeros_b[:, :], 1.0, ALU.add, ALU.add))
            step(dve.tensor_tensor(passed[:, :, :], runs[:, :, None].broadcast_to([P, TABLE, MULTIPLES]), multiples[:, None, :].broadcast_to([P, TABLE, MULTIPLES]), ALU.is_ge))
            step(dve.tensor_reduce(expert[:, :, :], passed[:, :, :], AX.X, ALU.add))
            step(dve.scalar_tensor_tensor(out=runs[:, :], in0=expert[:, :, :].rearrange("p b a -> p (b a)"), scalar=-float(LOADED), in1=runs[:, :], op0=ALU.mult, op1=ALU.add))
            step(dve.tensor_copy(plan[:, 1, :], runs[:, :]))
            step(dve.tensor_copy(plan[:, 2, :], fresh[:, :]))
            step(dve.tensor_copy(plan[:, 3, :], ends[:, N_EXP - 1:N_EXP].broadcast_to([P, TABLE])))
            step(dve.tensor_scalar(plan[:, 3, :], plan[:, 3, :], 1, None, ALU.add))
            dve.tensor_scalar(plan[:, 3, :], plan[:, 3, :], 1, None, ALU.arith_shift_right).then_inc(plan_set, 1)
            for q in range(TOP * NT):
                c, t = divmod(q, NT)
                if q >= 4:
                    dve.wait_ge(placed, q - 3)
                if q % 2 == 1:
                    dve.tensor_scalar(row_hot[q % 4][:, :], index_row[:, :], row_f[:, c, t:t + 1], None, ALU.is_equal)
                dve.tensor_scalar(block_hot[q % 4][:, :], index_block[:, :, :].rearrange("p b a -> p (b a)"), block_f[:, c, t:t + 1],
                                  name[:, c, t:t + 1], ALU.is_equal, ALU.mult).then_inc(hot, 1)
            dve.wait_ge(placed, TOP * NT)
            step(dve.tensor_scalar(slot_pad[:, :], ps_slot[:, 0:TABLE], 0.0, float(PAD), ALU.is_equal, ALU.mult))
            step(dve.scalar_tensor_tensor(out=slot_f[:, :], in0=ps_slot[:, 0:TABLE], scalar=-1.0, in1=slot_pad[:, :], op0=ALU.add, op1=ALU.add))
            step(dve.tensor_copy(slots[:, 0, :], slot_f[:, :]))
            step(dve.tensor_scalar(slots[:, 1, :], slots[:, 0, :], S - 1, None, ALU.bitwise_and))

        @block.tensor
        def _(pe):
            pe.wait_ge(hot, 3)
            flat = both_r[:, :]
            nc.tensor.matmul(ps_before[:, :, :].rearrange("p t e -> p (t e)"), before_r[:, :], flat, start=True, stop=True).then_inc(counted, 1)
            nc.tensor.matmul(ps_total[:, :, :].rearrange("p t e -> p (t e)"), ones_r[:, :], flat, start=True, stop=True).then_inc(counted, 1)
            for q in range(TOP * NT):
                pe.wait_ge(row_set, q // 2 + 1)
                pe.wait_ge(hot, q + 4)
                nc.tensor.matmul(ps_slot[:, 0:TABLE], row_hot[q % 4][:, :], block_hot[q % 4][:, :],
                                 start=(q == 0), stop=(q == TOP * NT - 1)).then_inc(placed, 1)


def experts(nc, w1, w3, w2, weights, ident, slots, plan, scratch):
    with ExitStack() as ctx:
        def sb(name, shape, dt=F32):
            return ctx.enter_context(nc.sbuf_tensor("ex_" + name, shape, dt))

        def sem(name):
            return ctx.enter_context(nc.semaphore("ex_" + name))

        raw_in, raw_out, w_loaded = (weights[n] for n in ("in", "out", "loaded"))
        in_hi = [sb(f"in_hi{b}", [P, KD, 2 * FE], F32R) for b in range(2)]
        in_lo = [sb(f"in_lo{b}", [P, KD, 2 * FE], F32R) for b in range(2)]
        out_hi = [sb(f"out_hi{b}", [P, FK, D], F32R) for b in range(2)]
        out_lo = [sb(f"out_lo{b}", [P, FK, D], F32R) for b in range(2)]
        x = [sb(f"x{b}", [P, D]) for b in range(2)]
        xT_hi = [sb(f"xT_hi{b}", [P, KD, P], F32R) for b in range(2)]
        xT_lo = [sb(f"xT_lo{b}", [P, KD, P], F32R) for b in range(2)]
        inner = sb("inner", [P, FE])
        iT_hi = [sb(f"iT_hi{b}", [P, FK, P], F32R) for b in range(2)]
        iT_lo = [sb(f"iT_lo{b}", [P, FK, P], F32R) for b in range(2)]
        y = [sb(f"y{b}", [P, D]) for b in range(2)]
        fetch = [sb(f"fetch{b}", [P, 1], I32) for b in range(2)]
        put = [sb(f"put{b}", [P, 1], I32) for b in range(2)]
        x_ps = [ctx.enter_context(nc.psum_tensor(f"ex_ps_x{j}", [P, 4, P], F32)) for j in range(2)]
        h_ps = [ctx.enter_context(nc.psum_tensor(f"ex_ps_h{b}", [P, 2 * FE], F32)) for b in range(2)]
        i_ps = ctx.enter_context(nc.psum_tensor("ex_ps_i", [P, 4, P], F32))
        y_ps = [ctx.enter_context(nc.psum_tensor(f"ex_ps_y{j}", [P, CH], F32)) for j in range(2)]
        fetched = [sem(f"fetched{b}") for b in range(2)]
        stored = [sem(f"stored{b}") for b in range(2)]
        fetch_set, put_set, may_move = sem("fetch_set"), sem("put_set"), sem("may_move")
        in_high, in_low, out_high, out_low = sem("in_high"), sem("in_low"), sem("out_high"), sem("out_low")
        x_turned, x_high, x_low = sem("x_turned"), sem("x_high"), sem("x_low")
        inner_done, silu_done, inner_set, i_turned, i_high, i_low = (sem("inner_done"), sem("silu_done"), sem("inner_set"),
                                                                     sem("i_turned"), sem("i_high"), sem("i_low"))
        y_product, y_copied = sem("y_product"), sem("y_copied")
        block = ctx.enter_context(nc.Block())
        LOADS = 3 * 16

        def wait_pair(eng, sems, b, u, each):
            if isinstance(b, int):
                eng.wait_ge(sems[u], each * (b // 2 + 1))
            else:
                eng.wait_ge(sems[u], b * (each // 2) + (each - each // 2 * u))

        def pairs_of(eng):
            return eng.value_load(plan[0:1, 3, 0:1], min_val=S * TOP // P // 2, max_val=BLOCKS // 2)

        def buffer_of(eng, b):
            return eng.value_load(plan[0:1, 1, bass.ds(b, 1)], min_val=0, max_val=LOADED - 1)

        @block.sync
        def _(sp):
            def load(b, u):
                through = b * (LOADS // 2) - LOADS // 2 * u
                load_expert(sp, weights, w1, w3, w2, plan, b, u, (w_loaded[u], through), (in_low, b * KD - 2 * KD), (out_low, b - 2))

            pairs = pairs_of(sp)
            sp.wait_ge(fetched[0], 16)
            load_expert(sp, weights, w1, w3, w2, plan, 2, 0, (w_loaded[0], LOADS))
            load(3, 1)
            with sp.Fori(2, BLOCKS // 2) as i:
                with sp.If(i < pairs):
                    for u in range(2):
                        load(i * 2 + u, u)

        @block.gpsimd
        def _(pool):
            def fetch_rows(b, u):
                if not isinstance(b, int) or b >= 2:
                    wait_pair(pool, fetched, b - 2, u, 16)
                    pool.wait_ge(x_turned, b * 2 - 2)
                pool.tensor_copy(fetch[u][:, :], slots[:, 1, bass.ds(b, 1)]).then_inc(fetch_set, 1)
                pool.wait_ge(fetch_set, b + 1)
                pool.sem_inc(may_move)
                pool.indirect_dma_start(x[u][:, :], None, scratch["h2"], bass.IndirectOffsetOnAxis(ap=fetch[u][:, :], axis=0)).then_inc(fetched[u], 16)

            def out_low_part(b, u):
                wait_pair(pool, w_loaded, b, u, LOADS)
                r = buffer_of(pool, b)
                pool.wait_ge(out_high, b + 1)
                pool.tensor_tensor(out_lo[u][:, :, :], raw_out[:, bass.ds(r, 1), :, :].rearrange("p a k n -> p (a k) n"),
                                   out_hi[u][:, :, :], ALU.subtract).then_inc(out_low, 1)

            def store_rows(b, u):
                if not isinstance(b, int) or b >= 2:
                    wait_pair(pool, stored, b - 2, u, 16)
                pool.tensor_copy(put[u][:, :], slots[:, 0, bass.ds(b, 1)]).then_inc(put_set, 1)
                pool.wait_ge(put_set, b + 1)
                pool.wait_ge(y_copied, b * 2 + 2)
                pool.sem_inc(may_move)
                pool.indirect_dma_start(scratch["y_slots"], bass.IndirectOffsetOnAxis(ap=put[u][:, :], axis=0), y[u][:, :], None,
                                        bounds_check=S * TOP - 1, oob_is_err=False).then_inc(stored[u], 16)

            pairs = pairs_of(pool)
            fetch_rows(0, 0)
            fetch_rows(1, 1)
            fetch_rows(2, 0)
            out_low_part(0, 0)
            fetch_rows(3, 1)
            out_low_part(1, 1)
            fetch_rows(4, 0)
            store_rows(0, 0)
            out_low_part(2, 0)
            with pool.Fori(1, BLOCKS // 2) as i:
                with pool.If(i < pairs - 1):
                    for u in (0, 1):
                        b = i * 2 + u
                        fetch_rows(b + 3, 1 - u)
                        store_rows(b - 1, 1 - u)
                        out_low_part(b + 1, 1 - u)
                with pool.If(i == pairs - 1):
                    b = i * 2
                    store_rows(b - 1, 1)
                    out_low_part(b + 1, 1)
                    store_rows(b, 0)
                    store_rows(b + 1, 1)
                    for u in range(2):
                        pool.wait_ge(stored[u], i * 16 + 16)
                    pool.wait_ge(fetched[0], i * 16 + 32)

        @block.tensor
        def _(pe):
            def turn_rows(b, u):
                wait_pair(pe, fetched, b, u, 16)
                for j in range(2):
                    if not (isinstance(b, int) and b == 0):
                        pe.wait_ge(x_low, b * 2 + (j - 1))
                    for q in range(4):
                        k = 4 * j + q
                        m = nc.tensor.transpose(x_ps[j][:, q, :], x[u][:, k * P:(k + 1) * P], ident[:, :])
                    m.then_inc(x_turned, 1)

            def into(b, u):
                pe.wait_ge(x_low, b * 2 + 2)
                if not isinstance(b, int) or b >= 2:
                    pe.wait_ge(inner_set, b - 1)
                n = 0
                for k in range(KD):
                    pe.wait_ge(in_low, b * KD + (k + 1))
                    for xs, ws in ((xT_hi, in_hi), (xT_hi, in_lo), (xT_lo, in_hi)):
                        m = nc.tensor.matmul(h_ps[u][:, :], xs[u][:, k, :], ws[u][:, k, :], start=(n == 0), stop=(n == 3 * KD - 1))
                        n += 1
                m.then_inc(inner_done, 1)

            def turn_inner(b, u):
                pe.wait_ge(inner_set, b + 1)
                if not (isinstance(b, int) and b == 0):
                    pe.wait_ge(i_low, b)
                for q in range(FK):
                    m = nc.tensor.transpose(i_ps[:, q, :], inner[:, q * P:(q + 1) * P], ident[:, :])
                m.then_inc(i_turned, 1)

            def out_of(b, u):
                pe.wait_ge(i_low, b + 1)
                pe.wait_ge(out_low, b + 1)
                for j in range(2):
                    if not (isinstance(b, int) and b == 0):
                        pe.wait_ge(y_copied, b * 2 + (j - 1))
                    n = 0
                    for k in range(FK):
                        for s, w in ((iT_hi, out_hi), (iT_hi, out_lo), (iT_lo, out_hi)):
                            m = nc.tensor.matmul(y_ps[j][:, :], s[u][:, k, :], w[u][:, k, j * CH:(j + 1) * CH], start=(n == 0), stop=(n == 3 * FK - 1))
                            n += 1
                    m.then_inc(y_product, 1)

            pairs = pairs_of(pe)
            turn_rows(0, 0)
            into(0, 0)
            turn_rows(1, 1)
            turn_inner(0, 0)
            into(1, 1)
            turn_rows(2, 0)
            out_of(0, 0)
            turn_inner(1, 1)
            with pe.Fori(1, BLOCKS // 2) as i:
                with pe.If(i < pairs - 1):
                    for u in range(2):
                        b = i * 2 + u
                        into(b, u)
                        turn_rows(b + 1, 1 - u)
                        out_of(b - 1, 1 - u)
                        turn_inner(b, u)
                with pe.If(i == pairs - 1):
                    for u in range(2):
                        b = i * 2 + u
                        into(b, u)
                        if u == 0:
                            turn_rows(b + 1, 1)
                        out_of(b - 1, 1 - u)
                        turn_inner(b, u)
                    out_of(i * 2 + 1, 1)

        @block.scalar
        def _(act):
            def in_high_part(b, u):
                wait_pair(act, w_loaded, b, u, LOADS)
                r = buffer_of(act, b)
                if not isinstance(b, int) or b >= 2:
                    act.wait_ge(inner_done, b - 1)
                for k in range(KD):
                    nc.scalar.copy(in_hi[u][:, k, :], raw_in[:, bass.ds(r, 1), k, :].rearrange("p a n -> p (a n)")).then_inc(in_high, 1)
                return r

            def out_high_part(b, u, r):
                if not isinstance(b, int) or b >= 2:
                    act.wait_ge(y_product, b * 2 - 2)
                nc.scalar.copy(out_hi[u][:, :, :], raw_out[:, bass.ds(r, 1), :, :].rearrange("p a k n -> p (a k) n")).then_inc(out_high, 1)

            def x_high_part(b, u):
                for j in range(2):
                    act.wait_ge(x_turned, b * 2 + (j + 1))
                    if not isinstance(b, int) or b >= 2:
                        act.wait_ge(inner_done, b - 1)
                    nc.scalar.copy(xT_hi[u][:, 4 * j:4 * j + 4, :], x_ps[j][:, :, :]).then_inc(x_high, 1)

            def silu(b, u):
                act.wait_ge(inner_done, b + 1)
                if not (isinstance(b, int) and b == 0):
                    act.wait_ge(i_turned, b)
                nc.scalar.activation(inner[:, :], h_ps[u][:, 0:FE], ACT.Silu).then_inc(silu_done, 1)

            def i_high_part(b, u):
                act.wait_ge(i_turned, b + 1)
                if not isinstance(b, int) or b >= 2:
                    act.wait_ge(y_product, b * 2 - 2)
                nc.scalar.copy(iT_hi[u][:, :, :], i_ps[:, 0:FK, :]).then_inc(i_high, 1)

            def step(b, u, last):
                if not last:
                    r = in_high_part(b + 1, 1 - u)
                silu(b, u)
                if not last:
                    x_high_part(b + 1, 1 - u)
                i_high_part(b, u)
                if not last:
                    out_high_part(b + 1, 1 - u, r)

            pairs = pairs_of(act)
            r = in_high_part(0, 0)
            x_high_part(0, 0)
            out_high_part(0, 0, r)
            step(0, 0, False)
            step(1, 1, False)
            with act.Fori(1, BLOCKS // 2) as i:
                with act.If(i < pairs - 1):
                    for u in range(2):
                        step(i * 2 + u, u, False)
                with act.If(i == pairs - 1):
                    step(i * 2, 0, False)
                    step(i * 2 + 1, 1, True)

        @block.vector
        def _(dve):
            def in_low_part(b, u):
                r = buffer_of(dve, b)
                for k in range(KD):
                    dve.wait_ge(in_high, b * KD + (k + 1))
                    dve.tensor_tensor(in_lo[u][:, k, :], raw_in[:, bass.ds(r, 1), k, :].rearrange("p a n -> p (a n)"), in_hi[u][:, k, :],
                                      ALU.subtract).then_inc(in_low, 1)

            def x_low_part(b, u):
                for j in range(2):
                    dve.wait_ge(x_high, b * 2 + (j + 1))
                    dve.tensor_tensor(xT_lo[u][:, 4 * j:4 * j + 4, :], x_ps[j][:, :, :], xT_hi[u][:, 4 * j:4 * j + 4, :], ALU.subtract).then_inc(x_low, 1)

            def set_inner(b, u):
                dve.wait_ge(silu_done, b + 1)
                dve.tensor_tensor(inner[:, :], inner[:, :], h_ps[u][:, FE:2 * FE], ALU.mult).then_inc(inner_set, 1)

            def i_low_part(b, u):
                dve.wait_ge(i_high, b + 1)
                dve.tensor_tensor(iT_lo[u][:, :, :], i_ps[:, 0:FK, :], iT_hi[u][:, :, :], ALU.subtract).then_inc(i_low, 1)

            def copy_y(b, u):
                for j in range(2):
                    dve.wait_ge(y_product, b * 2 + (j + 1))
                    if j == 0 and (not isinstance(b, int) or b >= 2):
                        wait_pair(dve, stored, b - 2, u, 16)
                    dve.tensor_copy(y[u][:, j * CH:(j + 1) * CH], y_ps[j][:, :]).then_inc(y_copied, 1)

            def step(b, u, last, first=False):
                if not last:
                    in_low_part(b + 1, 1 - u)
                set_inner(b, u)
                if not last:
                    x_low_part(b + 1, 1 - u)
                if not first:
                    copy_y(b - 1, 1 - u)
                i_low_part(b, u)

            pairs = pairs_of(dve)
            in_low_part(0, 0)
            x_low_part(0, 0)
            step(0, 0, False, True)
            step(1, 1, False)
            with dve.Fori(1, BLOCKS // 2) as i:
                with dve.If(i < pairs - 1):
                    for u in range(2):
                        step(i * 2 + u, u, False)
                with dve.If(i == pairs - 1):
                    step(i * 2, 0, False)
                    step(i * 2 + 1, 1, True)
                    copy_y(i * 2 + 1, 1)


def combine(nc, gates, out, scratch):
    RING = 4
    with ExitStack() as ctx:
        def sb(name, shape, dt=F32):
            return ctx.enter_context(nc.sbuf_tensor("co_" + name, shape, dt))

        def sem(name):
            return ctx.enter_context(nc.semaphore("co_" + name))

        x2 = [sb(f"x2{b}", [P, D]) for b in range(RING)]
        y = [sb(f"y{b}", [P, TOP, D]) for b in range(RING)]
        loaded = [sem(f"loaded{b}") for b in range(RING)]
        stored = [sem(f"stored{b}") for b in range(RING)]
        first, second = sem("first"), sem("second")
        block = ctx.enter_context(nc.Block())
        y_view = scratch["y_slots"].rearrange("(c s) d -> s c d", c=TOP)

        @block.sync
        def _(sp):
            for t in range(NT):
                b, rows = t % RING, slice(t * P, (t + 1) * P)
                if t >= RING:
                    sp.wait_ge(stored[b], 16 * (t // RING))
                sp.dma_start(x2[b][:, :], scratch["x2"][rows, :]).then_inc(loaded[b], 16)
                sp.dma_start(y[b][:, :, :], y_view[rows, :, :]).then_inc(loaded[b], 16)

        @block.vector
        def _(dve):
            for t in range(NT):
                b = t % RING
                dve.wait_ge(loaded[b], 32 * (t // RING + 1))
                dve.scalar_tensor_tensor(out=x2[b][:, :], in0=y[b][:, 0, :], scalar=gates[:, t, 0:1], in1=x2[b][:, :],
                                         op0=ALU.mult, op1=ALU.add).then_inc(first, 1)
                dve.wait_ge(first, t + 1)
                dve.scalar_tensor_tensor(out=x2[b][:, :], in0=y[b][:, 1, :], scalar=gates[:, t, 1:2], in1=x2[b][:, :],
                                         op0=ALU.mult, op1=ALU.add).then_inc(second, 1)

        @block.scalar
        def _(act):
            for t in range(NT):
                b = t % RING
                act.wait_ge(second, t + 1)
                act.dma_start(out[t * P:(t + 1) * P, :], x2[b][:, :]).then_inc(stored[b], 16)
            for b in range(RING):
                act.wait_ge(stored[b], 16 * NT // RING)


def hybrid_layer(nc, x, g_mix, w_in, b_fgate, b_gate, g_q, g_k, w_pool, s_pool, g_sgu, w_sgu, b_sgu, w_branch, w_out,
                 g_ffn, w_rg, b_rg, w_re, b_re, w1, w3, w2, out):
    x, out = x.rearrange("o s d -> (o s) d"), out.rearrange("o s d -> (o s) d")

    def dram(name, shape):
        return nc.dram_tensor(name, shape, F32, kind="Internal").ap()

    scratch = {
        "qk_hi": dram("qk_hi", (QK_TILES, P, S)),
        "qk_lo": dram("qk_lo", (QK_TILES, P, S)),
        "v": dram("v_parts", (NCH, P, TPC, HEADS, 2, HD)),
        "cum": dram("cum_parts", (HEADS, 2, S)),
        "y": dram("branch_out", (N_BR, BR_K, P, S)),
        "gates": dram("branch_gates", (GATE_TILES, P, S)),
        "merged": dram("merged", (KD, P, S)),
        "x2": dram("x2", (S, D)),
        "h2": dram("h2", (S, D)),
        "y_slots": dram("y_slots", (S * TOP, D)),
    }
    half = QK_TILES // 2
    flat = [scratch[n].rearrange("t p s -> (t p) s") for n in ("qk_hi", "qk_lo")]
    scratch["q_rows"] = [f[0:half * P] for f in flat]
    scratch["k_rows"] = [f[half * P:QK_TILES * P] for f in flat]

    with nc.sbuf_tensor("ident", [P, P], F32) as ident, nc.sbuf_tensor("ones_col", [P, 1], F32) as ones_col:
        with nc.sbuf_tensor("head_ones", [P, P], F32) as head_ones, nc.sbuf_tensor("hT_hi", [P, KD, S], F32R) as hT_hi, \
                nc.sbuf_tensor("hT_lo", [P, KD, S], F32R) as hT_lo, ExitStack() as ctx:
            spent = build_constants(nc, ident, head_ones, ones_col)
            weights = projection_weights(nc, ctx)
            spent += norm_and_transpose(nc, x, g_mix, ident, ones_col, w_in, weights, hT_hi, hT_lo)
            spent += project(nc, hT_hi, hT_lo, ident, head_ones, ones_col, weights, w_in, b_fgate, b_gate, g_q, g_k, w_pool,
                             s_pool, g_sgu, w_sgu, b_sgu, scratch)
        attend(nc, ident, scratch, spent)
        merge(nc, ones_col, w_branch, scratch)
        with nc.sbuf_tensor("gates", [P, NT, TOP], F32) as gates, nc.sbuf_tensor("slots", [P, 2, TABLE], I32) as slots, \
                nc.sbuf_tensor("plan", [P, 4, TABLE], I32) as plan, ExitStack() as ctx:
            weights = expert_weights(nc, ctx)
            with nc.sbuf_tensor("logits", [P, NT, N_LOGIT], F32) as logits:
                project_out(nc, ones_col, weights["in"], x, w_out, g_ffn, w_rg, b_rg, w_re, b_re, ident, logits, scratch)
                route(nc, logits, gates, slots, plan, w1, w3, w2, weights)
            experts(nc, w1, w3, w2, weights, ident, slots, plan, scratch)
            combine(nc, gates, out, scratch)


_INS = ["x", "g_mix", "w_in", "b_fgate", "b_gate", "g_q", "g_k", "w_pool", "s_pool", "g_sgu", "w_sgu", "b_sgu",
        "w_branch", "w_out", "g_ffn", "w_rg", "b_rg", "w_re", "b_re", "w1", "w3", "w2"]
_OUTS = [((1, S, D), "float32")]


def kernel(**inputs):
    import numpy as _np
    import concourse.bacc as _bacc
    from concourse import mybir as _mybir
    from concourse.bass_utils import run_bass_kernel_spmd as _run

    nc = _bacc.Bacc("TRN2", target_bir_lowering=False, num_devices=1)
    arrays, args = {}, []
    for name in _INS:
        a = _np.ascontiguousarray(inputs[name])
        arrays[f"in_{name}_dram"] = a
        args.append(nc.dram_tensor(f"in_{name}_dram", a.shape, _mybir.dt.from_np(a.dtype), kind="ExternalInput").ap())
    for i, (shape, dtype) in enumerate(_OUTS):
        dt = _mybir.dt.from_np(_np.dtype(dtype))
        args.append(nc.dram_tensor(f"out_{i}_dram", shape, dt, kind="ExternalOutput").ap())
    hybrid_layer(nc, *args)
    r = _run(nc, [arrays], core_ids=[0])
    got = tuple(r.results[0][f"out_{i}_dram"] for i in range(len(_OUTS)))
    return got[0]
```
